# Optimizing a Trainium2 kernel written in Bass

```python
import math
import jax
import jax.numpy as jnp
from jax import lax
import numpy as np
import jax, jax.numpy as jnp

D_MODEL = 1024
BATCH = 1
SEQ = 512
DEPTH = 2

GRID_W = 64
CTX_LEN = 256
N_MIXERS = 3
DN_ALPHA = (2 * DEPTH) ** 0.25
DN_BETA = (8 * DEPTH) ** -0.25
LN_EPS = 1e-5

RK_HEAD = 64
RK_HEADS = D_MODEL // RK_HEAD
RK_DECAY_LORA = 64
RK_ICLR_LORA = 64
RK_GATE_LORA = 128
RK_DECAY_SCALE = math.exp(-0.5)
RK_GN_EPS = 64e-5

POOL_WINDOWS = (2, 4, 8, 16)
POOL_GROUP = D_MODEL // len(POOL_WINDOWS)

GDN_HEAD = 128
GDN_HEADS = D_MODEL // GDN_HEAD
GDN_CONV = 4
GDN_CHUNK = 64
GDN_NORM_EPS = 1e-6
GDN_IN = 4 * D_MODEL + 4 * GDN_HEADS

D_FF = 2816
N_EXPERTS = 8
TOP_K = 2
D_FF_EXPERT = 1408

N_RWKV_LAYERS = len(range(0, DEPTH, N_MIXERS))
N_POOL_LAYERS = len(range(1, DEPTH, N_MIXERS))
N_GDN_LAYERS = len(range(2, DEPTH, N_MIXERS))
N_DENSE_LAYERS = len(range(0, DEPTH, 2))
N_MOE_LAYERS = len(range(1, DEPTH, 2))


def layer_norm(x, g, b):
    xf = x.astype(jnp.float32)
    mean = jnp.mean(xf, axis=-1, keepdims=True)
    var = jnp.mean(jnp.square(xf - mean), axis=-1, keepdims=True)
    return ((xf - mean) * lax.rsqrt(var + LN_EPS) * g + b).astype(x.dtype)

def flip_time(t):
    return jnp.flip(t, axis=1)

def identity(t):
    return t

def qshift_grid(h, n_rows):
    b, n, d = h.shape
    q = d // 4
    grid = h.reshape(b, n_rows, GRID_W, d)
    left = jnp.pad(grid[:, :, :-1, :q], ((0, 0), (0, 0), (1, 0), (0, 0)))
    right = jnp.pad(grid[:, :, 1:, q:2 * q], ((0, 0), (0, 0), (0, 1), (0, 0)))
    up = jnp.pad(grid[:, :-1, :, 2 * q:3 * q], ((0, 0), (1, 0), (0, 0), (0, 0)))
    down = jnp.pad(grid[:, 1:, :, 3 * q:], ((0, 0), (0, 1), (0, 0), (0, 0)))
    return jnp.concatenate([left, right, up, down], axis=-1).reshape(b, n, d)

def bishift_seq(h):
    half = h.shape[-1] // 2
    prev = jnp.pad(h[:, :-1, :half], ((0, 0), (1, 0), (0, 0)))
    nxt = jnp.pad(h[:, 1:, half:], ((0, 0), (0, 1), (0, 0)))
    return jnp.concatenate([prev, nxt], axis=-1)

def to_heads(t, n_heads, head_dim):
    return t.reshape(*t.shape[:-1], n_heads, head_dim)

def rwkv7_branch(h, shifted, mu, w_rkv, w0, w1, w2, a0, a1, a2, k_k, k_a):
    f32 = jnp.float32
    xx = shifted - h
    xr, xw, xk, xv, xa, xg = (h + xx * mu[m] for m in range(6))
    r = (xr @ w_rkv[0]).astype(f32)
    k = (xk @ w_rkv[1]).astype(f32)
    v = (xv @ w_rkv[2]).astype(f32)
    d_lora = jnp.einsum('zbtr,zrd->zbtd', jnp.tanh(jnp.einsum('btd,zdr->zbtr', xw, w1)), w2)
    log_w = -RK_DECAY_SCALE * jax.nn.sigmoid((w0[:, None, None, :] + d_lora).astype(f32))
    a_lora = jnp.einsum('zbtr,zrd->zbtd', jnp.einsum('btd,zdr->zbtr', xa, a1), a2)
    a = jax.nn.sigmoid((a0[:, None, None, :] + a_lora).astype(f32))
    kk = to_heads(k * k_k.astype(f32), RK_HEADS, RK_HEAD)
    kk = kk / jnp.maximum(jnp.sqrt(jnp.sum(kk * kk, axis=-1, keepdims=True)), 1e-12)
    k_dir = k[None] * (1.0 + (a - 1.0) * k_a.astype(f32))
    hd = lambda t: to_heads(t, RK_HEADS, RK_HEAD)
    return (hd(r), hd(log_w), kk, hd(a), hd(k_dir), hd(v), xg)

def wkv7_scan(s0, r, w, kk, a, k, v):
    def step(s, inp):
        r_t, w_t, kk_t, a_t, k_t, v_t = inp
        s_kk = jnp.einsum('bhvk,bhk->bhv', s, kk_t)
        s = (s * w_t[:, :, None, :] - s_kk[..., None] * (kk_t * a_t)[:, :, None, :]
             + v_t[..., None] * k_t[:, :, None, :])
        return s, jnp.einsum('bhvk,bhk->bhv', s, r_t)
    xs = tuple(jnp.moveaxis(t, 1, 0) for t in (r, w, kk, a, k, v))
    s_final, ys = lax.scan(step, s0, xs)
    return jnp.moveaxis(ys, 0, 1), s_final

def rwkv7_dir_inputs(feats, d, flip):
    r, log_w, kk, a, k_dir, v, _ = feats
    return [flip(t) for t in (r, jnp.exp(log_w[d]), kk, a[d], k_dir[d], v)]

def rwkv7_out(y, feats, r_k, g1, g2, lnx_g, lnx_b, w_o):
    r, _, _, _, k_dir, v, xg = feats
    b, n = y.shape[:2]
    mean = jnp.mean(y, axis=-1, keepdims=True)
    var = jnp.mean(jnp.square(y - mean), axis=-1, keepdims=True)
    yn = ((y - mean) * lax.rsqrt(var + RK_GN_EPS)).reshape(b, n, D_MODEL) * lnx_g + lnx_b
    coef = jnp.einsum('bthn,zbthn,hn->bth', r, k_dir, r_k.astype(jnp.float32))
    bonus = (coef[..., None] * v).reshape(b, n, D_MODEL)
    gate = jax.nn.sigmoid(xg @ g1) @ g2
    return ((yn + bonus).astype(xg.dtype) * gate) @ w_o

def rwkv7_mixer(h, hc, n_rows, mu, w_rkv, w0, w1, w2, a0, a1, a2, g1, g2, k_k, k_a, r_k,
                lnx_g, lnx_b, w_o, want_ctx):
    lat = rwkv7_branch(h, qshift_grid(h, n_rows), mu, w_rkv, w0, w1, w2, a0, a1, a2, k_k, k_a)
    cx = rwkv7_branch(hc, bishift_seq(hc), mu, w_rkv, w0, w1, w2, a0, a1, a2, k_k, k_a)
    zero_state = jnp.zeros((h.shape[0], RK_HEADS, RK_HEAD, RK_HEAD), jnp.float32)
    y_lat = 0.0
    y_ctx = 0.0
    for d in range(2):
        flip = flip_time if d == 1 else identity
        yc, s_ctx = wkv7_scan(zero_state, *rwkv7_dir_inputs(cx, d, flip))
        yl, _ = wkv7_scan(s_ctx, *rwkv7_dir_inputs(lat, d, flip))
        y_lat = y_lat + flip(yl)
        y_ctx = y_ctx + flip(yc)
    out_lat = rwkv7_out(y_lat, lat, r_k, g1, g2, lnx_g, lnx_b, w_o)
    out_ctx = rwkv7_out(y_ctx, cx, r_k, g1, g2, lnx_g, lnx_b, w_o) if want_ctx else None
    return out_lat, out_ctx

def centred_pool_minus_self(x, window):
    n = x.shape[-2]
    xf = x.astype(jnp.float32)
    csum = jnp.cumsum(xf, axis=-2)
    csum = jnp.concatenate([jnp.zeros_like(csum[..., :1, :]), csum], axis=-2)
    t = jnp.arange(n)
    lo = jnp.clip(t - window // 2, 0, n)
    hi = jnp.clip(t + window // 2, 0, n)
    total = jnp.take(csum, hi, axis=-2) - jnp.take(csum, lo, axis=-2)
    count = (hi - lo).astype(jnp.float32)[:, None]
    return (total / count - xf).astype(x.dtype)

def pool_mixer(h, pool_w, pool_scale):
    outs = []
    for gi, win in enumerate(POOL_WINDOWS):
        xg = h[..., gi * POOL_GROUP:(gi + 1) * POOL_GROUP]
        outs.append(centred_pool_minus_self(xg, win) @ pool_w[gi])
    return jnp.concatenate(outs, axis=-1) * pool_scale

def depthwise_conv_centred(x, w):
    left = GDN_CONV // 2
    right = GDN_CONV - 1 - left
    return lax.conv_general_dilated(x, w[:, None, :], window_strides=(1,), padding=[(left, right)],
                                    dimension_numbers=('NWC', 'WIO', 'NWC'),
                                    feature_group_count=x.shape[-1])

def l2_normalize(t, eps):
    return t * lax.rsqrt(jnp.sum(t * t, axis=-1, keepdims=True) + eps)

def gdn_features(h, w_in, conv_w, a_log, dt_bias):
    f32 = jnp.float32
    b, n, d = h.shape
    proj = h @ w_in
    qkv = jax.nn.silu(depthwise_conv_centred(proj[..., :3 * d], conv_w)).astype(f32)
    q, k, v = (to_heads(t, GDN_HEADS, GDN_HEAD) for t in jnp.split(qkv, 3, axis=-1))
    q = l2_normalize(q, 1e-6) * GDN_HEAD ** -0.5
    k = l2_normalize(k, 1e-6)
    z = proj[..., 3 * d:4 * d]
    a_pre = proj[..., 4 * d:4 * d + 2 * GDN_HEADS].astype(f32).reshape(b, n, 2, GDN_HEADS)
    b_pre = proj[..., 4 * d + 2 * GDN_HEADS:].astype(f32).reshape(b, n, 2, GDN_HEADS)
    g = -jnp.exp(a_log.astype(f32)) * jax.nn.softplus(a_pre + dt_bias.astype(f32))
    beta = jax.nn.sigmoid(b_pre)
    return q, k, v, z, g, beta

def gated_delta_chunked(q, k, v, g, beta, s0):
    b, n, nh, dk = k.shape
    c = GDN_CHUNK
    nc = n // c

    def chunks(t):
        t = jnp.moveaxis(t, 2, 1)
        return t.reshape(b, nh, nc, c, *t.shape[3:])

    q, k, v, g, beta = chunks(q), chunks(k), chunks(v), chunks(g), chunks(beta)
    gc = jnp.cumsum(g, axis=-1)
    causal = jnp.tril(jnp.ones((c, c), bool))
    strict = jnp.tril(jnp.ones((c, c), bool), -1)
    decay = jnp.exp(jnp.where(causal, gc[..., :, None] - gc[..., None, :], -jnp.inf))
    kb = k * beta[..., None]
    vb = v * beta[..., None]
    lower = jnp.where(strict, jnp.einsum('bhnid,bhnjd->bhnij', kb, k) * decay, 0.0)
    eye = jnp.eye(c, dtype=lower.dtype)
    tmat = lax.linalg.triangular_solve(eye + lower, jnp.broadcast_to(eye, lower.shape),
                                       left_side=True, lower=True)
    u = tmat @ vb
    w = tmat @ (kb * jnp.exp(gc)[..., None])
    a_qk = jnp.where(causal, jnp.einsum('bhnid,bhnjd->bhnij', q, k) * decay, 0.0)
    q_dec = q * jnp.exp(gc)[..., None]
    k_dec = k * jnp.exp(gc[..., -1:] - gc)[..., None]
    g_last = jnp.exp(gc[..., -1])

    def step(s, inp):
        u_i, w_i, q_i, k_i, a_i, gl_i = inp
        v_new = u_i - w_i @ s
        o_i = q_i @ s + a_i @ v_new
        s = s * gl_i[..., None, None] + jnp.swapaxes(k_i, -1, -2) @ v_new
        return s, o_i

    xs = tuple(jnp.moveaxis(t, 2, 0) for t in (u, w, q_dec, k_dec, a_qk, g_last))
    s_final, o = lax.scan(step, s0, xs)
    o = jnp.moveaxis(o, 0, 2).reshape(b, nh, n, -1)
    return jnp.moveaxis(o, 1, 2), s_final

def gdn_out(o, z, norm_w, w_o):
    b, n = z.shape[:2]
    on = o * lax.rsqrt(jnp.mean(o * o, axis=-1, keepdims=True) + GDN_NORM_EPS) * norm_w.astype(jnp.float32)
    zf = to_heads(z.astype(jnp.float32), GDN_HEADS, GDN_HEAD)
    y = (on * jax.nn.silu(zf)).reshape(b, n, D_MODEL).astype(z.dtype)
    return y @ w_o

def gdn_mixer(h, hc, w_in, conv_w, a_log, dt_bias, norm_w, w_o, want_ctx):
    lq, lk, lv, lz, lg, lb = gdn_features(h, w_in, conv_w, a_log, dt_bias)
    cq, ck, cv, cz, cg, cb = gdn_features(hc, w_in, conv_w, a_log, dt_bias)
    zero_state = jnp.zeros((h.shape[0], GDN_HEADS, GDN_HEAD, GDN_HEAD), jnp.float32)
    o_lat = 0.0
    o_ctx = 0.0
    for d in range(2):
        flip = flip_time if d == 1 else identity
        oc, s_ctx = gated_delta_chunked(flip(cq), flip(ck), flip(cv), flip(cg[:, :, d]), flip(cb[:, :, d]),
                                        zero_state)
        ol, _ = gated_delta_chunked(flip(lq), flip(lk), flip(lv), flip(lg[:, :, d]), flip(lb[:, :, d]), s_ctx)
        o_lat = o_lat + flip(ol)
        o_ctx = o_ctx + flip(oc)
    y_lat = gdn_out(o_lat, lz, norm_w, w_o)
    y_ctx = gdn_out(o_ctx, cz, norm_w, w_o) if want_ctx else None
    return y_lat, y_ctx

def swiglu(h, w1, w3, w2):
    return (jax.nn.silu(h @ w1) * (h @ w3)) @ w2

def moe_swiglu(h, router_w, router_b, w1, w3, w2):
    logits = (h @ router_w).astype(jnp.float32) + router_b.astype(jnp.float32)
    top_logit, top_idx = lax.top_k(logits, TOP_K)
    top_p = jax.nn.softmax(top_logit, axis=-1)
    gates = jnp.einsum('btk,btke->bte', top_p,
                       jax.nn.one_hot(top_idx, N_EXPERTS, dtype=jnp.float32)).astype(h.dtype)
    y = jnp.zeros_like(h)
    for e in range(N_EXPERTS):
        y = y + gates[..., e:e + 1] * swiglu(h, w1[e], w3[e], w2[e])
    return y

def first_inputs(seed: int = 0) -> dict:
    key = jax.random.key(seed)
    ks = iter(jax.random.split(key, 64))
    f32 = jnp.float32

    def nrm(shape, std):
        return jax.random.normal(next(ks), shape, f32) * std

    def near_one(shape):
        return 1.0 + nrm(shape, 0.1)

    D, H, N = D_MODEL, RK_HEADS, RK_HEAD
    NA, NB, NC, ND, NM = N_RWKV_LAYERS, N_POOL_LAYERS, N_GDN_LAYERS, N_DENSE_LAYERS, N_MOE_LAYERS
    dt = jnp.exp(jax.random.uniform(next(ks), (NC, 2, GDN_HEADS), f32, math.log(1e-3), math.log(1e-1)))
    gdn_dt_bias = dt + jnp.log(-jnp.expm1(-dt))
    return {
        'x': nrm((BATCH, SEQ, D), 1.0),
        'c': nrm((BATCH, D), 1.0),
        'ctx': nrm((BATCH, CTX_LEN, D), 1.0),
        'c_ctx': nrm((D,), 1.0),
        'ada_w': nrm((DEPTH, D, 6 * D), D ** -0.5),
        'ada_b': nrm((DEPTH, 6 * D), 0.02),
        'ln_g': near_one((DEPTH, 2, D)),
        'ln_b': nrm((DEPTH, 2, D), 0.02),
        'rk_mu': jax.random.uniform(next(ks), (NA, 6, D), f32),
        'rk_w_rkv': nrm((NA, 3, D, D), D ** -0.5),
        'rk_w0': nrm((NA, 2, D), 1.0),
        'rk_w1': nrm((NA, 2, D, RK_DECAY_LORA), D ** -0.5),
        'rk_w2': nrm((NA, 2, RK_DECAY_LORA, D), 0.5 * RK_DECAY_LORA ** -0.5),
        'rk_a0': nrm((NA, 2, D), 0.5),
        'rk_a1': nrm((NA, 2, D, RK_ICLR_LORA), D ** -0.5),
        'rk_a2': nrm((NA, 2, RK_ICLR_LORA, D), 0.5 * RK_ICLR_LORA ** -0.5),
        'rk_g1': nrm((NA, D, RK_GATE_LORA), D ** -0.5),
        'rk_g2': nrm((NA, RK_GATE_LORA, D), RK_GATE_LORA ** -0.5),
        'rk_k_k': near_one((NA, D)),
        'rk_k_a': near_one((NA, D)),
        'rk_r_k': nrm((NA, H, N), 0.1),
        'rk_lnx_g': near_one((NA, D)),
        'rk_lnx_b': nrm((NA, D), 0.02),
        'rk_w_o': nrm((NA, D, D), DN_BETA * D ** -0.5),
        'pool_w': nrm((NB, len(POOL_WINDOWS), POOL_GROUP, POOL_GROUP), DN_BETA * POOL_GROUP ** -0.5),
        'pool_scale': near_one((NB, D)),
        'gdn_w_in': nrm((NC, D, GDN_IN), D ** -0.5),
        'gdn_conv_w': nrm((NC, GDN_CONV, 3 * D), GDN_CONV ** -0.5),
        'gdn_a_log': jnp.log(jax.random.uniform(next(ks), (NC, 2, GDN_HEADS), f32, 1.0, 16.0)),
        'gdn_dt_bias': gdn_dt_bias,
        'gdn_norm_w': near_one((NC, GDN_HEAD)),
        'gdn_w_o': nrm((NC, D, D), DN_BETA * D ** -0.5),
        'ffn_w1': nrm((ND, D, D_FF), D ** -0.5),
        'ffn_w3': nrm((ND, D, D_FF), D ** -0.5),
        'ffn_w2': nrm((ND, D_FF, D), DN_BETA * D_FF ** -0.5),
        'moe_router_w': nrm((NM, D, N_EXPERTS), D ** -0.5),
        'moe_router_b': nrm((NM, N_EXPERTS), 0.01),
        'moe_w1': nrm((NM, N_EXPERTS, D, D_FF_EXPERT), D ** -0.5),
        'moe_w3': nrm((NM, N_EXPERTS, D, D_FF_EXPERT), D ** -0.5),
        'moe_w2': nrm((NM, N_EXPERTS, D_FF_EXPERT, D), DN_BETA * D_FF_EXPERT ** -0.5),
    }

def first_block(x, c, ctx, c_ctx, ada_w, ada_b, ln_g, ln_b,
              rk_mu, rk_w_rkv, rk_w0, rk_w1, rk_w2, rk_a0, rk_a1, rk_a2, rk_g1, rk_g2,
              rk_k_k, rk_k_a, rk_r_k, rk_lnx_g, rk_lnx_b, rk_w_o,
              pool_w, pool_scale,
              gdn_w_in, gdn_conv_w, gdn_a_log, gdn_dt_bias, gdn_norm_w, gdn_w_o,
              ffn_w1, ffn_w3, ffn_w2,
              moe_router_w, moe_router_b, moe_w1, moe_w3, moe_w2):
    b, n, d = x.shape
    n_rows = n // GRID_W
    for i in range(DEPTH):
        want_ctx = i < DEPTH - 1
        mod = jax.nn.silu(c) @ ada_w[i] + ada_b[i]
        mod_c = jax.nn.silu(c_ctx) @ ada_w[i] + ada_b[i]
        sh1, sc1, gt1, sh2, sc2, gt2 = jnp.split(mod[:, None, :], 6, axis=-1)
        csh1, csc1, cgt1, csh2, csc2, cgt2 = jnp.split(mod_c, 6, axis=-1)
        h = x * (1.0 + sc1) + sh1
        hc = ctx * (1.0 + csc1) + csh1
        kind, j = i % N_MIXERS, i // N_MIXERS
        if kind == 0:
            y, yc = rwkv7_mixer(h, hc, n_rows, rk_mu[j], rk_w_rkv[j], rk_w0[j], rk_w1[j], rk_w2[j],
                                rk_a0[j], rk_a1[j], rk_a2[j], rk_g1[j], rk_g2[j], rk_k_k[j], rk_k_a[j],
                                rk_r_k[j], rk_lnx_g[j], rk_lnx_b[j], rk_w_o[j], want_ctx)
        elif kind == 1:
            y = pool_mixer(h.reshape(b, n_rows, GRID_W, d), pool_w[j], pool_scale[j]).reshape(b, n, d)
            yc = pool_mixer(hc, pool_w[j], pool_scale[j]) if want_ctx else None
        else:
            y, yc = gdn_mixer(h, hc, gdn_w_in[j], gdn_conv_w[j], gdn_a_log[j], gdn_dt_bias[j],
                              gdn_norm_w[j], gdn_w_o[j], want_ctx)
        if i % 2 == 0:
            e = i // 2
            channel_mixer = lambda t, e=e: swiglu(t, ffn_w1[e], ffn_w3[e], ffn_w2[e])
        else:
            e = i // 2
            channel_mixer = lambda t, e=e: moe_swiglu(t, moe_router_w[e], moe_router_b[e],
                                                      moe_w1[e], moe_w3[e], moe_w2[e])
        x = layer_norm(DN_ALPHA * x + gt1 * y, ln_g[i, 0], ln_b[i, 0])
        x = layer_norm(DN_ALPHA * x + gt2 * channel_mixer(x * (1.0 + sc2) + sh2), ln_g[i, 1], ln_b[i, 1])
        if want_ctx:
            ctx = layer_norm(DN_ALPHA * ctx + cgt1 * yc, ln_g[i, 0], ln_b[i, 0])
            ctx = layer_norm(DN_ALPHA * ctx + cgt2 * channel_mixer(ctx * (1.0 + csc2) + csh2),
                             ln_g[i, 1], ln_b[i, 1])
    return x


DEPTH_2 = 1

HEAD_DIM = 64
MIX_WIDTH = D_MODEL
WIDTH_A = MIX_WIDTH // 2
WIDTH_B = MIX_WIDTH - WIDTH_A
N_HEADS_A = WIDTH_A // HEAD_DIM
DIFF_V_DIM = 2 * HEAD_DIM
N_HEADS_B = WIDTH_B // DIFF_V_DIM
DILATED_PATTERNS = ((128, 1), (512, 4), (2048, 16))
CONV_WIDTH = 3
NUM_BUCKETS = 32
MAX_DISTANCE = 2048
N_BIAS_HEADS = N_HEADS_A + N_HEADS_B
Q_BLOCK = 128
EPS = 1e-6
NEG = -1e30
PROJ_WIDTH = 3 * WIDTH_A + 2 * N_HEADS_B * 2 * HEAD_DIM + WIDTH_B


def rms_norm(x, g):
    xf = x.astype(jnp.float32)
    return xf * lax.rsqrt(jnp.mean(xf * xf, axis=-1, keepdims=True) + EPS) * g

def modulate(h, shift, scale):
    return h * (1.0 + scale) + shift

def t5_bucket(rel):
    nb = NUM_BUCKETS // 2
    max_exact = nb // 2
    base = jnp.where(rel > 0, nb, 0)
    n = jnp.abs(rel)
    nf = jnp.maximum(n, 1).astype(jnp.float32)
    large = max_exact + (jnp.log(nf / max_exact) / math.log(MAX_DISTANCE / max_exact)
                         * (nb - max_exact)).astype(jnp.int32)
    large = jnp.minimum(large, nb - 1)
    return base + jnp.where(n < max_exact, n, large)

def dilated_window_attention(q, k, v, table, window, dilation):
    B, H, S, Dh = q.shape
    half = window // (2 * dilation)
    L = S // dilation
    nblk = -(-L // half)
    pad = nblk * half - L

    def by_residue(t):
        return t.reshape(B, H, L, dilation, Dh).transpose(0, 1, 3, 2, 4)

    qs = jnp.pad(by_residue(q), ((0, 0),) * 3 + ((0, pad), (0, 0))).reshape(B, H, dilation, nblk, half, Dh)

    def band(t):
        tp = jnp.pad(by_residue(t), ((0, 0),) * 3 + ((half, half + pad), (0, 0)))
        tp = tp.reshape(B, H, dilation, nblk + 2, half, Dh)
        return jnp.concatenate([tp[:, :, :, :-2], tp[:, :, :, 1:-1], tp[:, :, :, 2:]], axis=4)

    kb, vb = band(k), band(v)
    qi = jnp.arange(half)
    kt = jnp.arange(3 * half)
    rel = kt[None, :] - half - qi[:, None]
    bias = table[t5_bucket(rel * dilation)].transpose(2, 0, 1)
    kpos = jnp.arange(nblk)[:, None] * half + kt[None, :] - half
    valid = (jnp.abs(rel) <= half)[None] & ((kpos >= 0) & (kpos < L))[:, None, :]
    s = jnp.einsum('bhrnqd,bhrnkd->bhrnqk', qs, kb) * (Dh ** -0.5) + bias[None, :, None, None]
    s = jnp.where(valid, s, NEG)
    lse = jax.nn.logsumexp(s, axis=-1)
    p = jnp.exp(s - lse[..., None])
    o = jnp.einsum('bhrnqk,bhrnkd->bhrnqd', p, vb)
    o = o.reshape(B, H, dilation, nblk * half, Dh)[:, :, :, :L].transpose(0, 1, 3, 2, 4).reshape(B, H, S, Dh)
    lse = lse.reshape(B, H, dilation, nblk * half)[:, :, :, :L].transpose(0, 1, 3, 2).reshape(B, H, S)
    return o, lse

def differential_attention(q1, q2, k1, k2, v, table, lam):
    B, H, S, Dh = q1.shape
    nqb = S // Q_BLOCK
    kpos = jnp.arange(S)
    scale = Dh ** -0.5

    def block(args):
        q1b, q2b, start = args
        rel = kpos[None, :] - (start + jnp.arange(Q_BLOCK))[:, None]
        bias = table[t5_bucket(rel)].transpose(2, 0, 1)[None]
        p1 = jax.nn.softmax(jnp.einsum('bhqd,bhkd->bhqk', q1b, k1) * scale + bias, axis=-1)
        p2 = jax.nn.softmax(jnp.einsum('bhqd,bhkd->bhqk', q2b, k2) * scale + bias, axis=-1)
        return jnp.einsum('bhqk,bhkd->bhqd', p1 - lam * p2, v)

    q1s = q1.reshape(B, H, nqb, Q_BLOCK, Dh).transpose(2, 0, 1, 3, 4)
    q2s = q2.reshape(B, H, nqb, Q_BLOCK, Dh).transpose(2, 0, 1, 3, 4)
    starts = jnp.arange(nqb, dtype=jnp.int32) * Q_BLOCK
    o = lax.map(block, (q1s, q2s, starts))
    return o.transpose(1, 2, 0, 3, 4).reshape(B, H, S, v.shape[-1])

def depthwise_conv_centred_2(u, w, b):
    C = u.shape[-1]
    y = lax.conv_general_dilated(u, w[:, None, :].astype(u.dtype), window_strides=(1,), padding='SAME',
                                 dimension_numbers=('NWC', 'WIO', 'NWC'), feature_group_count=C)
    return y + b

def split_heads(t, n_heads, dh):
    B, S, _ = t.shape
    return t.reshape(B, S, n_heads, dh).transpose(0, 2, 1, 3)

def second_inputs(seed: int = 0) -> dict:
    key = jax.random.key(seed)
    ks = jax.random.split(key, 24)
    nrm = jax.random.normal
    f32 = jnp.float32
    return {
        'x': nrm(ks[0], (BATCH, SEQ, D_MODEL), f32),
        'c': nrm(ks[1], (BATCH, D_MODEL), f32),
        'w_ada': nrm(ks[2], (DEPTH_2, D_MODEL, 6 * D_MODEL), f32) * D_MODEL ** -0.5,
        'b_ada': nrm(ks[3], (DEPTH_2, 6 * D_MODEL), f32) * 0.02,
        'norm1_g': 1.0 + 0.1 * nrm(ks[4], (DEPTH_2, D_MODEL), f32),
        'w_in': nrm(ks[5], (DEPTH_2, D_MODEL, PROJ_WIDTH), f32) * D_MODEL ** -0.5,
        'q_norm_a': 1.0 + 0.1 * nrm(ks[6], (DEPTH_2, HEAD_DIM), f32),
        'k_norm_a': 1.0 + 0.1 * nrm(ks[7], (DEPTH_2, HEAD_DIM), f32),
        'q_norm_b': 1.0 + 0.1 * nrm(ks[8], (DEPTH_2, HEAD_DIM), f32),
        'k_norm_b': 1.0 + 0.1 * nrm(ks[9], (DEPTH_2, HEAD_DIM), f32),
        'rel_bias': nrm(ks[10], (NUM_BUCKETS, N_BIAS_HEADS), f32) * 0.3,
        'lambda_q1': nrm(ks[11], (DEPTH_2, HEAD_DIM), f32) * 0.1,
        'lambda_k1': nrm(ks[12], (DEPTH_2, HEAD_DIM), f32) * 0.1,
        'lambda_q2': nrm(ks[13], (DEPTH_2, HEAD_DIM), f32) * 0.1,
        'lambda_k2': nrm(ks[14], (DEPTH_2, HEAD_DIM), f32) * 0.1,
        'subln_g': 1.0 + 0.1 * nrm(ks[15], (DEPTH_2, DIFF_V_DIM), f32),
        'w_out': nrm(ks[16], (DEPTH_2, MIX_WIDTH, D_MODEL), f32) * MIX_WIDTH ** -0.5,
        'norm2_g': 1.0 + 0.1 * nrm(ks[17], (DEPTH_2, D_MODEL), f32),
        'w_up': nrm(ks[18], (DEPTH_2, D_MODEL, 2 * D_FF), f32) * D_MODEL ** -0.5,
        'conv_w': nrm(ks[19], (DEPTH_2, CONV_WIDTH, 2 * D_FF), f32) * CONV_WIDTH ** -0.5,
        'conv_b': nrm(ks[20], (DEPTH_2, 2 * D_FF), f32) * 0.02,
        'w_down': nrm(ks[21], (DEPTH_2, D_FF, D_MODEL), f32) * D_FF ** -0.5,
    }

def second_block(x, c, w_ada, b_ada, norm1_g, w_in, q_norm_a, k_norm_a, q_norm_b, k_norm_b, rel_bias,
              lambda_q1, lambda_k1, lambda_q2, lambda_k2, subln_g, w_out, norm2_g, w_up, conv_w, conv_b,
              w_down):
    B, S, D = x.shape
    out_dtype = x.dtype
    h = x.astype(jnp.float32)
    c_act = jax.nn.silu(c.astype(jnp.float32))
    table_a = rel_bias[:, :N_HEADS_A].astype(jnp.float32)
    table_b = rel_bias[:, N_HEADS_A:].astype(jnp.float32)
    qk_b = N_HEADS_B * 2 * HEAD_DIM
    splits = [WIDTH_A, 2 * WIDTH_A, 3 * WIDTH_A, 3 * WIDTH_A + qk_b, 3 * WIDTH_A + 2 * qk_b]

    for layer in range(DEPTH_2):
        lambda_init = 0.8 - 0.6 * math.exp(-0.3 * layer)
        mod = (c_act @ w_ada[layer] + b_ada[layer])[:, None, :]
        shift1, scale1, gate1, shift2, scale2, gate2 = jnp.split(mod, 6, axis=-1)

        hn = modulate(rms_norm(h, norm1_g[layer]), shift1, scale1)
        proj = hn @ w_in[layer]
        qa, ka, va, qb, kb, vb = jnp.split(proj, splits, axis=-1)

        qa = rms_norm(split_heads(qa, N_HEADS_A, HEAD_DIM), q_norm_a[layer])
        ka = rms_norm(split_heads(ka, N_HEADS_A, HEAD_DIM), k_norm_a[layer])
        va = split_heads(va, N_HEADS_A, HEAD_DIM)
        outs, lses = [], []
        for window, dilation in DILATED_PATTERNS:
            o, l = dilated_window_attention(qa, ka, va, table_a, window, dilation)
            outs.append(o)
            lses.append(l)
        wts = jax.nn.softmax(jnp.stack(lses, axis=0), axis=0)
        o_a = jnp.sum(jnp.stack(outs, axis=0) * wts[..., None], axis=0)
        o_a = o_a.transpose(0, 2, 1, 3).reshape(B, S, WIDTH_A)

        qb = qb.reshape(B, S, N_HEADS_B, 2, HEAD_DIM).transpose(3, 0, 2, 1, 4)
        kb = kb.reshape(B, S, N_HEADS_B, 2, HEAD_DIM).transpose(3, 0, 2, 1, 4)
        qb = rms_norm(qb, q_norm_b[layer])
        kb = rms_norm(kb, k_norm_b[layer])
        vb = split_heads(vb, N_HEADS_B, DIFF_V_DIM)
        lam = (jnp.exp(jnp.sum(lambda_q1[layer] * lambda_k1[layer]).astype(jnp.float32))
               - jnp.exp(jnp.sum(lambda_q2[layer] * lambda_k2[layer]).astype(jnp.float32)) + lambda_init)
        o_b = differential_attention(qb[0], qb[1], kb[0], kb[1], vb, table_b, lam)
        o_b = rms_norm(o_b, subln_g[layer]) * (1.0 - lambda_init)
        o_b = o_b.transpose(0, 2, 1, 3).reshape(B, S, WIDTH_B)

        mixed = jnp.concatenate([o_a, o_b], axis=-1) @ w_out[layer]
        h = h + gate1 * mixed

        hn = modulate(rms_norm(h, norm2_g[layer]), shift2, scale2)
        u = depthwise_conv_centred_2(hn @ w_up[layer], conv_w[layer], conv_b[layer])
        val, gate = jnp.split(u, 2, axis=-1)
        h = h + gate2 * ((jax.nn.silu(gate) * val) @ w_down[layer])

    return h.astype(out_dtype)


def setup_inputs(seed=0):
    out = dict(first_inputs(seed))
    for name, value in second_inputs(seed + 1).items():
        if name != "x":
            out[name + "_2"] = value
    return out


def reference(
    x, c, ctx, c_ctx, ada_w, ada_b, ln_g, ln_b, rk_mu, rk_w_rkv, rk_w0, rk_w1, rk_w2, rk_a0,
    rk_a1, rk_a2, rk_g1, rk_g2, rk_k_k, rk_k_a, rk_r_k, rk_lnx_g, rk_lnx_b, rk_w_o, pool_w,
    pool_scale, gdn_w_in, gdn_conv_w, gdn_a_log, gdn_dt_bias, gdn_norm_w, gdn_w_o, ffn_w1,
    ffn_w3, ffn_w2, moe_router_w, moe_router_b, moe_w1, moe_w3, moe_w2, c_2, w_ada_2, b_ada_2,
    norm1_g_2, w_in_2, q_norm_a_2, k_norm_a_2, q_norm_b_2, k_norm_b_2, rel_bias_2, lambda_q1_2,
    lambda_k1_2, lambda_q2_2, lambda_k2_2, subln_g_2, w_out_2, norm2_g_2, w_up_2, conv_w_2,
    conv_b_2, w_down_2,
):
    x = first_block(
        x, c, ctx, c_ctx, ada_w, ada_b, ln_g, ln_b, rk_mu, rk_w_rkv, rk_w0, rk_w1, rk_w2, rk_a0,
        rk_a1, rk_a2, rk_g1, rk_g2, rk_k_k, rk_k_a, rk_r_k, rk_lnx_g, rk_lnx_b, rk_w_o, pool_w,
        pool_scale, gdn_w_in, gdn_conv_w, gdn_a_log, gdn_dt_bias, gdn_norm_w, gdn_w_o, ffn_w1,
        ffn_w3, ffn_w2, moe_router_w, moe_router_b, moe_w1, moe_w3, moe_w2,
    )
    return second_block(
        x, c_2, w_ada_2, b_ada_2, norm1_g_2, w_in_2, q_norm_a_2, k_norm_a_2, q_norm_b_2,
        k_norm_b_2, rel_bias_2, lambda_q1_2, lambda_k1_2, lambda_q2_2, lambda_k2_2, subln_g_2,
        w_out_2, norm2_g_2, w_up_2, conv_w_2, conv_b_2, w_down_2,
    )


_drawn_inputs = setup_inputs


def setup_inputs(seed=0):
    import zlib

    import numpy as np

    out = dict(_drawn_inputs(seed))
    spreads = {}
    factors = {'ctx': 5.675,
     'c_ctx': 5.844,
     'rk_w1': 3.408,
     'rk_w2': 3.507,
     'rk_k_k': 6.218,
     'rk_lnx_g': 3.09,
     'rk_lnx_b': 8.0,
     'moe_router_b': 5.662,
     'norm1_g_2': 3.198,
     'q_norm_a_2': 8.0,
     'k_norm_a_2': 8.0,
     'q_norm_b_2': 8.0,
     'k_norm_b_2': 8.0,
     'lambda_q1_2': 3.799,
     'lambda_k1_2': 3.555,
     'lambda_q2_2': 4.277,
     'lambda_k2_2': 3.64,
     'conv_b_2': 5.056}
    for name, (base, spread) in spreads.items():
        noise = np.random.default_rng([zlib.crc32(name.encode()), seed]).standard_normal(out[name].shape)
        drawn = base * np.exp(spread * noise) if base else spread * noise
        out[name] = jnp.asarray(drawn.astype(out[name].dtype))
    for name, factor in factors.items():
        out[name] = (out[name] * factor).astype(out[name].dtype)
    return out
```

```python
from contextlib import ExitStack

import numpy as np
from concourse import mybir
from concourse.bass import AP, ds

F32 = mybir.dt.float32
ALU = mybir.AluOpType
ACT = mybir.ActivationFunctionType
AX = mybir.AxisListType.X

P = 128
D = 1024
KT = D // P
SEQ = 512
CTX = 256
TOK = CTX + SEQ
HALF = TOK // 2
BANK = 512
FF = 2816
FT = FF // P
NE = 8
FE = 1408
ET = FE // P
ALPHA = float((2 * 2) ** 0.25)
LN_EPS = 1e-5
GN_EPS = 64e-5
RMS_EPS = 1e-6
DECAY = float(np.exp(-0.5))
LAMBDA_INIT = 0.8 - 0.6
GRID_W = 64
CH = 64
NCH = TOK // CH
CCH = CTX // CH
SLOTS = 3
SLOT = FT * P
PAIR_W = 3 * D + 5 * P
WINDOWS = (2, 4, 8, 16)
PADW = 8
LEVELS = (1, 2, 4, 8, 16, 32)

COLS = {}
_at = 0
for _name, _n in (("c", 24), ("cc", 24), ("adab", 144), ("lng", 32), ("lnb", 32), ("mu", 48), ("pair", 72),
                  ("pscale", 8), ("n1g", 8), ("n2g", 8), ("qna", 1), ("kna", 1), ("qnb", 1), ("knb", 1),
                  ("sub", 1), ("lam", 4)):
    COLS[_name] = (_at, _at + _n)
    _at += _n
NCOL = _at
CONST = {}
_at = 0
for _name, _n in (("id", P), ("hsum", P), ("hmean", P), ("mean", P), ("ones", P), ("mS", 4 * P), ("mK", 4 * P),
                  ("mL", 12 * P), ("scan", TOK), ("rcnt", 4 * GRID_W)):
    CONST[_name] = (_at, _at + _n)
    _at += _n
NCONST = _at


class Marks:

    def __init__(self, sem, names):
        self.sem, self.names, self.next = sem, list(names), 0
        assert len(set(self.names)) == len(self.names)

    def at(self, name, it=0):
        return it * len(self.names) + self.names.index(name) + 1

    def did(self, name):
        assert self.names[self.next % len(self.names)] == name, (name, self.names[self.next % len(self.names)])
        self.next += 1
        return self.sem, 1


class Ring:

    def __init__(self, nc, ctx):
        self.all = ctx.enter_context(nc.sbuf_tensor("w_ring", [P, SLOTS * SLOT], F32))
        self.buf = [self.all[:, s * SLOT:(s + 1) * SLOT] for s in range(SLOTS)]
        self.loaded = [ctx.enter_context(nc.semaphore(f"w_loaded{s}")) for s in range(SLOTS)]
        self.used = [ctx.enter_context(nc.semaphore(f"w_used{s}")) for s in range(SLOTS)]
        self.drained = [ctx.enter_context(nc.semaphore(f"ps_drained{s}")) for s in range(SLOTS)]
        self.fills = [0] * SLOTS
        self.drains = [0] * SLOTS

    def end(self, n, drains_per_chunk=1):
        for s in range(SLOTS):
            k = n // SLOTS + (s < n % SLOTS)
            self.fills[s] += k
            self.drains[s] += k * drains_per_chunk


def over_chunks(eng, n, body):
    trips = n // SLOTS
    if trips:
        with eng.Fori(0, trips) as i:
            for s in range(SLOTS):
                body(s, i, i * SLOTS + s)
    for s in range(n % SLOTS):
        body(s, trips, trips * SLOTS + s)


def load_chunks(sp, ring, src, n, width):

    def body(s, trip, c):
        sp.wait_ge(ring.used[s], ring.fills[s] + trip)
        sp.dma_start(ring.buf[s][:, 0:width], src[ds(c, 1), :, :].rearrange("a p n -> (a p) n")).then_inc(
            ring.loaded[s], 16)

    over_chunks(sp, n, body)


def project(pe, ring, ps, n, m_tiles, k_tiles, moving, width=BANK, between=None):

    def body(s, trip, c):
        pe.wait_ge(ring.loaded[s], (ring.fills[s] + trip + 1) * 16)
        pe.wait_ge(ring.drained[s], ring.drains[s] + trip)
        for m in range(m_tiles):
            for k in range(k_tiles):
                at = (k * m_tiles + m) * P
                last = pe.matmul(ps[:, 2 * s + m, 0:width], ring.buf[s][:, at:at + P], moving(k),
                                 start=(k == 0), stop=(k == k_tiles - 1))
        last.then_inc(ring.used[s], 1)

    over_chunks(pe, n, body)


class Kernel:
    def __init__(self, nc, A):
        self.nc, self.A = nc, A
        self.ctx = ExitStack()

    def sb(self, ctx, name, *shape):
        return ctx.enter_context(self.nc.sbuf_tensor("sb_" + name, [P, *shape], F32))

    def marks(self, name, names):
        return Marks(self.ctx.enter_context(self.nc.semaphore(name)), names)

    def sem(self, name):
        return self.ctx.enter_context(self.nc.semaphore(name))

    def col(self, name, i=0, n=1):
        a = COLS[name][0] + i
        return self.par[:, a:a + n]

    def con(self, name, i=0, n=P):
        a = CONST[name][0] + i
        return self.cst[:, a:a + n]

    def build(self):
        nc = self.nc
        with self.ctx:
            ctx = self.ctx
            self.ring = Ring(nc, ctx)
            self.par = self.sb(ctx, "params", NCOL)
            self.cst = self.sb(ctx, "consts", NCONST)
            self.mod = self.sb(ctx, "mod", 3, 48, 2)
            self.tiny = self.sb(ctx, "tiny", 8)
            self.ps = ctx.enter_context(nc.psum_tensor("ps", [P, 8, BANK], F32))
            self.adaln()
            self.B0 = self.sb(ctx, "b0", KT, SEQ)
            self.rwkv()
            self.X, self.T, self.H = (self.sb(ctx, n, KT, SEQ) for n in ("x", "t", "hm"))
            for stage in (self.rwkv_out, self.ffn, self.pool, self.moe, self.attention, self.convffn):
                stage()

    def adaln(self):
        nc, A, ring, ps, mod = self.nc, self.A, self.ring, self.ps, self.mod
        s_par = self.sem("params_in")
        V = nc.vector
        NB = 4
        pe_m = self.marks("ada_pe", ["cols"])
        act_m = self.marks("ada_act", ["row0", "row1", "row2"])
        dve_m = self.marks("ada_dve", ["mod"])
        s_silu = self.sem("silu_c")
        s_fix = self.sem("mod_plus_one")
        with ExitStack() as st:
            cs = self.sb(st, "c_silu", 3, KT, 2)
            row = self.sb(st, "ada_row", 3, BANK)
            with nc.Block() as block:
                @block.sync
                def _(sp):
                    sp.dma_start(self.par[:, :], A["params"]).then_inc(s_par, 16)
                    sp.dma_start(self.cst[:, :], A["consts"]).then_inc(s_par, 16)
                    load_chunks(sp, ring, A["w_ada"], 72, 2048)

                @block.scalar
                def _(act):
                    act.wait_ge(s_par, 32)
                    for v in range(2):
                        last = nc.scalar.activation(cs[:, :, :, v],
                                                    self.col(("c", "cc")[v], 0, 24).rearrange("p (a k) -> p a k", a=3),
                                                    ACT.Silu)
                        last.then_inc(s_silu, 1)
                    for a in range(3):
                        with act.Fori(a * NB, (a + 1) * NB) as i:
                            act.wait_ge(pe_m.sem, i)
                            for b in range(3):
                                act.wait_ge(ring.used[(2 * b + 1) % SLOTS], 2 * i + (2 * b + 1) // SLOTS + 1)
                                nc.scalar.activation(row[0:2, b, :], ps[0:2, b, :], ACT.Copy).then_inc(
                                    *act_m.did(f"row{b}"))

                @block.tensor
                def _(pe):
                    pe.wait_ge(s_silu, 2)
                    pe.wait_ge(s_par, 32)
                    for a in range(3):
                        with pe.Fori(a * NB, (a + 1) * NB) as i:
                            for b in range(3):
                                for half in range(2):
                                    ch = 2 * b + half
                                    s = ch % SLOTS
                                    k = 2 * i + ch // SLOTS
                                    pe.wait_ge(ring.loaded[s], (k + 1) * 16)
                                    for kt in range(4):
                                        last = pe.matmul(ps[0:2, b, :], cs[:, a, 4 * half + kt, :],
                                                         ring.buf[s][:, kt * BANK:(kt + 1) * BANK],
                                                         start=(half == 0 and kt == 0), stop=(half == 1 and kt == 3))
                                    last.then_inc(ring.used[s], 1)
                            pe.wait_ge(dve_m.sem, i)
                            for b in range(3):
                                pe.wait_ge(act_m.sem, act_m.at(f"row{b}", i))
                                for j in range(4):
                                    at = 2 * (4 * b + j)
                                    last = pe.matmul(ps[:, 3, at:at + 2], row[0:2, b, j * P:(j + 1) * P],
                                                     self.con("id", 0, 2)[0:2, :], start=True, stop=True)
                            last.then_inc(*pe_m.did("cols"))

                @block.vector
                def _(dve):
                    dve.wait_ge(s_par, 32)
                    for a in range(3):
                        with dve.Fori(0, NB) as i:
                            dve.wait_ge(pe_m.sem, pe_m.at("cols", i + a * NB))
                            dst = mod[:, a, ds(i * 12, 12), :]
                            b = self.par[:, ds(i * 12 + (COLS["adab"][0] + 48 * a), 12)]
                            nc.vector.tensor_tensor(dst, ps[:, 3, 0:24].rearrange("p (a b) -> p a b", b=2),
                                                    b.unsqueeze(2).broadcast_to([P, 12, 2]),
                                                    ALU.add).then_inc(*dve_m.did("mod"))
                    for i, eps in enumerate((LN_EPS, GN_EPS, RMS_EPS)):
                        V.memset(self.tiny[:, i:i + 1], eps)
                    dve.wait_ge(dve_m.sem, 3 * NB)
                    for j in (8, 32):
                        nc.vector.tensor_scalar(mod[:, :, j:j + 8, :], mod[:, :, j:j + 8, :], 1.0, None,
                                                ALU.add).then_inc(s_fix, 1)
        ring.end(72, 0)

    def rwkv(self):
        YG = self.B0
        with ExitStack() as mix:
            xk, xv = self.sb(mix, "xk", KT, TOK), self.sb(mix, "xv", KT, TOK)
            xr = self.sb(mix, "xr", KT, SEQ)
            TW, TA, TG = self.sb(mix, "tw", TOK), self.sb(mix, "ta", TOK), self.sb(mix, "tg", SEQ)
            with ExitStack() as hs:
                h, xx = self.sb(hs, "h", KT, TOK), self.sb(hs, "xx", KT, TOK)
                self.token_mix(h, xx, xk, xv, xr, TW, TA, TG)
            self.pairs(xk, xv, xr, TW, TA, TG, YG)

    def token_mix(self, h, xx, xk, xv, xr, TW, TA, TG):
        nc, A, ring, ps, mod = self.nc, self.A, self.ring, self.ps, self.mod
        V = nc.vector
        s_x, s_lw = self.sem("x_in"), self.sem("lora_in")
        dve_m = self.marks("mix_dve", ["h", "xw", "xa", "xg", "xk", "xv", "xr"])
        s_h = self.sem("h_steps")
        pe_m = self.marks("mix_pe", ["w", "a", "g"])
        act_m = self.marks("mix_act", ["w", "a", "g"])
        lw = [ring.buf[s][:, 0:KT * P] for s in range(3)]
        with nc.Block() as block:
            @block.sync
            def _(sp):
                sp.dma_start(h[:, :, 0:CTX], A["ctxT"]).then_inc(s_x, 16)
                sp.dma_start(h[:, :, CTX:TOK], A["xT"]).then_inc(s_x, 16)
                for i in range(3):
                    sp.dma_start(lw[i], A["w_lora1"][i]).then_inc(s_lw, 16)

            @block.vector
            def _(dve):
                dve.wait_ge(s_x, 32)
                for k in range(KT):
                    for who, a, b in ((1, 0, CTX), (0, CTX, TOK)):
                        last = V.tensor_scalar(h[:, k, a:b], h[:, k, a:b], mod[:, 0, 8 + k, who:who + 1],
                                               mod[:, 0, k, who:who + 1], ALU.mult, ALU.add)
                        last.then_inc(s_h, 1)
                dve.wait_ge(s_h, 2 * KT)
                V.tensor_scalar(xx[:, :, :], h[:, :, :], -1.0, None, ALU.mult).then_inc(*dve_m.did("h"))
                dve.wait_ge(dve_m.sem, dve_m.at("h"))
                ops = [(slice(0, 4), (1, CTX), (0, CTX - 1)), (slice(4, 8), (0, CTX - 1), (1, CTX))]
                for f, (a, b), (c, d) in ops:
                    V.tensor_tensor(xx[:, f, a:b], h[:, f, c:d], h[:, f, a:b], ALU.subtract).then_inc(s_h, 1)
                R = SEQ // GRID_W
                for f, (r0, c0), (nr, ncol), (rs, cs) in (
                        (slice(0, 2), (0, 1), (R, GRID_W - 1), (0, 0)), (slice(2, 4), (0, 0), (R, GRID_W - 1), (0, 1)),
                        (slice(4, 6), (1, 0), (R - 1, GRID_W), (0, 0)), (slice(6, 8), (0, 0), (R - 1, GRID_W), (1, 0))):
                    for k in range(f.start, f.stop):
                        g = h[:, k, CTX:TOK].rearrange("p (r c) -> p r c", c=GRID_W)
                        o = xx[:, k, CTX:TOK].rearrange("p (r c) -> p r c", c=GRID_W)
                        V.tensor_tensor(o[:, r0:r0 + nr, c0:c0 + ncol], g[:, rs:rs + nr, cs:cs + ncol],
                                        g[:, r0:r0 + nr, c0:c0 + ncol], ALU.subtract).then_inc(s_h, 1)
                dve.wait_ge(s_h, 2 * KT + 2 + KT)
                for name, mu, dst, a, free in (("xw", 1, xk, 0, None), ("xa", 4, xv, 0, None), ("xg", 5, xr, CTX, None),
                                               ("xk", 2, xk, 0, "w"), ("xv", 3, xv, 0, "a"), ("xr", 0, xr, CTX, "g")):
                    if free:
                        dve.wait_ge(pe_m.sem, pe_m.at(free))
                    for k in range(KT):
                        last = V.scalar_tensor_tensor(out=dst[:, k, :], in0=xx[:, k, a:TOK],
                                                      scalar=self.col("mu", mu * 8 + k), in1=h[:, k, a:TOK],
                                                      op0=ALU.mult, op1=ALU.add)
                    last.then_inc(*dve_m.did(name))

            @block.tensor
            def _(pe):
                pe.wait_ge(s_lw, 48)
                for i, (name, src, need) in enumerate((("w", xk, "xw"), ("a", xv, "xa"), ("g", xr, "xg"))):
                    pe.wait_ge(dve_m.sem, dve_m.at(need))
                    spans = [(0, HALF), (HALF, TOK)] if i < 2 else [(0, SEQ)]
                    for b, (c, d) in enumerate(spans):
                        for k in range(KT):
                            last = pe.matmul(ps[:, 2 * i + b, 0:d - c], lw[i][:, k * P:(k + 1) * P], src[:, k, c:d],
                                             start=(k == 0), stop=(k == KT - 1))
                    last.then_inc(*pe_m.did(name))

            @block.scalar
            def _(act):
                for i, (name, dst, f) in enumerate((("w", TW, ACT.Tanh), ("a", TA, ACT.Copy), ("g", TG, ACT.Sigmoid))):
                    act.wait_ge(pe_m.sem, pe_m.at(name))
                    if i < 2:
                        o, src = dst[:, :].rearrange("p (a b) -> p a b", a=2), ps[:, 2 * i:2 * i + 2, 0:HALF]
                    else:
                        o, src = dst[:, :], ps[:, 4, :]
                    nc.scalar.activation(o, src, f).then_inc(*act_m.did(name))

    def pairs(self, xk, xv, xr, TW, TA, TG, YG):
        nc, A, ring, ps = self.nc, self.A, self.ring, self.ps
        V, S = nc.vector, nc.scalar
        N = KT
        lin = self.marks("lin_pe", ["k", "v", "r", "g", "w0", "w1", "a0", "a1"])
        nrm = self.marks("norm_pe", ["norm", "coef"])
        f_act = self.marks("feat_act", ["k", "v", "r", "g", "w0", "w1", "a0", "a1", "root", "Px", "Pi", "P"])
        f_dve = self.marks("feat_dve", ["pj", "omka", "kkr", "sq", "max", "rec", "kk", "scan", "ex", "in1", "A", "kka", "B",
                                        "kd", "kdk", "K", "R", "kds", "rr", "coefin", "bonus"])
        o_pe = self.marks("out_pe", ["mean", "var"])
        o_act = self.marks("out_act", ["root"])
        o_dve = self.marks("out_dve", ["Y", "yc", "sq", "rec", "yn", "affine", "bonus", "gated"])
        passed = self.sem("barriers_passed")
        phase, s_w, z_init = self.sem("phase"), self.sem("w_pair_in"), self.sem("state_zeroed")
        loops = []
        for kind, n in (("c", CCH), ("l", NCH - CCH)):
            lat = kind == "l"
            loops.append(dict(
                lat=lat, n=n,
                pool=self.marks(f"{kind}_pool", ["bd"]),
                pe=self.marks(f"{kind}_pe", ["score", "trans", "L"] + [x for i in range(5) for x in (f"X{i}", f"T{i}")]
                              + ["akv", "U", "Z"] + ["Y"] * lat),
                dve=self.marks(f"{kind}_dve", ["sS", "sK", "t0a", "t0b", "t0"]
                               + [x for i in range(5) for x in (f"x{i}", f"t{i + 1}")]),
                act=self.marks(f"{kind}_act", ["trB", "tr", "akv", "U"] + ["y"] * lat + ["z0", "z1"])))

        with ExitStack() as st:
            k, v, kk, t1 = (self.sb(st, n, TOK) for n in ("k", "v", "kk", "t1"))
            r, g, bon = (self.sb(st, n, SEQ) for n in ("r", "g", "bon"))
            a, sg, cs, ex, Pi = (self.sb(st, n, 2, TOK) for n in ("a", "sg", "cs", "ex", "Pi"))
            FR, Y = self.sb(st, "FR", 2, SEQ), self.sb(st, "Y", 2, SEQ)
            PJ = self.sb(st, "pj", 10)
            Z, AT, Us = self.sb(st, "Z", 2, P), self.sb(st, "AT", 2, 2, P), self.sb(st, "Us", 2, P)
            W = ring.all[:, 0:PAIR_W]
            free = [PAIR_W]

            def spare(*shape):
                n = int(np.prod(shape))
                x = ring.all[:, free[0]:free[0] + n]
                free[0] += n
                names = "abcd"[:len(shape)]
                return x.rearrange(f"p ({' '.join(names)}) -> p {' '.join(names)}",
                                   **{q: m for q, m in zip(names[1:], shape[1:])})

            bd = spare(2, 5, P)
            tr = spare(2, 4, P)
            LK = spare(2, 4, P)
            TB = spare(2, 2, P)
            Xs = spare(2, P)
            FB, FK, FA, Pn = sg, Pi, ex, cs

            def wcol(i):
                return W[:, i * P:(i + 1) * P]

            def barrier(eng, own, j, i):
                for m, trips in own:
                    eng.wait_ge(m.sem, len(m.names) * trips)
                eng.sem_inc(phase, 1)
                eng.wait_ge(phase, 4 * (4 * j + i + 1))
                eng.sem_inc(passed, 1)

            def halves(x):
                return x.rearrange("p (a b) -> p a b", a=2)

            with nc.Block() as block:
                @block.sync
                def _(sp):
                    sp.dma_start(W, A["w_pair"][0]).then_inc(s_w, 16)
                    with sp.Fori(1, N) as j:
                        sp.wait_ge(lin.sem, j * len(lin.names))
                        sp.dma_start(W, A["w_pair"][ds(j, 1)].rearrange("a p n -> (a p) n")).then_inc(s_w, 16)

                @block.gpsimd
                def _(pool):
                    G = nc.gpsimd
                    G.memset(bd[:, :, :, :], 0.0).then_inc(z_init, 1)
                    pool.wait_ge(z_init, 1)
                    with pool.Fori(0, N) as j:
                        G.memset(Z[:, :, :], 0.0).then_inc(z_init, 1)
                        pool.wait_ge(z_init, j + 2)
                        pool.sem_inc(phase, 1)
                        pool.wait_ge(phase, 4 * (4 * j + 1))
                        pool.sem_inc(passed, 1)
                        for q, L in enumerate(loops):
                            with pool.Fori(0, L["n"]) as c:
                                it = j * L["n"] + c
                                pool.wait_ge(L["pe"].sem, it * len(L["pe"].names))
                                for d, at in ((0, c * CH), (1, (L["n"] - 1) * CH - c * CH)):
                                    off = CTX if L["lat"] else 0
                                    srcs = [(0, FA[:, d, ds(at + off, CH)]), (2, FB[:, d, ds(at + off, CH)]),
                                            (3, FK[:, d, ds(at + off, CH)]), (4, v[:, ds(at + off, CH)])]
                                    if L["lat"]:
                                        srcs.append((1, FR[:, d, ds(at, CH)]))
                                    for i, src in srcs:
                                        for hh in range(2):
                                            last = G.tensor_copy(bd[64 * hh:64 * hh + 64, d, i, 64 * hh:64 * hh + 64],
                                                                 src[64 * hh:64 * hh + 64])
                                last.then_inc(*L["pool"].did("bd"))
                            barrier(pool, [(L["pool"], (j + 1) * L["n"])], j, q + 1)
                        pool.sem_inc(phase, 1)
                        pool.wait_ge(phase, 4 * (4 * j + 4))
                        pool.sem_inc(passed, 1)

                @block.tensor
                def _(pe):
                    ident = self.con("id")
                    with pe.Fori(0, N) as j:
                        pe.wait_ge(s_w, (j + 1) * 16)
                        for name, i, src, bank in (("k", 1, xk, 0), ("v", 2, xv, 2), ("r", 0, xr, 4)):
                            spans = [(0, HALF), (HALF, TOK)] if name != "r" else [(0, SEQ)]
                            for b, (lo, hi) in enumerate(spans):
                                for kt in range(KT):
                                    last = pe.matmul(ps[:, bank + b, 0:hi - lo], wcol(i * KT + kt), src[:, kt, lo:hi],
                                                     start=(kt == 0), stop=(kt == KT - 1))
                            last.then_inc(*lin.did(name))
                        base = 3 * KT
                        pe.matmul(ps[:, 5, :], wcol(base + 4), TG[:, :], start=True, stop=True).then_inc(*lin.did("g"))
                        for name, i, src, bank, need in (("w0", 0, TW, 6, None), ("w1", 1, TW, 0, "k"),
                                                         ("a0", 2, TA, 2, "v"), ("a1", 3, TA, 6, "w0")):
                            if need:
                                pe.wait_ge(f_act.sem, f_act.at(need, j))
                            for b in range(2):
                                last = pe.matmul(ps[:, bank + b, 0:HALF], wcol(base + i), src[:, b * HALF:(b + 1) * HALF],
                                                 start=True, stop=True)
                            last.then_inc(*lin.did(name))
                        pe.wait_ge(f_dve.sem, f_dve.at("sq", j))
                        pe.wait_ge(f_act.sem, f_act.at("g", j))
                        for b in range(2):
                            last = pe.matmul(ps[:, 4 + b, 0:HALF], self.con("hsum"), t1[:, b * HALF:(b + 1) * HALF],
                                             start=True, stop=True)
                        last.then_inc(*nrm.did("norm"))
                        pe.wait_ge(f_dve.sem, f_dve.at("coefin", j))
                        pe.wait_ge(f_act.sem, f_act.at("a1", j))
                        pe.matmul(ps[:, 6, :], self.con("hsum"), t1[:, 0:SEQ], start=True, stop=True).then_inc(
                            *nrm.did("coef"))
                        barrier(pe, [(nrm, j + 1)], j, 0)
                        for q, L in enumerate(loops):
                            m, dve_m, act_m = L["pe"], L["dve"], L["act"]
                            with pe.Fori(0, L["n"]) as c:
                                it = j * L["n"] + c

                                def after(marks, name):
                                    pe.wait_ge(marks.sem, marks.at(name, it))

                                pe.wait_ge(L["pool"].sem, L["pool"].at("bd", it))
                                nr = 2 if L["lat"] else 1
                                for i, bank in ((2, 0), (3, 1)):
                                    for d in range(2):
                                        last = pe.matmul(
                                            ps[:, bank, 256 * d:256 * d + nr * P], bd[:, d, i, :],
                                            bd[:, d, 0:nr, :].rearrange("p a b -> p (a b)"), start=True, stop=True)
                                last.then_inc(*m.did("score"))
                                for d in range(2):
                                    for o, i in enumerate((0, 3, 4, 2)):
                                        last = pe.transpose(ps[:, 2 + d, o * P:(o + 1) * P], bd[:, d, i, :], ident)
                                last.then_inc(*m.did("trans"))
                                after(dve_m, "sS")
                                pe.wait_ge(act_m.sem, it * len(act_m.names))
                                for d in range(2):
                                    last = pe.matmul(ps[:, 4, d * P:(d + 1) * P], LK[:, d, 0, :], ident, start=True, stop=True)
                                last.then_inc(*m.did("L"))
                                for i in range(5):
                                    after(dve_m, f"t{i}")
                                    for d in range(2):
                                        last = pe.matmul(ps[:, 4, d * P:(d + 1) * P], LK[:, d, 0, :], TB[:, d, 0, :],
                                                         start=True, stop=True)
                                    last.then_inc(*m.did(f"X{i}"))
                                    after(dve_m, f"x{i}")
                                    for d in range(2):
                                        if i < 4:
                                            pe.matmul(ps[:, 5, 256 * d:256 * d + P], TB[:, d, 1, :], Xs[:, d, :],
                                                      start=True, stop=True)
                                        last = pe.matmul(ps[:, 5, 256 * d + P:256 * d + 2 * P], Xs[:, d, :], TB[:, d, 1, :],
                                                         start=True, stop=True)
                                    last.then_inc(*m.did(f"T{i}"))
                                after(act_m, "tr")
                                after(dve_m, "t5")
                                for d in range(2):
                                    pe.matmul(ps[:, 6, d * P:(d + 1) * P], LK[:, d, 2, :], tr[:, d, 2, :],
                                              start=True, stop=True)
                                    last = pe.matmul(ps[:, 6, (2 + d) * P:(3 + d) * P], tr[:, d, 0, :], TB[:, d, 1, :],
                                                     start=True, stop=True)
                                last.then_inc(*m.did("akv"))
                                after(act_m, "akv")
                                for d in range(2):
                                    pe.matmul(ps[:, 7, d * P:(d + 1) * P], TB[:, d, 1, :], AT[:, 0, d, :],
                                              start=True, stop=False)
                                    last = pe.matmul(ps[:, 7, d * P:(d + 1) * P], AT[:, 1, d, :], Z[:, d, :],
                                                     start=False, stop=True)
                                last.then_inc(*m.did("U"))
                                after(act_m, "U")
                                for d in range(2):
                                    o = ps[:, 7, (2 + d) * P:(3 + d) * P]
                                    pe.matmul(o, ident, Z[:, d, :], start=True, stop=False)
                                    pe.matmul(o, tr[:, d, 1, :], tr[:, d, 2, :], start=False, stop=False)
                                    last = pe.matmul(o, tr[:, d, 3, :], Us[:, d, :], start=False, stop=True)
                                last.then_inc(*m.did("Z"))
                                if L["lat"]:
                                    for d in range(2):
                                        o = ps[:, 4, d * P:(d + 1) * P]
                                        pe.matmul(o, Z[:, d, :], bd[:, d, 1, :], start=True, stop=False)
                                        pe.matmul(o, tr[:, d, 2, :], LK[:, d, 3, :], start=False, stop=False)
                                        last = pe.matmul(o, Us[:, d, :], LK[:, d, 1, :], start=False, stop=True)
                                    last.then_inc(*m.did("Y"))
                            barrier(pe, [(m, (j + 1) * L["n"])], j, q + 1)
                        for name, need, src in (("mean", "Y", bon), ("var", "sq", t1)):
                            pe.wait_ge(o_dve.sem, o_dve.at(need, j))
                            pe.matmul(ps[:, 0 if name == "mean" else 1, :], self.con("hmean"),
                                      Y[:, 0, :] if name == "mean" else t1[:, 0:SEQ], start=True, stop=True).then_inc(
                                *o_pe.did(name))
                        barrier(pe, [(o_pe, j + 1)], j, 3)

                @block.scalar
                def _(act):
                    with act.Fori(0, N) as j:
                        act.wait_ge(f_dve.sem, f_dve.at("pj", j))
                        for name, bank, dst, f, pc in (
                                ("k", 0, k[:, :], ACT.Copy, None), ("v", 2, v[:, :], ACT.Copy, None),
                                ("r", 4, r, ACT.Copy, None), ("g", 5, g, ACT.Copy, None),
                                ("w0", 6, sg[:, 0, :], ACT.Sigmoid, 0), ("w1", 0, sg[:, 1, :], ACT.Sigmoid, 1),
                                ("a0", 2, a[:, 0, :], ACT.Sigmoid, 2), ("a1", 6, a[:, 1, :], ACT.Sigmoid, 3)):
                            act.wait_ge(lin.sem, lin.at(name, j))
                            if name in "rg":
                                S.activation(dst[:, :], ps[:, bank, :], f).then_inc(*f_act.did(name))
                            elif pc is None:
                                S.activation(halves(dst), ps[:, bank:bank + 2, 0:HALF], f).then_inc(*f_act.did(name))
                            else:
                                S.activation(halves(dst), ps[:, bank:bank + 2, 0:HALF], f,
                                             bias=PJ[:, pc:pc + 1]).then_inc(*f_act.did(name))
                        act.wait_ge(nrm.sem, nrm.at("norm", j))
                        S.activation(halves(kk[:, :]), ps[:, 4:6, 0:HALF], ACT.Sqrt).then_inc(*f_act.did("root"))
                        act.wait_ge(f_dve.sem, f_dve.at("in1", j))
                        S.activation(ex[:, :, :], ex[:, :, :], ACT.Exp, scale=-DECAY).then_inc(*f_act.did("Px"))
                        S.activation(Pi[:, :, :], cs[:, :, :], ACT.Exp, scale=DECAY).then_inc(*f_act.did("Pi"))
                        act.wait_ge(f_act.sem, f_act.at("Pi", j))
                        S.activation(Pn[:, :, :], cs[:, :, :], ACT.Exp, scale=-DECAY).then_inc(*f_act.did("P"))
                        barrier(act, [(f_act, j + 1)], j, 0)
                        for q, L in enumerate(loops):
                            m, pe_m = L["act"], L["pe"]
                            with act.Fori(0, L["n"]) as c:
                                it = j * L["n"] + c
                                last_at = (L["n"] - 1) * CH - c * CH + (CTX if L["lat"] else 0)
                                first_at = c * CH + (CTX if L["lat"] else 0)

                                def after(name):
                                    act.wait_ge(pe_m.sem, pe_m.at(name, it))

                                after("trans")
                                S.activation(tr[:, :, 3, :], ps[:, 2:4, 3 * P:4 * P], ACT.Copy, scale=-1.0).then_inc(
                                    *m.did("trB"))
                                S.activation(tr[:, :, 0:3, :], ps[:, 2:4, 0:3 * P].rearrange("p d (o n) -> p d o n", o=3),
                                             ACT.Copy).then_inc(*m.did("tr"))
                                after("akv")
                                S.activation(AT[:, :, :, :].rearrange("p a d n -> p (a d n)"), ps[:, 6, :],
                                             ACT.Copy).then_inc(*m.did("akv"))
                                after("U")
                                S.activation(Us[:, :, :].rearrange("p d n -> p (d n)"), ps[:, 7, 0:256],
                                             ACT.Copy).then_inc(*m.did("U"))
                                if L["lat"]:
                                    after("Y")
                                    for d, at in ((0, c * CH), (1, (L["n"] - 1) * CH - c * CH)):
                                        for hh in range(2):
                                            last = S.activation(
                                                Y[64 * hh:64 * hh + 64, d, ds(at, CH)],
                                                ps[64 * hh:64 * hh + 64, 4, d * P + 64 * hh:d * P + 64 * hh + 64], ACT.Copy)
                                    last.then_inc(*m.did("y"))
                                else:
                                    after("Z")
                                for d, at in ((0, first_at + CH - 1), (1, last_at)):
                                    S.activation(Z[:, d, :], ps[:, 7, (2 + d) * P:(3 + d) * P], ACT.Copy,
                                                 scale=Pn[:, d, ds(at, 1)]).then_inc(*m.did(f"z{d}"))
                            barrier(act, [(m, (j + 1) * L["n"])], j, q + 1)
                        act.wait_ge(o_pe.sem, o_pe.at("var", j))
                        S.activation(t1[:, 0:SEQ], ps[:, 1, :], ACT.Sqrt, bias=self.tiny[:, 1:2]).then_inc(*o_act.did("root"))
                        barrier(act, [(o_act, j + 1)], j, 3)

                @block.vector
                def _(dve):
                    with dve.Fori(0, N) as j:
                        def own(name):
                            dve.wait_ge(f_dve.sem, f_dve.at(name, j))

                        def sc(name):
                            dve.wait_ge(f_act.sem, f_act.at(name, j))

                        b0 = COLS["pair"][0]
                        V.tensor_copy(PJ[:, 0:9], self.par[:, ds(j * 9 + b0, 9)]).then_inc(*f_dve.did("pj"))
                        own("pj")
                        V.tensor_scalar(PJ[:, 9:10], PJ[:, 5:6], -1.0, 1.0, ALU.mult, ALU.add).then_inc(*f_dve.did("omka"))
                        sc("k")
                        V.tensor_scalar(t1[:, :], k[:, :], PJ[:, 4:5], None, ALU.mult).then_inc(*f_dve.did("kkr"))
                        own("kkr")
                        V.tensor_tensor(t1[:, :], t1[:, :], t1[:, :], ALU.mult).then_inc(*f_dve.did("sq"))
                        sc("root")
                        V.tensor_scalar(kk[:, :], kk[:, :], 1e-12, None, ALU.max).then_inc(*f_dve.did("max"))
                        own("max")
                        V.reciprocal(kk[:, :], kk[:, :]).then_inc(*f_dve.did("rec"))
                        own("rec")
                        V.tensor_tensor(kk[:, :], kk[:, :], k[:, :], ALU.mult)
                        sc("w1")
                        for d in range(2):
                            last = V.tensor_tensor_scan(cs[:, d, :], self.con("scan", 0, TOK), sg[:, d, :], 0.0,
                                                        ALU.mult, ALU.add)
                        last.then_inc(*f_dve.did("kk"))
                        own("kk")
                        V.tensor_scalar(kk[:, :], kk[:, :], PJ[:, 4:5], None, ALU.mult).then_inc(*f_dve.did("scan"))
                        chunks = "p (c t) -> p c t"
                        c1 = cs[:, 1, :].rearrange(chunks, t=CH)
                        V.tensor_tensor(ex[:, 0, :], cs[:, 0, :], sg[:, 0, :], ALU.subtract)
                        V.tensor_tensor(ex[:, 1, :].rearrange(chunks, t=CH), c1[:, :, CH - 1:CH].broadcast_to([P, NCH, CH]), c1,
                                        ALU.subtract).then_inc(*f_dve.did("ex"))
                        own("ex")
                        V.tensor_tensor(cs[:, 1, :], ex[:, 1, :], sg[:, 1, :], ALU.add).then_inc(*f_dve.did("in1"))
                        own("in1")
                        sc("Px")
                        kk2 = kk[:, :].unsqueeze(1).broadcast_to([P, 2, TOK])
                        k2 = k[:, :].unsqueeze(1).broadcast_to([P, 2, TOK])
                        V.tensor_tensor(FA[:, :, :], ex[:, :, :], kk2, ALU.mult).then_inc(*f_dve.did("A"))
                        V.tensor_tensor(FB[:, :, :], a[:, :, :], kk2, ALU.mult).then_inc(*f_dve.did("kka"))
                        own("kka")
                        sc("Pi")
                        V.tensor_tensor(FB[:, :, :], FB[:, :, :], Pi[:, :, :], ALU.mult).then_inc(*f_dve.did("B"))
                        V.tensor_scalar(a[:, :, :], a[:, :, :], PJ[:, 5:6], PJ[:, 9:10], ALU.mult, ALU.add).then_inc(
                            *f_dve.did("kd"))
                        own("kd")
                        V.tensor_tensor(a[:, :, :], a[:, :, :], k2, ALU.mult).then_inc(*f_dve.did("kdk"))
                        own("kdk")
                        V.tensor_tensor(FK[:, :, :], a[:, :, :], Pi[:, :, :], ALU.mult).then_inc(*f_dve.did("K"))
                        sc("P")
                        V.tensor_tensor(FR[:, :, :], Pn[:, :, CTX:TOK], r[:, :].unsqueeze(1).broadcast_to([P, 2, SEQ]),
                                        ALU.mult).then_inc(*f_dve.did("R"))
                        V.tensor_tensor(bon[:, :], a[:, 0, CTX:TOK], a[:, 1, CTX:TOK], ALU.add).then_inc(*f_dve.did("kds"))
                        own("R")
                        V.tensor_scalar(r[:, :], r[:, :], PJ[:, 6:7], None, ALU.mult).then_inc(*f_dve.did("rr"))
                        own("rr")
                        V.tensor_tensor(t1[:, 0:SEQ], r[:, :], bon[:, :], ALU.mult).then_inc(*f_dve.did("coefin"))
                        dve.wait_ge(nrm.sem, nrm.at("coef", j))
                        V.tensor_tensor(bon[:, :], ps[:, 6, :], v[:, CTX:TOK], ALU.mult).then_inc(*f_dve.did("bonus"))
                        barrier(dve, [(f_dve, j + 1)], j, 0)
                        for q, L in enumerate(loops):
                            m, pe_m = L["dve"], L["pe"]
                            with dve.Fori(0, L["n"]) as c:
                                it = j * L["n"] + c

                                def after(name):
                                    dve.wait_ge(pe_m.sem, pe_m.at(name, it))

                                def mine(name):
                                    dve.wait_ge(m.sem, m.at(name, it))

                                def four(x):
                                    return x.rearrange("p (a b n) -> p a b n", a=2, b=2)

                                nr = 2 if L["lat"] else 1
                                after("score")
                                for name, bank, mask, o in (("sS", 0, "mS", 0), ("sK", 1, "mK", 2)):
                                    V.tensor_tensor(LK[:, :, o:o + nr, :], four(ps[:, bank, :])[:, :, 0:nr, :],
                                                    four(self.con(mask, 0, 4 * P))[:, :, 0:nr, :],
                                                    ALU.mult).then_inc(*m.did(name))
                                mL = self.con("mL", 0, 12 * P).rearrange("p (l d n) -> p l d n", l=6, d=2)
                                after("L")
                                V.tensor_tensor(TB[:, :, 0, :], ps[:, 4, 0:256].rearrange("p (d n) -> p d n", d=2),
                                                mL[:, 0, :, :], ALU.mult).then_inc(*m.did("t0a"))
                                mine("sS")
                                for d in range(2):
                                    last = V.tensor_tensor(TB[:, d, 1, :], LK[:, d, 0, :], mL[:, 0, 1 - d, :], ALU.mult)
                                last.then_inc(*m.did("t0b"))
                                mine("t0b")
                                V.tensor_tensor(TB[:, :, :, :], TB[:, :, :, :],
                                                self.con("id").unsqueeze(1).unsqueeze(1).broadcast_to([P, 2, 2, P]),
                                                ALU.add).then_inc(*m.did("t0"))
                                for i in range(5):
                                    after(f"X{i}")
                                    V.tensor_tensor(Xs[:, :, :], ps[:, 4, 0:256].rearrange("p (d n) -> p d n", d=2),
                                                    mL[:, i + 1, :, :], ALU.mult).then_inc(*m.did(f"x{i}"))
                                    after(f"T{i}")
                                    lo = 0 if i < 4 else 1
                                    V.tensor_tensor(TB[:, :, lo:2, :], TB[:, :, lo:2, :], four(ps[:, 5, :])[:, :, lo:2, :],
                                                    ALU.add).then_inc(*m.did(f"t{i + 1}"))
                            barrier(dve, [(m, (j + 1) * L["n"])], j, q + 1)

                        def out(name):
                            dve.wait_ge(o_dve.sem, o_dve.at(name, j))

                        y, t = Y[:, 0, :], t1[:, 0:SEQ]
                        V.tensor_tensor(y, Y[:, 0, :], Y[:, 1, :], ALU.add).then_inc(*o_dve.did("Y"))
                        dve.wait_ge(o_pe.sem, o_pe.at("mean", j))
                        V.tensor_tensor(Y[:, 1, :], y, ps[:, 0, :], ALU.subtract).then_inc(*o_dve.did("yc"))
                        out("yc")
                        V.tensor_tensor(t, Y[:, 1, :], Y[:, 1, :], ALU.mult).then_inc(*o_dve.did("sq"))
                        dve.wait_ge(o_act.sem, o_act.at("root", j))
                        V.reciprocal(t, t).then_inc(*o_dve.did("rec"))
                        out("rec")
                        V.tensor_tensor(t, t, Y[:, 1, :], ALU.mult).then_inc(*o_dve.did("yn"))
                        out("yn")
                        V.tensor_scalar(t, t, PJ[:, 7:8], PJ[:, 8:9], ALU.mult, ALU.add).then_inc(*o_dve.did("affine"))
                        out("affine")
                        V.tensor_tensor(t, t, bon[:, :], ALU.add).then_inc(*o_dve.did("bonus"))
                        out("bonus")
                        V.tensor_tensor(YG[:, ds(j, 1), :].rearrange("p a n -> p (a n)"), t, g[:, :], ALU.mult).then_inc(
                            *o_dve.did("gated"))
                        barrier(dve, [(o_dve, j + 1)], j, 3)

    def residual(self, name, src, n, m_tiles, k_tiles, moving, layer, gate, alpha, load_x=None, scale=None):
        nc, ring, ps, X, T = self.nc, self.ring, self.ps, self.X, self.T
        V = nc.vector
        width = m_tiles * k_tiles * P
        s_x, s_a, s_g, s_t = (self.sem(f"{name}_{q}") for q in ("x_in", "scaled", "gate", "sum"))
        with nc.Block() as block:
            @block.sync
            def _(sp):
                if load_x is not None:
                    sp.dma_start(X[:, :, :], load_x).then_inc(s_x, 16)
                load_chunks(sp, ring, src, n, width)

            @block.tensor
            def _(pe):
                project(pe, ring, ps, n, m_tiles, k_tiles, moving)

            @block.scalar
            def _(act):
                if load_x is not None:
                    act.wait_ge(s_x, 16)
                nc.scalar.activation(T[:, :, :], X[:, :, :], ACT.Copy, scale=alpha).then_inc(s_a, 1)

            @block.vector
            def _(dve):
                dve.wait_ge(s_a, 1)

                def body(s, trip, c):
                    dve.wait_ge(ring.used[s], ring.fills[s] + trip + 1)
                    for m in range(m_tiles):
                        t = T[:, ds(c * m_tiles + m, 1), :].rearrange("p a n -> p (a n)")
                        g = self.mod[:, layer, ds(c * m_tiles + (gate + m), 1), 0:1].rearrange("p a b -> p (a b)")
                        last = V.scalar_tensor_tensor(out=t, in0=ps[:, 2 * s + m, :], scalar=g, in1=t,
                                                      op0=ALU.mult, op1=ALU.add)
                    last.then_inc(ring.drained[s], 1)

                over_chunks(dve, n, body)
        ring.end(n)

    def norm(self, name, src, gamma, beta, layer, scale, shift, center=True):
        nc, ps, X, H, mod = self.nc, self.ps, self.X, self.H, self.mod
        V, S = nc.vector, nc.scalar
        tiles = range(KT)
        pe_m = self.marks(name + "_pe", ["mean"] * center + ["var"])
        act_m = self.marks(name + "_act", [f"q{k}" for k in tiles] + ["root"] + [f"x{k}" for k in tiles] * center)
        dve_m = self.marks(name + "_dve", [f"c{k}" for k in tiles] * center + ["gs"] * (not center) + ["rec"]
                           + [f"n{k}" for k in tiles] + [f"h{k}" for k in tiles])
        with ExitStack() as st:
            SQ, R = self.sb(st, name + "sq", KT, SEQ), self.sb(st, name + "r", SEQ)
            gs = self.sb(st, name + "gs", KT)
            with nc.Block() as block:
                @block.tensor
                def _(pe):
                    if center:
                        for k in tiles:
                            last = pe.matmul(ps[:, 6, :], self.con("mean"), src[:, k, :], start=(k == 0), stop=(k == KT - 1))
                        last.then_inc(*pe_m.did("mean"))
                    for k in tiles:
                        pe.wait_ge(act_m.sem, act_m.at(f"q{k}"))
                        last = pe.matmul(ps[:, 7, :], self.con("mean"), SQ[:, k, :], start=(k == 0), stop=(k == KT - 1))
                    last.then_inc(*pe_m.did("var"))

                @block.scalar
                def _(act):
                    for k in tiles:
                        if center:
                            act.wait_ge(dve_m.sem, dve_m.at(f"c{k}"))
                        S.activation(SQ[:, k, :], src[:, k, :], ACT.Square).then_inc(*act_m.did(f"q{k}"))
                    act.wait_ge(pe_m.sem, pe_m.at("var"))
                    S.activation(R[:, :], ps[:, 7, :], ACT.Sqrt, bias=self.tiny[:, 0:1] if center else self.tiny[:, 2:3]).then_inc(
                        *act_m.did("root"))
                    if center:
                        for k in tiles:
                            act.wait_ge(dve_m.sem, dve_m.at(f"n{k}"))
                            S.activation(X[:, k, :], src[:, k, :], ACT.Identity, bias=beta[:, k:k + 1],
                                         scale=gamma[:, k:k + 1]).then_inc(*act_m.did(f"x{k}"))

                @block.vector
                def _(dve):
                    if center:
                        dve.wait_ge(pe_m.sem, pe_m.at("mean"))
                        for k in tiles:
                            V.tensor_tensor(src[:, k, :], src[:, k, :], ps[:, 6, :], ALU.subtract).then_inc(
                                *dve_m.did(f"c{k}"))
                    else:
                        V.tensor_tensor(gs[:, :], gamma, mod[:, layer, scale:scale + KT, 0], ALU.mult).then_inc(
                            *dve_m.did("gs"))
                    dve.wait_ge(act_m.sem, act_m.at("root"))
                    V.reciprocal(R[:, :], R[:, :]).then_inc(*dve_m.did("rec"))
                    dve.wait_ge(dve_m.sem, dve_m.at("rec"))
                    for k in tiles:
                        dst = src if center else H
                        V.tensor_tensor(dst[:, k, :], src[:, k, :], R[:, :], ALU.mult).then_inc(*dve_m.did(f"n{k}"))
                    for k in tiles:
                        if center:
                            dve.wait_ge(act_m.sem, act_m.at(f"x{k}"))
                        else:
                            dve.wait_ge(dve_m.sem, dve_m.at(f"n{k}"))
                        V.tensor_scalar(H[:, k, :], X[:, k, :] if center else H[:, k, :],
                                        mod[:, layer, scale + k, 0:1] if center else gs[:, k:k + 1],
                                        mod[:, layer, shift + k, 0:1], ALU.mult, ALU.add).then_inc(*dve_m.did(f"h{k}"))

    def rwkv_out(self):
        self.residual("wo", self.A["w_o"], 4, 2, KT, lambda k: self.B0[:, k, :], 0, 16, ALPHA, load_x=self.A["xT"])
        self.norm("ln00", self.T, self.col("lng", 0, 8), self.col("lnb", 0, 8), 0, 32, 24)

    def ffn(self):
        nc, ring, ps, H = self.nc, self.ring, self.ps, self.H
        silu_m = [self.sem(f"ffn_silu{s}") for s in range(SLOTS)]
        with ExitStack() as st:
            HID, G = self.sb(st, "hid", FT, SEQ), self.sb(st, "silu", SLOTS, SEQ)
            with nc.Block() as block:
                @block.sync
                def _(sp):
                    load_chunks(sp, ring, self.A["w_ffn13"], FT, 2 * KT * P)

                @block.tensor
                def _(pe):
                    project(pe, ring, ps, FT, 2, KT, lambda k: H[:, k, :])

                @block.scalar
                def _(act):
                    def body(s, trip, c):
                        act.wait_ge(ring.used[s], ring.fills[s] + trip + 1)
                        act.wait_ge(ring.drained[s], ring.drains[s] + trip)
                        nc.scalar.activation(G[:, s, :], ps[:, 2 * s, :], ACT.Silu).then_inc(silu_m[s], 1)

                    over_chunks(act, FT, body)

                @block.vector
                def _(dve):
                    def body(s, trip, c):
                        dve.wait_ge(silu_m[s], trip + 1)
                        nc.vector.tensor_tensor(HID[:, ds(c, 1), :].rearrange("p a n -> p (a n)"), G[:, s, :],
                                                ps[:, 2 * s + 1, :], ALU.mult).then_inc(ring.drained[s], 1)

                    over_chunks(dve, FT, body)
            ring.end(FT)
            self.residual("ffn2", self.A["w_ffn2"], KT, 1, FT, lambda k: HID[:, k, :], 0, 40, ALPHA)
        self.norm("ln01", self.T, self.col("lng", 8, 8), self.col("lnb", 8, 8), 1, 8, 0)

    def pool(self):
        nc, ring, ps, X, T, H = self.nc, self.ring, self.ps, self.X, self.T, self.H
        V = nc.vector
        R, WIDE = SEQ // GRID_W, GRID_W + 2 * PADW
        s_w, s_pe, s_a, s_g = (self.sem(f"pool_{q}") for q in ("w", "done", "scaled", "gate"))
        dve_m = self.marks("pool_dve", ["zero", "pad", "s2", "s4", "s8", "s16", "mean0", "mean1", "mean2", "mean3", "pooled", "gps"])
        Q = self.B0
        with ExitStack() as st:
            pads = [self.sb(st, f"pad{i}", KT, R, WIDE) for i in range(2)]
            gps = self.sb(st, "gps", KT)
            with nc.Block() as block:
                @block.sync
                def _(sp):
                    sp.dma_start(ring.buf[0][:, 0:2048], self.A["w_pool"]).then_inc(s_w, 16)

                @block.scalar
                def _(act):
                    nc.scalar.activation(T[:, :, :], X[:, :, :], ACT.Copy, scale=ALPHA).then_inc(s_a, 1)

                @block.tensor
                def _(pe):
                    pe.wait_ge(s_w, 16)
                    pe.wait_ge(dve_m.sem, dve_m.at("pooled"))
                    for g in range(4):
                        for m in range(2):
                            for k in range(2):
                                at = (g * 4 + k * 2 + m) * P
                                last = pe.matmul(ps[:, 2 * g + m, :], ring.buf[0][:, at:at + P], Q[:, 2 * g + k, :],
                                                 start=(k == 0), stop=(k == 1))
                            last.then_inc(s_pe, 1)

                @block.vector
                def _(dve):
                    def mine(name):
                        dve.wait_ge(dve_m.sem, dve_m.at(name))

                    def grid(x):
                        return x.rearrange("p k (r c) -> p k r c", c=GRID_W)

                    V.memset(pads[0][:, :, :, :], 0.0).then_inc(*dve_m.did("zero"))
                    mine("zero")
                    for k in range(KT):
                        last = V.tensor_copy(pads[0][:, k, :, PADW:PADW + GRID_W],
                                             H[:, k, :].rearrange("p (r c) -> p r c", c=GRID_W))
                    last.then_inc(*dve_m.did("pad"))
                    prev = "pad"
                    for i, (lo, back, ahead) in enumerate(((1, 1, 0), (2, 1, 1), (4, 2, 2), (8, 4, 4))):
                        a, b = pads[i % 2], pads[(i + 1) % 2]
                        hi = WIDE - ahead - (0, 1, 2, 4)[i]
                        mine(prev)
                        for k in range(2 * i, KT):
                            last = V.tensor_tensor(b[:, k, :, lo:hi], a[:, k, :, lo - back:hi - back],
                                                   a[:, k, :, lo + ahead:hi + ahead], ALU.add)
                        prev = f"s{2 ** (i + 1)}"
                        last.then_inc(*dve_m.did(prev))
                        if i == 3:
                            break
                    mine("s16")
                    for g in range(4):
                        src = pads[(g + 1) % 2]
                        for k in (2 * g, 2 * g + 1):
                            o = Q[:, k, :].rearrange("p (r c) -> p r c", c=GRID_W)
                            last = V.tensor_tensor(o, src[:, k, :, PADW:PADW + GRID_W],
                                                   self.con("rcnt", g * GRID_W, GRID_W).unsqueeze(1).broadcast_to(
                                                       [P, R, GRID_W]), ALU.mult)
                        last.then_inc(*dve_m.did(f"mean{g}"))
                    mine("mean3")
                    V.tensor_tensor(Q[:, :, :], Q[:, :, :], H[:, :, :], ALU.subtract).then_inc(*dve_m.did("pooled"))
                    V.tensor_tensor(gps[:, :], self.col("pscale", 0, 8), self.mod[:, 1, 16:24, 0], ALU.mult).then_inc(
                        *dve_m.did("gps"))
                    mine("gps")
                    dve.wait_ge(s_a, 1)
                    for m in range(KT):
                        dve.wait_ge(s_pe, m + 1)
                        V.scalar_tensor_tensor(out=T[:, m, :], in0=ps[:, m, :], scalar=gps[:, m:m + 1], in1=T[:, m, :],
                                               op0=ALU.mult, op1=ALU.add)
        self.norm("ln10", T, self.col("lng", 16, 8), self.col("lnb", 16, 8), 1, 32, 24)

    def moe(self):
        nc, ring, ps, X, T, H = self.nc, self.ring, self.ps, self.X, self.T, self.H
        V, S = nc.vector, nc.scalar
        TT = SEQ // P
        with ExitStack() as st:
            GB = self.sb(st, "gate_rows", NE, SEQ)
            self.router(GB)
            HID, G, GY = self.sb(st, "ehid", ET, SEQ), self.sb(st, "esilu", SLOTS, SEQ), self.sb(st, "egy", 2, SEQ)
            Y = self.B0
            silu_m = [self.sem(f"moe_silu{s}") for s in range(SLOTS)]
            s_gy, s_acc = self.sem("moe_gated"), self.sem("moe_added")
            CHN = ET + 4
            with nc.Block() as block:
                @block.sync
                def _(sp):
                    with sp.Fori(0, NE) as e:
                        for c in range(CHN):
                            s = c % SLOTS
                            sp.wait_ge(ring.used[s], ring.fills[s] + e * (CHN // SLOTS) + c // SLOTS)
                            if c < ET:
                                src, w = self.A["w_moe13"][ds(e * ET + c, 1)], 2 * KT * P
                            else:
                                src, w = self.A["w_moe2"][ds(e * 4 + (c - ET), 1)], 2 * ET * P
                            sp.dma_start(ring.buf[s][:, 0:w], src.rearrange("a p n -> (a p) n")).then_inc(ring.loaded[s], 16)

                @block.tensor
                def _(pe):
                    with pe.Fori(0, NE) as e:
                        for c in range(CHN):
                            s = c % SLOTS
                            k0 = e * (CHN // SLOTS) + c // SLOTS
                            pe.wait_ge(ring.loaded[s], (ring.fills[s] + k0 + 1) * 16)
                            pe.wait_ge(ring.drained[s], ring.drains[s] + k0)
                            if c == ET:
                                for c2 in (ET - 1, ET - 2, ET - 3):
                                    s2 = c2 % SLOTS
                                    pe.wait_ge(ring.drained[s2], ring.drains[s2] + e * (CHN // SLOTS) + c2 // SLOTS + 1)
                            src, kts = (H, KT) if c < ET else (HID, ET)
                            for m in range(2):
                                for k in range(kts):
                                    at = (k * 2 + m) * P
                                    last = pe.matmul(ps[:, 2 * s + m, :], ring.buf[s][:, at:at + P], src[:, k, :],
                                                     start=(k == 0), stop=(k == kts - 1))
                            last.then_inc(ring.used[s], 1)

                @block.scalar
                def _(act):
                    with act.Fori(0, NE) as e:
                        for c in range(ET):
                            s = c % SLOTS
                            act.wait_ge(ring.used[s], ring.fills[s] + e * (CHN // SLOTS) + c // SLOTS + 1)
                            act.wait_ge(ring.drained[s], ring.drains[s] + e * (CHN // SLOTS) + c // SLOTS)
                            S.activation(G[:, s, :], ps[:, 2 * s, :], ACT.Silu).then_inc(silu_m[s], 1)

                @block.vector
                def _(dve):
                    per = [len(range(s, ET, SLOTS)) for s in range(SLOTS)]
                    with dve.Fori(0, NE) as e:
                        for c in range(CHN):
                            s = c % SLOTS
                            if c < ET:
                                dve.wait_ge(silu_m[s], e * per[s] + c // SLOTS + 1)
                                V.tensor_tensor(HID[:, c, :], G[:, s, :], ps[:, 2 * s + 1, :], ALU.mult).then_inc(
                                    ring.drained[s], 1)
                            else:
                                dve.wait_ge(ring.used[s], ring.fills[s] + e * (CHN // SLOTS) + c // SLOTS + 1)
                                for m in range(2):
                                    n = 2 * (c - ET) + m
                                    if n >= 2:
                                        dve.wait_ge(s_acc, e * KT + n - 1)
                                    else:
                                        dve.wait_ge(s_acc, e * KT)
                                    V.tensor_tensor(GY[:, n % 2, :], ps[:, 2 * s + m, :],
                                                    GB[:, ds(e, 1), :].rearrange("p a n -> p (a n)"), ALU.mult).then_inc(s_gy, 1)
                                dve.wait_ge(s_gy, e * KT + n + 1)
                                dve.sem_inc(ring.drained[s], 1)

                @block.gpsimd
                def _(pool):
                    s_z = self.sem("moe_zero")
                    nc.gpsimd.memset(Y[:, :, :], 0.0).then_inc(s_z, 1)
                    pool.wait_ge(s_z, 1)
                    with pool.Fori(0, NE) as e:
                        for n in range(KT):
                            pool.wait_ge(s_gy, e * KT + n + 1)
                            nc.gpsimd.tensor_tensor(Y[:, n, :], Y[:, n, :], GY[:, n % 2, :], ALU.add).then_inc(s_acc, 1)
            ring.end(NE * CHN)
            s_t, s_g = self.sem("moe_T"), self.sem("moe_G")
            with nc.Block() as block:
                @block.scalar
                def _(act):
                    S.activation(T[:, :, :], X[:, :, :], ACT.Copy, scale=ALPHA).then_inc(s_t, 1)

                @block.vector
                def _(dve):
                    dve.wait_ge(s_t, 1)
                    for k in range(KT):
                        V.scalar_tensor_tensor(out=T[:, k, :], in0=Y[:, k, :], scalar=self.mod[:, 1, 40 + k, 0:1],
                                               in1=T[:, k, :], op0=ALU.mult, op1=ALU.add)
        self.norm("ln11", T, self.col("lng", 24, 8), self.col("lnb", 24, 8), 1, 8, 0)

    def router(self, GB):
        nc, ring, ps, H = self.nc, self.ring, self.ps, self.H
        V, S = nc.vector, nc.scalar
        TT = SEQ // P
        s_w, s_l = self.sem("router_in"), self.sem("logits")
        dve_m = self.marks("router_dve", ["lg", "gt", "eq", "eqlow", "beats", "rank", "sel", "max", "shift", "num", "den",
                                          "rec", "gate"])
        act_m = self.marks("router_act", ["exp"])
        s_b, s_e = self.sem("gate_rows_pe"), self.sem("gate_rows_out")
        with ExitStack() as st:
            L = self.sb(st, "logit", TT, NE)
            cmp, eq = self.sb(st, "cmp", TT, NE, NE), self.sb(st, "eqs", TT, NE, NE)
            rank, E, Z, mx = (self.sb(st, n, TT, NE) for n in ("rank", "rexp", "rz", "rmx"))
            rw, rb, low = self.sb(st, "rw", KT * NE), self.sb(st, "rb", NE), self.sb(st, "low", NE * NE)
            gwide = self.sb(st, "gwide", 2, TT, P)
            with nc.Block() as block:
                @block.sync
                def _(sp):
                    sp.dma_start(rw[:, :], self.A["w_router"]).then_inc(s_w, 16)
                    sp.dma_start(rb[:, :], self.A["router_b"].broadcast_to([P, NE])).then_inc(s_w, 16)
                    sp.dma_start(low[:, :], self.A["tie_mask"].broadcast_to([P, NE * NE])).then_inc(s_w, 16)

                @block.tensor
                def _(pe):
                    pe.wait_ge(s_w, 48)
                    for t in range(TT):
                        for k in range(KT):
                            last = pe.matmul(ps[:, 6, t * NE:(t + 1) * NE], H[:, k, t * P:(t + 1) * P],
                                             rw[:, k * NE:(k + 1) * NE], start=(k == 0), stop=(k == KT - 1))
                    last.then_inc(s_l, 1)
                    for e in range(NE):
                        pe.wait_ge(dve_m.sem, dve_m.at("gate") + e + 1)
                        if e >= 2:
                            pe.wait_ge(s_e, e - 1)
                        for t in range(TT):
                            last = pe.matmul(ps[:, e % 2, t * P:(t + 1) * P], gwide[:, e % 2, t, :], self.con("id"),
                                             start=True, stop=True)
                        last.then_inc(s_b, 1)

                @block.scalar
                def _(act):
                    act.wait_ge(dve_m.sem, dve_m.at("shift"))
                    S.activation(E[:, :, :], Z[:, :, :], ACT.Exp).then_inc(*act_m.did("exp"))
                    for e in range(NE):
                        act.wait_ge(s_b, e + 1)
                        S.activation(GB[:, e, :], ps[:, e % 2, :], ACT.Copy).then_inc(s_e, 1)

                @block.vector
                def _(dve):
                    def mine(name):
                        dve.wait_ge(dve_m.sem, dve_m.at(name))

                    full = [P, TT, NE, NE]
                    dve.wait_ge(s_l, 1)
                    V.tensor_tensor(L[:, :, :], ps[:, 6, 0:TT * NE].rearrange("p (t e) -> p t e", e=NE),
                                    rb[:, :].unsqueeze(1).broadcast_to([P, TT, NE]), ALU.add).then_inc(*dve_m.did("lg"))
                    mine("lg")
                    other = L[:, :, :].unsqueeze(2).broadcast_to(full)
                    own = L[:, :, :].unsqueeze(3).broadcast_to(full)
                    V.tensor_tensor(cmp[:, :, :, :], other, own, ALU.is_gt).then_inc(*dve_m.did("gt"))
                    V.tensor_tensor(eq[:, :, :, :], other, own, ALU.is_equal).then_inc(*dve_m.did("eq"))
                    mine("eq")
                    tie = low[:, :].rearrange("p (a b) -> p a b", b=NE).unsqueeze(1).broadcast_to(full)
                    V.tensor_tensor(eq[:, :, :, :], eq[:, :, :, :], tie, ALU.mult).then_inc(*dve_m.did("eqlow"))
                    mine("eqlow")
                    V.tensor_tensor(cmp[:, :, :, :], cmp[:, :, :, :], eq[:, :, :, :], ALU.add).then_inc(*dve_m.did("beats"))
                    mine("beats")
                    V.tensor_reduce(rank[:, :, :], cmp[:, :, :, :], AX, ALU.add).then_inc(*dve_m.did("rank"))
                    mine("rank")
                    V.tensor_scalar(rank[:, :, :], rank[:, :, :], 1.5, None, ALU.is_lt).then_inc(*dve_m.did("sel"))
                    V.tensor_reduce(mx[:, :, 0:1], L[:, :, :], AX, ALU.max).then_inc(*dve_m.did("max"))
                    mine("max")
                    V.tensor_tensor(Z[:, :, :], L[:, :, :], mx[:, :, 0:1].broadcast_to([P, TT, NE]),
                                    ALU.subtract).then_inc(*dve_m.did("shift"))
                    dve.wait_ge(act_m.sem, act_m.at("exp"))
                    V.tensor_tensor(E[:, :, :], E[:, :, :], rank[:, :, :], ALU.mult).then_inc(*dve_m.did("num"))
                    mine("num")
                    V.tensor_reduce(mx[:, :, 1:2], E[:, :, :], AX, ALU.add).then_inc(*dve_m.did("den"))
                    mine("den")
                    V.reciprocal(mx[:, :, 1:2], mx[:, :, 1:2]).then_inc(*dve_m.did("rec"))
                    mine("rec")
                    V.tensor_tensor(E[:, :, :], E[:, :, :], mx[:, :, 1:2].broadcast_to([P, TT, NE]), ALU.mult).then_inc(
                        *dve_m.did("gate"))
                    mine("gate")
                    for e in range(NE):
                        if e >= 2:
                            dve.wait_ge(s_b, e - 1)
                        V.tensor_copy(gwide[:, e % 2, :, :], E[:, :, e:e + 1].broadcast_to([P, TT, P])).then_inc(dve_m.sem, 1)

    def attention(self):
        nc, A, ring, ps, X, T, H, mod = self.nc, self.A, self.ring, self.ps, self.X, self.T, self.H, self.mod
        V, S = nc.vector, nc.scalar
        self.norm("rms1", X, self.col("n1g", 0, 8), None, 2, 8, 0, center=False)
        TT = SEQ // P
        with ExitStack() as st:
            QK = self.sb(st, "qk", 16, SEQ)
            VV = self.sb(st, "vv", 2, TT, BANK)
            lam = self.sb(st, "lamv", 8)
            self.qkv(QK, VV, lam)
            O = self.B0
            self.heads(QK, VV, lam, O)
        self.residual("wout", A["w_out"], 4, 2, KT, lambda k: self.B0[:, k, :], 2, 16, 1.0)
        self.move_t_to_x("h1")

    def move_t_to_x(self, name):
        s = self.sem(name + "_moved")
        with self.nc.Block() as block:
            @block.scalar
            def _(act):
                self.nc.scalar.activation(self.X[:, :, :], self.T[:, :, :], ACT.Copy).then_inc(s, 1)

    def qkv(self, QK, VV, lam):
        nc, A, ring, ps, H = self.nc, self.A, self.ring, self.ps, self.H
        V, S = nc.vector, nc.scalar
        TT = SEQ // P
        NV = 4
        s_v, s_vo, s_sq, s_var, s_root, s_rec = (self.sem(f"qkv_{q}") for q in ("v", "vout", "sq", "var", "root", "rec"))
        s_n, s_nn = self.sem("qk_copied"), self.sem("qk_normed")
        lam_d, lam_p, lam_a = self.marks("lam_dve", ["prod", "sub", "lam"]), self.sem("lam_pe"), self.sem("lam_act")
        s_b = [self.sem(f"bias_{q}") for q in ("in", "pe", "act", "out")]
        with ExitStack() as st:
            SQ, R = self.sb(st, "qk_sq", 2, SEQ), self.sb(st, "qk_r", 2, SEQ)
            tab, oh, row = self.sb(st, "tab", 12), self.sb(st, "onehot", 1024), self.sb(st, "biasrow", 1024)
            with nc.Block() as block:
                @block.sync
                def _(sp):
                    sp.dma_start(tab[0:33, :], A["bias_table"]).then_inc(s_b[0], 16)
                    sp.dma_start(oh[0:33, :], A["bucket_onehot"]).then_inc(s_b[0], 16)
                    load_chunks(sp, ring, A["w_qk"], 8, 2 * KT * P)
                    sp.wait_ge(s_b[2], 2)
                    sp.dma_start(A["bias_rows"], row[0:12, :]).then_inc(s_b[3], 16)
                    sp.wait_ge(s_b[3], 16)

                @block.tensor
                def _(pe):
                    pe.wait_ge(s_b[0], 32)
                    for b in range(2):
                        last = pe.matmul(ps[0:12, 6 + b, :], tab[0:33, :], oh[0:33, b * BANK:(b + 1) * BANK],
                                         start=True, stop=True)
                    last.then_inc(s_b[1], 1)
                    pe.wait_ge(lam_d.sem, lam_d.at("prod"))
                    pe.wait_ge(s_b[2], 2)
                    pe.matmul(ps[:, 6, 0:2], self.con("ones"), lam[:, 0:2], start=True, stop=True).then_inc(lam_p, 1)
                    project(pe, ring, ps, 8, 2, KT, lambda k: H[:, k, :])

                @block.scalar
                def _(act):
                    act.wait_ge(s_b[1], 1)
                    for b in range(2):
                        S.activation(row[0:12, b * BANK:(b + 1) * BANK], ps[0:12, 6 + b, :], ACT.Copy).then_inc(s_b[2], 1)
                    act.wait_ge(lam_p, 1)
                    S.activation(lam[:, 2:4], ps[:, 6, 0:2], ACT.Exp).then_inc(lam_a, 1)

                    def body(s, trip, c):
                        act.wait_ge(ring.used[s], ring.fills[s] + trip + 1)
                        S.activation(QK[:, ds(2 * c, 2), :], ps[:, 2 * s:2 * s + 2, :], ACT.Copy).then_inc(ring.drained[s], 1)

                    over_chunks(act, 8, body)

                @block.vector
                def _(dve):
                    V.tensor_tensor(lam[:, 0:2], self.col("lam", 0, 4).rearrange("p (a b) -> p a b", b=2)[:, :, 0],
                                    self.col("lam", 0, 4).rearrange("p (a b) -> p a b", b=2)[:, :, 1],
                                    ALU.mult).then_inc(*lam_d.did("prod"))
                    dve.wait_ge(lam_a, 1)
                    V.tensor_tensor(lam[:, 4:5], lam[:, 2:3], lam[:, 3:4], ALU.subtract).then_inc(*lam_d.did("sub"))
                    dve.wait_ge(lam_d.sem, lam_d.at("sub"))
                    V.tensor_scalar(lam[:, 5:6], lam[:, 4:5], LAMBDA_INIT, None, ALU.add).then_inc(*lam_d.did("lam"))
            ring.end(8)
            with nc.Block() as block:
                @block.sync
                def _(sp):
                    load_chunks(sp, ring, A["w_v"], NV, 4 * BANK)

                @block.tensor
                def _(pe):
                    for c in range(NV):
                        s, kind, half = c % SLOTS, c // 2, c % 2
                        pe.wait_ge(ring.loaded[s], (ring.fills[s] + c // SLOTS + 1) * 16)
                        if c == 2:
                            pe.wait_ge(s_vo, 1)
                        for t in range(TT):
                            for k in range(4):
                                last = pe.matmul(ps[:, t, :], H[:, 4 * half + k, t * P:(t + 1) * P],
                                                 ring.buf[s][:, k * BANK:(k + 1) * BANK],
                                                 start=(half == 0 and k == 0), stop=(half == 1 and k == 3))
                        last.then_inc(ring.used[s], 1)
                    with pe.Fori(0, 16) as i:
                        pe.wait_ge(s_sq, i + 1)
                        pe.wait_ge(s_root, i)
                        pe.matmul(ps[:, 7, :], self.con("hmean"), SQ[:, 0, :], start=True, stop=True).then_inc(s_var, 1)

                @block.scalar
                def _(act):
                    for kind in range(2):
                        s = (2 * kind + 1) % SLOTS
                        act.wait_ge(ring.used[s], ring.fills[s] + (2 * kind + 1) // SLOTS + 1)
                        S.activation(VV[:, kind, :, :], ps[:, 0:TT, :], ACT.Copy).then_inc(s_vo, 1)
                    with act.Fori(0, 16) as i:
                        act.wait_ge(s_var, i)
                        S.activation(SQ[:, 0, :], QK[:, ds(i, 1), :].rearrange("p a n -> p (a n)"), ACT.Square).then_inc(
                            s_sq, 1)
                        act.wait_ge(s_var, i + 1)
                        act.wait_ge(s_nn, i)
                        S.activation(R[:, 0, :], ps[:, 7, :], ACT.Sqrt, bias=self.tiny[:, 2:3]).then_inc(s_root, 1)

                @block.vector
                def _(dve):
                    with dve.Fori(0, 16) as i:
                        dve.wait_ge(s_root, i + 1)
                        V.reciprocal(R[:, 0, :], R[:, 0, :]).then_inc(s_rec, 1)
                        dve.wait_ge(s_rec, i + 1)
                        x = QK[:, ds(i, 1), :].rearrange("p a n -> p (a n)")
                        V.tensor_tensor(x, x, R[:, 0, :], ALU.mult).then_inc(s_nn, 1)
                    dve.wait_ge(s_nn, 16)
                    for i, name in enumerate(("qna", "kna", "qnb", "knb")):
                        V.tensor_scalar(QK[:, 4 * i:4 * i + 4, :], QK[:, 4 * i:4 * i + 4, :], self.col(name), None, ALU.mult)
            ring.end(NV, 0)

    def heads(self, QK, VV, lam, O):
        nc, A, ps = self.nc, self.A, self.ps
        V, S = nc.vector, nc.scalar
        TT = SEQ // P
        GW = SEQ + (TT - 1) * P
        units = [(0, h, q) for h in range(2) for q in range(TT)] + [(1, h, q) for q in range(TT) for h in range(2)]
        turns = [i for i, u in enumerate(units) if u[0] == 0 or u[1] == 1]
        U, NTURN = len(units), len(turns)
        U_ = range(U)
        pe_m = self.marks("at_pe", [x for i in range(U + 1) for x in
                                    ([f"s{i}"] if i < U else []) + ([f"t{i - 1}"] if i - 1 in turns else [])
                                    + ([f"pv{0 if i - 1 == 7 else 1}"] if i - 1 in (7, 15) else [])] + ["sub"])
        act_m = self.marks("at_act", [x for i in range(U + 1) for x in
                                      ([f"e{i}"] if i < U else []) + ([f"p{i - 1}"] if i - 1 in turns else [])]
                           + ["oa", "ob", "sq", "root"])
        dve_m = self.marks("at_dve", [x for i in range(U + 1) for x in
                                      ([f"b{i}", f"m{i}"] if i < U else [])
                                      + ([f"r{i - 1}"] + ([f"l{i - 1}"] if units[i - 1][:2] == (1, 1) else [])
                                         + [f"n{i - 1}"] if i >= 1 else [])] + ["rec", "obn", "obg"])
        pool_m = self.marks("at_pool", ["copied"])
        s_half = self.sem("queries_copied")
        s_g, s_z = self.sem("bias_loaded"), self.sem("heads_zero")
        with ExitStack() as st:
            Qz, Ks, Vz = self.sb(st, "qz", 4, SEQ), self.sb(st, "ks", 2, SEQ), self.sb(st, "vz", 3, TT, P)
            GT = self.sb(st, "gt", 3, GW)
            PR = self.sb(st, "pr", 4, SEQ)
            PT, SC = self.H[:, 0:TT, :], self.H[:, TT:TT + 2, :]
            stat = self.sb(st, "stat", U, 4)
            ON, R = self.sb(st, "on", 2, SEQ), self.sb(st, "on_r", SEQ)
            with nc.Block() as block:
                @block.sync
                def _(sp):
                    with sp.Fori(0, 4) as t:
                        sp.wait_ge(dve_m.sem, t * len(dve_m.names))
                        for i in range(3):
                            hd = 2 * t + i if i < 2 else t + 8
                            sp.dma_start(GT[:, i, :], self.toeplitz(hd, GW)).then_inc(s_g, 16)

                @block.gpsimd
                def _(pool):
                    G = nc.gpsimd
                    G.memset(Qz[:, :, :], 0.0).then_inc(s_z, 1)
                    G.memset(Vz[:, :, :, :], 0.0).then_inc(s_z, 1)
                    pool.wait_ge(s_z, 2)
                    with pool.Fori(0, 4) as t:
                        pool.wait_ge(pe_m.sem, t * len(pe_m.names))
                        for kind in range(2):
                            for h in range(2):
                                r = slice(64 * h, 64 * h + 64)
                                G.tensor_copy(Qz[r, 2 * kind + h, ::-1], QK[r, ds(8 * kind + t, 1), :].rearrange(
                                    "p a n -> p (a n)")).then_inc(s_half, 1)
                        pool.wait_ge(s_half, 4 * t + 4)
                        for kind in range(2):
                            G.tensor_copy(Ks[:, kind, :], QK[:, ds(8 * kind + 4 + t, 1), :].rearrange("p a n -> p (a n)"))
                        for h in range(2):
                            G.tensor_copy(Vz[:, h, :, 64 * h:64 * h + 64], VV[:, 0, :, ds(t * P + 64 * h, 64)])
                        G.tensor_copy(Vz[:, 2, :, :], VV[:, 1, :, ds(t * P, P)]).then_inc(*pool_m.did("copied"))
                        pool.wait_ge(pool_m.sem, t + 1)

                @block.tensor
                def _(pe):
                    with pe.Fori(0, 4) as t:
                        pe.wait_ge(pool_m.sem, t + 1)
                        for i in range(U + 1):
                            if i < U:
                                kind, h, q = units[i]
                                if i >= 2:
                                    pe.wait_ge(dve_m.sem, dve_m.at(f"b{i - 2}", t))
                                else:
                                    pe.wait_ge(dve_m.sem, t * len(dve_m.names))
                                pe.matmul(ps[:, i % 2, :], Qz[:, 2 * kind + h, q * P:(q + 1) * P], Ks[:, kind, :],
                                          start=True, stop=True).then_inc(*pe_m.did(f"s{i}"))
                            if i - 1 in turns:
                                n = turns.index(i - 1)
                                pe.wait_ge(dve_m.sem, dve_m.at(f"n{i - 1}", t))
                                if n >= 2:
                                    pe.wait_ge(act_m.sem, act_m.at(f"p{turns[n - 2]}", t))
                                for k in range(TT):
                                    last = pe.transpose(ps[:, 2 + n % 2, k * P:(k + 1) * P],
                                                        PR[:, (i - 1) % 4, k * P:(k + 1) * P], self.con("id"))
                                last.then_inc(*pe_m.did(f"t{i - 1}"))
                            if i - 1 in (3, 7, 15):
                                pe.wait_ge(act_m.sem, act_m.at(f"p{i - 1}", t))
                                bank = 4 if i - 1 < 8 else 5
                                vi = {3: 0, 7: 1, 15: 2}[i - 1]
                                for k in range(TT):
                                    last = pe.matmul(ps[:, bank, :], Vz[:, vi, k, :], PT[:, k, :],
                                                     start=(k == 0 and vi != 1), stop=(k == TT - 1 and vi != 0))
                                if vi:
                                    last.then_inc(*pe_m.did(f"pv{vi - 1}"))
                        pe.wait_ge(act_m.sem, act_m.at("sq", t))
                        pe.matmul(ps[:, 6, :], self.con("ones"), ON[:, 1, :], start=True, stop=True).then_inc(
                            *pe_m.did("sub"))

                @block.scalar
                def _(act):
                    with act.Fori(0, 4) as t:
                        for i in range(U + 1):
                            if i < U:
                                act.wait_ge(dve_m.sem, dve_m.at(f"m{i}", t))
                                S.activation(PR[:, i % 4, :], SC[:, i % 2, :], ACT.Exp, bias=stat[:, i, 0:1],
                                             accum_out=stat[:, i, 1:2]).then_inc(*act_m.did(f"e{i}"))
                            if i - 1 in turns:
                                q = units[i - 1][2]
                                act.wait_ge(pe_m.sem, pe_m.at(f"t{i - 1}", t))
                                n = turns.index(i - 1)
                                S.activation(PT[:, :, q * P:(q + 1) * P],
                                             ps[:, 2 + n % 2, :].rearrange("p (k c) -> p k c", k=TT),
                                             ACT.Copy).then_inc(*act_m.did(f"p{i - 1}"))
                        act.wait_ge(pe_m.sem, pe_m.at("pv0", t))
                        S.activation(O[:, ds(t, 1), :].rearrange("p a n -> p (a n)"), ps[:, 4, ::-1], ACT.Copy).then_inc(
                            *act_m.did("oa"))
                        act.wait_ge(pe_m.sem, pe_m.at("pv1", t))
                        S.activation(ON[:, 0, :], ps[:, 5, ::-1], ACT.Copy).then_inc(*act_m.did("ob"))
                        act.wait_ge(act_m.sem, act_m.at("ob", t))
                        S.activation(ON[:, 1, :], ON[:, 0, :], ACT.Square).then_inc(*act_m.did("sq"))
                        act.wait_ge(pe_m.sem, pe_m.at("sub", t))
                        S.activation(R[:, :], ps[:, 6, :], ACT.Sqrt, bias=self.tiny[:, 2:3], scale=1.0 / P).then_inc(
                            *act_m.did("root"))

                @block.vector
                def _(dve):
                    with dve.Fori(0, 4) as t:
                        dve.wait_ge(s_g, (t + 1) * 48)

                        def mine(name):
                            dve.wait_ge(dve_m.sem, dve_m.at(name, t))

                        for i in range(U + 1):
                            if i < U:
                                kind, h, q = units[i]
                                dve.wait_ge(pe_m.sem, pe_m.at(f"s{i}", t))
                                if i >= 2:
                                    dve.wait_ge(act_m.sem, act_m.at(f"e{i - 2}", t))
                                lo = q * P
                                gi = h if kind == 0 else 2
                                V.scalar_tensor_tensor(out=SC[:, i % 2, :], in0=ps[:, i % 2, :], scalar=0.125,
                                                       in1=GT[:, gi, lo:lo + SEQ], op0=ALU.mult, op1=ALU.add).then_inc(
                                    *dve_m.did(f"b{i}"))
                                mine(f"b{i}")
                                V.tensor_reduce(stat[:, i, 0:1], SC[:, i % 2, :], AX, ALU.max, negate=True).then_inc(
                                    *dve_m.did(f"m{i}"))
                            if i >= 1:
                                u = i - 1
                                kind, h, q = units[u]
                                dve.wait_ge(act_m.sem, act_m.at(f"e{u}", t))
                                V.reciprocal(stat[:, u, 2:3], stat[:, u, 1:2]).then_inc(*dve_m.did(f"r{u}"))
                                mine(f"r{u}")
                                if kind == 0 or h == 0:
                                    V.tensor_scalar(PR[:, u % 4, :], PR[:, u % 4, :], stat[:, u, 2:3], None,
                                                    ALU.mult).then_inc(*dve_m.did(f"n{u}"))
                                else:
                                    V.tensor_tensor(stat[:, u, 3:4], stat[:, u, 2:3], lam[:, 5:6], ALU.mult).then_inc(
                                        *dve_m.did(f"l{u}"))
                                    mine(f"l{u}")
                                    V.tensor_scalar(PR[:, u % 4, :], PR[:, u % 4, :], stat[:, u, 3:4], None, ALU.mult)
                                    dve.drain()
                                    V.tensor_tensor(PR[:, u % 4, :], PR[:, (u - 1) % 4, :], PR[:, u % 4, :],
                                                    ALU.subtract).then_inc(*dve_m.did(f"n{u}"))
                        dve.wait_ge(act_m.sem, act_m.at("root", t))
                        V.reciprocal(R[:, :], R[:, :]).then_inc(*dve_m.did("rec"))
                        mine("rec")
                        V.tensor_tensor(ON[:, 0, :], ON[:, 0, :], R[:, :], ALU.mult).then_inc(*dve_m.did("obn"))
                        mine("obn")
                        V.tensor_scalar(O[:, ds(t + 4, 1), :].rearrange("p a n -> p (a n)"), ON[:, 0, :], self.col("sub"),
                                        1.0 - LAMBDA_INIT, ALU.mult, ALU.mult).then_inc(*dve_m.did("obg"))

    def toeplitz(self, head, width):
        a = self.A["bias_rows"]
        x = a[ds(head, 1), 0:1]
        return AP(x.tensor, x.offset, [(1, P), (1, width)])

    def convffn(self):
        nc, A, ring, ps, X, T, H = self.nc, self.A, self.ring, self.ps, self.X, self.T, self.H
        V, S = nc.vector, nc.scalar
        self.norm("rms2", X, self.col("n2g", 0, 8), None, 2, 32, 24, center=False)
        W = 2 * KT * P + 8
        up = [self.sem(f"up{s}") for s in range(SLOTS)]
        cv = [self.sem(f"conv{s}") for s in range(SLOTS)]
        sl = [self.sem(f"conv_silu{s}") for s in range(SLOTS)]
        s_z = self.sem("conv_zero")
        with ExitStack() as st:
            HID = self.sb(st, "chid", FT, SEQ)
            UP = self.sb(st, "up", SLOTS, 2, SEQ + 2)
            CV, PC = self.sb(st, "cv", SLOTS, 2, SEQ), self.sb(st, "convw", FT, 8)
            s_pc = self.sem("convw_in")
            with nc.Block() as block:
                @block.sync
                def _(sp):
                    sp.dma_start(PC[:, :, :], A["conv_cols"]).then_inc(s_pc, 16)
                    load_chunks(sp, ring, A["w_up"], FT, 2 * KT * P)

                @block.tensor
                def _(pe):
                    project(pe, ring, ps, FT, 2, KT, lambda k: H[:, k, :])

                @block.gpsimd
                def _(pool):
                    nc.gpsimd.memset(UP[:, :, :, :], 0.0).then_inc(s_z, 1)

                @block.scalar
                def _(act):
                    act.wait_ge(s_z, 1)

                    def body(s, trip, c):
                        act.wait_ge(ring.used[s], ring.fills[s] + trip + 1)
                        act.wait_ge(cv[s], trip * 6)
                        S.activation(UP[:, s, :, 1:SEQ + 1], ps[:, 2 * s:2 * s + 2, :], ACT.Copy).then_inc(
                            ring.drained[s], 1)
                        act.wait_ge(cv[s], trip * 6 + 6)
                        S.activation(CV[:, s, 1, :], CV[:, s, 1, :], ACT.Silu).then_inc(sl[s], 1)

                    over_chunks(act, FT, body)

                @block.vector
                def _(dve):
                    dve.wait_ge(s_pc, 16)
                    hid = [self.sem(f"conv_hid{s}") for s in range(SLOTS)]

                    def body(s, trip, c):
                        dve.wait_ge(ring.drained[s], ring.drains[s] + trip + 1)
                        dve.wait_ge(hid[s], trip)

                        def w(i):
                            return PC[:, ds(c, 1), i:i + 1].rearrange("p a b -> p (a b)")

                        for m in range(2):
                            V.tensor_scalar(CV[:, s, m, :], UP[:, s, m, 1:SEQ + 1], w(4 * m + 1), w(4 * m + 3), ALU.mult,
                                            ALU.add).then_inc(cv[s], 1)
                        for n, tap in enumerate((0, 2)):
                            dve.wait_ge(cv[s], trip * 6 + 2 * n + 2)
                            for m in range(2):
                                V.scalar_tensor_tensor(out=CV[:, s, m, :], in0=UP[:, s, m, tap:tap + SEQ], scalar=w(4 * m + tap),
                                                       in1=CV[:, s, m, :], op0=ALU.mult, op1=ALU.add).then_inc(cv[s], 1)
                        dve.wait_ge(sl[s], trip + 1)
                        V.tensor_tensor(HID[:, ds(c, 1), :].rearrange("p a n -> p (a n)"), CV[:, s, 0, :], CV[:, s, 1, :],
                                        ALU.mult).then_inc(hid[s], 1)

                    over_chunks(dve, FT, body)
            ring.end(FT)
            self.residual("down", A["w_down"], KT, 1, FT, lambda k: HID[:, k, :], 2, 40, 1.0)
        s_o = self.sem("stored")
        with nc.Block() as block:
            @block.sync
            def _(sp):
                sp.dma_start(A["out"], T[:, :, :]).then_inc(s_o, 16)
                sp.wait_ge(s_o, 16)


def _blocks(w, width, dtype=np.float32):
    k, m = w.shape
    return np.ascontiguousarray(w.reshape(k // P, P, m // width, width).transpose(2, 1, 0, 3)).reshape(
        m // width, P, (k // P) * width)


def _cols(v):
    return np.asarray(v).reshape(-1, P).T


def _constants():
    c = np.zeros((P, NCONST), np.float32)

    def put(name, a):
        lo, hi = CONST[name]
        c[:, lo:hi] = a.reshape(P, hi - lo)

    i = np.arange(P)
    same = (i[:, None] // CH) == (i[None, :] // CH)
    put("id", np.eye(P))
    put("hsum", same.astype(np.float32))
    put("hmean", same / float(CH))
    put("ones", np.ones((P, P)))
    put("mean", np.full((P, P), 1.0 / D))
    a, b = i[:, None] % CH, i[None, :] % CH
    strict = [same & (a < b), same & (a > b)]
    incl = [same & (a <= b), same & (a >= b)]
    put("mS", np.stack([np.stack([strict[d] * 1.0, incl[d] * -1.0], 1) for d in range(2)], 1))
    put("mK", np.stack([np.stack([strict[d] * 1.0, incl[d] * 1.0], 1) for d in range(2)], 1))
    lv = []
    for m in LEVELS:
        low = same & (a // (2 * m) == b // (2 * m)) & (a % (2 * m) >= m) & (b % (2 * m) < m)
        lv.append(np.stack([low * -1.0, low.T * -1.0], 1))
    put("mL", np.stack(lv, 1))
    t = np.arange(TOK)
    put("scan", np.broadcast_to((t % CH != 0) * 1.0, (P, TOK)))
    pos = np.arange(GRID_W)
    cnt = [np.clip(pos + w // 2, 0, GRID_W) - np.clip(pos - w // 2, 0, GRID_W) for w in WINDOWS]
    put("rcnt", np.broadcast_to(1.0 / np.stack(cnt), (P, 4, GRID_W)))
    return c


def _layout(z):
    g = {k: np.asarray(v) for k, v in z.items()}
    par = np.zeros((P, NCOL), np.float32)

    def put(name, a):
        lo, hi = COLS[name]
        par[0:a.shape[0], lo:hi] = a

    put("c", np.concatenate([_cols(g["c"][0]), _cols(g["c"][0]), _cols(g["c_2"][0])], 1))
    put("cc", np.concatenate([_cols(g["c_ctx"]), _cols(g["c"][0]), _cols(g["c_2"][0])], 1))
    put("adab", np.concatenate([_cols(g["ada_b"][0]), _cols(g["ada_b"][1]), _cols(g["b_ada_2"][0])], 1))
    put("lng", _cols(g["ln_g"].reshape(-1)))
    put("lnb", _cols(g["ln_b"].reshape(-1)))
    put("mu", _cols(g["rk_mu"][0].reshape(-1)))
    pair = [g["rk_w0"][0, 0], g["rk_w0"][0, 1], g["rk_a0"][0, 0], g["rk_a0"][0, 1], g["rk_k_k"][0], g["rk_k_a"][0],
            g["rk_r_k"][0].reshape(-1), g["rk_lnx_g"][0], g["rk_lnx_b"][0]]
    put("pair", np.stack([_cols(v) for v in pair], 2).reshape(P, 72))
    put("pscale", _cols(g["pool_scale"][0]))
    put("n1g", _cols(g["norm1_g_2"][0]))
    put("n2g", _cols(g["norm2_g_2"][0]))
    for n, k in (("qna", "q_norm_a_2"), ("kna", "k_norm_a_2"), ("qnb", "q_norm_b_2"), ("knb", "k_norm_b_2")):
        put(n, np.tile(g[k][0], 2)[:, None])
    put("sub", g["subln_g_2"][0][:, None])
    put("lam", np.stack([g[k][0] for k in ("lambda_q1_2", "lambda_k1_2", "lambda_q2_2", "lambda_k2_2")], 1))

    a = {"params": par, "consts": _constants()}
    a["xT"] = np.ascontiguousarray(g["x"][0].T.reshape(KT, P, SEQ).transpose(1, 0, 2))
    a["ctxT"] = np.ascontiguousarray(g["ctx"][0].T.reshape(KT, P, CTX).transpose(1, 0, 2))
    ada = np.stack([g["ada_w"][0], g["ada_w"][1], g["w_ada_2"][0]])
    a["w_ada"] = np.ascontiguousarray(ada.reshape(3, 2, 4, P, 12, 512).transpose(0, 4, 1, 3, 2, 5)).reshape(72, P, 2048)
    w1 = np.concatenate([g["rk_w1"][0, 0], g["rk_w1"][0, 1]], 1)
    a1 = np.concatenate([g["rk_a1"][0, 0], g["rk_a1"][0, 1]], 1)
    a["w_lora1"] = np.stack([_blocks(w, P)[0] for w in (w1, a1, g["rk_g1"][0])])
    zero = np.zeros((64, D), np.float32)
    second = [np.concatenate([g["rk_w2"][0, 0], zero]), np.concatenate([zero, g["rk_w2"][0, 1]]),
              np.concatenate([g["rk_a2"][0, 0], zero]), np.concatenate([zero, g["rk_a2"][0, 1]]), g["rk_g2"][0]]
    a["w_pair"] = np.concatenate([_blocks(w, P) for w in (*g["rk_w_rkv"][0], *second)], 2)
    a["w_o"] = _blocks(g["rk_w_o"][0], 2 * P)

    def side(x, y):
        bx, by = _blocks(x, P), _blocks(y, P)
        n = bx.shape[0]
        return np.stack([bx.reshape(n, P, -1, P), by.reshape(n, P, -1, P)], 3).reshape(n, P, -1)

    a["w_ffn13"] = side(g["ffn_w1"][0], g["ffn_w3"][0])
    a["w_ffn2"] = _blocks(g["ffn_w2"][0], P)
    a["w_pool"] = np.concatenate([_blocks(w, 2 * P)[0] for w in g["pool_w"][0]], 1)
    a["w_router"] = _blocks(g["moe_router_w"][0], NE)[0]
    a["router_b"] = g["moe_router_b"][0:1]
    a["tie_mask"] = np.tril(np.ones((NE, NE), np.float32), -1).reshape(1, NE * NE)
    a["w_moe13"] = np.concatenate([side(g["moe_w1"][0, e], g["moe_w3"][0, e]) for e in range(NE)])
    a["w_moe2"] = np.concatenate([_blocks(g["moe_w2"][0, e], 2 * P) for e in range(NE)])
    w = g["w_in_2"][0]
    a["w_qk"] = _blocks(np.concatenate([w[:, 0:1024], w[:, 1536:2560]], 1), 2 * P)
    v = np.stack([w[:, 1024:1536], w[:, 2560:3072]])
    a["w_v"] = np.ascontiguousarray(v.reshape(2, 2, 4, P, 512).transpose(0, 1, 3, 2, 4)).reshape(4, P, 2048)
    a["w_out"] = _blocks(g["w_out_2"][0], 2 * P)
    extra = np.zeros((1, 12), np.float32)
    extra[0, :8] = 1.0
    a["bias_table"] = np.concatenate([g["rel_bias_2"], extra])
    a["bucket_onehot"] = _buckets()
    up = g["w_up_2"][0]
    a["w_up"] = side(up[:, :FF], up[:, FF:])
    cw = np.concatenate([g["conv_w_2"][0], g["conv_b_2"]])
    a["conv_cols"] = np.ascontiguousarray(cw.reshape(4, 2, FT, P).transpose(3, 2, 1, 0)).reshape(P, FT, 8)
    a["w_down"] = _blocks(g["w_down_2"][0], P)
    return a


def _buckets():
    rel = np.arange(-511, 513)
    n = np.abs(rel)
    edge = [8, 16, 32, 64, 128, 256, 512]
    large = 7 + np.searchsorted(edge, n, side="right")
    b = np.where(rel > 0, 16, 0) + np.where(n < 8, n, np.minimum(large, 15))
    out = np.zeros((33, 1024), np.float32)
    out[b, np.arange(1024)] = 1.0
    cnt = sum(((rel % d == 0) & (n <= w // 2)).astype(int) for w, d in ((128, 1), (512, 4), (2048, 16)))
    out[32] = np.where(cnt > 0, np.log(np.maximum(cnt, 1)), -1e30)
    return out


def kernel(**inputs):
    import concourse.bacc as bacc
    from concourse.bass_utils import run_bass_kernel_spmd

    nc = bacc.Bacc("TRN2", target_bir_lowering=False, num_devices=1)
    arrays = _layout(inputs)
    A = {n: nc.dram_tensor(n, a.shape, mybir.dt.from_np(a.dtype), kind="ExternalInput").ap()
         for n, a in arrays.items()}
    A["bias_rows"] = nc.dram_tensor("bias_rows", (12, 1024), F32).ap()
    A["out"] = nc.dram_tensor("out", (P, KT, SEQ), F32, kind="ExternalOutput").ap()
    Kernel(nc, A).build()
    r = run_bass_kernel_spmd(nc, [arrays], core_ids=[0])
    y = r.results[0]["out"]
    return np.ascontiguousarray(y.transpose(1, 0, 2).reshape(D, SEQ).T)[None]
```

```python
from contextlib import ExitStack

import numpy as np
from concourse import mybir
from concourse.bass import AP, IndirectOffsetOnAxis, ds

F32 = mybir.dt.float32
I32 = mybir.dt.int32
ALU = mybir.AluOpType
ACT = mybir.ActivationFunctionType
AX = mybir.AxisListType.X

P = 128
D = 1024
KT = D // P
SEQ = 512
CTX = 256
TOK = CTX + SEQ
HALF = TOK // 2
BANK = 512
FF = 2816
FT = FF // P
NE = 8
FE = 1408
ET = FE // P
TT = SEQ // P
ITEMS = 2 * SEQ // P + NE - 1
HCOL, YCOL = 176, 256
ALPHA = float((2 * 2) ** 0.25)
LN_EPS = 1e-5
GN_EPS = 64e-5
RMS_EPS = 1e-6
DECAY = float(np.exp(-0.5))
LAMBDA_INIT = 0.8 - 0.6
GRID_W = 64
CH = 64
NCH = TOK // CH
CCH = CTX // CH
SLOTS = 3
SLOT = FT * P
WINDOWS = (2, 4, 8, 16)
PADW = 8
LEVELS = (1, 2, 4, 8, 16, 32)

COLS = {}
_at = 0
for _name, _n in (("c", 24), ("cc", 24), ("adab", 144), ("lng", 32), ("lnb", 32), ("mu", 48), ("pair", 72),
                  ("pscale", 8), ("n1g", 8), ("n2g", 8), ("qna", 1), ("kna", 1), ("qnb", 1), ("knb", 1),
                  ("sub", 1), ("lam", 4)):
    COLS[_name] = (_at, _at + _n)
    _at += _n
NCOL = _at
CONST = {}
_at = 0
for _name, _n in (("id", P), ("hsum", P), ("hmean", P), ("mean", P), ("ones", P), ("mS", 4 * P), ("mK", 4 * P),
                  ("mL", 12 * P), ("scan", TOK), ("rcnt", 4 * GRID_W)):
    CONST[_name] = (_at, _at + _n)
    _at += _n
NCONST = _at


class Marks:

    def __init__(self, sem, names, first=0):
        self.sem, self.names, self.next, self.first = sem, list(names), 0, first
        assert len(set(self.names)) == len(self.names)

    def at(self, name, it=0):
        return it * len(self.names) + self.names.index(name) + (1 + self.first)

    def trips(self, it):
        return it * len(self.names) + self.first

    def begin(self, eng):
        eng.sem_inc(self.sem, self.first)

    def did(self, name):
        assert self.names[self.next % len(self.names)] == name, (name, self.names[self.next % len(self.names)])
        self.next += 1
        return self.sem, 1


class Ring:

    def __init__(self, nc, ctx):
        self.all = ctx.enter_context(nc.sbuf_tensor("w_ring", [P, SLOTS * SLOT], F32))
        self.buf = [self.all[:, s * SLOT:(s + 1) * SLOT] for s in range(SLOTS)]
        self.loaded = [ctx.enter_context(nc.semaphore(f"w_loaded{s}")) for s in range(SLOTS)]
        self.used = [ctx.enter_context(nc.semaphore(f"w_used{s}")) for s in range(SLOTS)]
        self.drained = [ctx.enter_context(nc.semaphore(f"ps_drained{s}")) for s in range(SLOTS)]
        self.fills = [0] * SLOTS
        self.drains = [0] * SLOTS

    def used_at(self, s, k):
        return self.fills[s] + k + 2

    def drained_at(self, s, k):
        return self.drains[s] + k + 2

    def end(self, n, drains_per_chunk=1):
        for s in range(SLOTS):
            k = n // SLOTS + (s < n % SLOTS)
            self.fills[s] += k
            self.drains[s] += k * drains_per_chunk


def over_chunks(eng, n, body):
    trips = n // SLOTS
    if trips:
        with eng.Fori(0, trips) as i:
            for s in range(SLOTS):
                body(s, i, i * SLOTS + s)
    for s in range(n % SLOTS):
        body(s, trips, trips * SLOTS + s)


def load_chunks(sp, ring, src, n, width):

    def body(s, trip, c):
        sp.wait_ge(ring.used[s], ring.used_at(s, trip - 1))
        sp.dma_start(ring.buf[s][:, 0:width], src[ds(c, 1), :, :].rearrange("a p n -> (a p) n")).then_inc(
            ring.loaded[s], 16)

    over_chunks(sp, n, body)


def project(pe, ring, ps, n, m_tiles, k_tiles, moving, width=BANK, between=None):

    def body(s, trip, c):
        pe.wait_ge(ring.loaded[s], (ring.fills[s] + trip + 1) * 16)
        pe.wait_ge(ring.drained[s], ring.drained_at(s, trip - 1))
        for m in range(m_tiles):
            for k in range(k_tiles):
                at = (k * m_tiles + m) * P
                last = pe.matmul(ps[:, 2 * s + m, 0:width], ring.buf[s][:, at:at + P], moving(k),
                                 start=(k == 0), stop=(k == k_tiles - 1))
        last.then_inc(ring.used[s], 1)

    over_chunks(pe, n, body)


class Kernel:
    def __init__(self, nc, A):
        self.nc, self.A = nc, A
        self.ctx = ExitStack()

    def sb(self, ctx, name, *shape):
        return ctx.enter_context(self.nc.sbuf_tensor("sb_" + name, [P, *shape], F32))

    def marks(self, name, names, first=0):
        return Marks(self.ctx.enter_context(self.nc.semaphore(name)), names, first)

    def sem(self, name):
        return self.ctx.enter_context(self.nc.semaphore(name))

    def col(self, name, i=0, n=1):
        a = COLS[name][0] + i
        return self.par[:, a:a + n]

    def con(self, name, i=0, n=P):
        a = CONST[name][0] + i
        return self.cst[:, a:a + n]

    def build(self):
        nc = self.nc
        with self.ctx:
            ctx = self.ctx
            self.ring = Ring(nc, ctx)
            self.par = self.sb(ctx, "params", NCOL)
            self.cst = self.sb(ctx, "consts", NCONST)
            self.mod = self.sb(ctx, "mod", 3, 48, 2)
            self.tiny = self.sb(ctx, "tiny", 8)
            self.ps = ctx.enter_context(nc.psum_tensor("ps", [P, 8, BANK], F32))
            self.adaln()
            self.B0 = self.sb(ctx, "b0", KT, SEQ)
            self.rwkv()
            self.X, self.T, self.H = (self.sb(ctx, n, KT, SEQ) for n in ("x", "t", "hm"))
            for stage in (self.rwkv_out, self.ffn, self.pool, self.moe, self.attention, self.convffn):
                stage()

    def adaln(self):
        nc, A, ring, ps, mod = self.nc, self.A, self.ring, self.ps, self.mod
        s_par = self.sem("params_in")
        V = nc.vector
        NB = 4
        pe_m = self.marks("ada_pe", ["cols"], 1)
        act_m = self.marks("ada_act", ["row0", "row1", "row2"])
        dve_m = self.marks("ada_dve", ["mod"], 1)
        s_silu = self.sem("silu_c")
        s_fix = self.sem("mod_plus_one")
        with ExitStack() as st:
            cs = self.sb(st, "c_silu", 3, KT, 2)
            row = self.sb(st, "ada_row", 3, BANK)
            with nc.Block() as block:
                @block.gpsimd
                def _(pool):
                    for q in (*ring.used, *ring.drained, pe_m.sem, dve_m.sem):
                        pool.sem_inc(q, 1)

                @block.sync
                def _(sp):
                    sp.dma_start(self.par[:, :], A["params"]).then_inc(s_par, 16)
                    sp.dma_start(self.cst[:, :], A["consts"]).then_inc(s_par, 16)
                    load_chunks(sp, ring, A["w_ada"], 72, 2048)

                @block.scalar
                def _(act):
                    act.wait_ge(s_par, 32)
                    for v in range(2):
                        last = nc.scalar.activation(cs[:, :, :, v],
                                                    self.col(("c", "cc")[v], 0, 24).rearrange("p (a k) -> p a k", a=3),
                                                    ACT.Silu)
                        last.then_inc(s_silu, 1)
                    for a in range(3):
                        with act.Fori(a * NB, (a + 1) * NB) as i:
                            act.wait_ge(pe_m.sem, pe_m.trips(i))
                            for b in range(3):
                                act.wait_ge(ring.used[(2 * b + 1) % SLOTS],
                                            ring.used_at((2 * b + 1) % SLOTS, 2 * i + (2 * b + 1) // SLOTS))
                                nc.scalar.activation(row[0:2, b, :], ps[0:2, b, :], ACT.Copy).then_inc(
                                    *act_m.did(f"row{b}"))

                @block.tensor
                def _(pe):
                    pe.wait_ge(s_silu, 2)
                    pe.wait_ge(s_par, 32)
                    for a in range(3):
                        with pe.Fori(a * NB, (a + 1) * NB) as i:
                            for b in range(3):
                                for half in range(2):
                                    ch = 2 * b + half
                                    s = ch % SLOTS
                                    k = 2 * i + ch // SLOTS
                                    pe.wait_ge(ring.loaded[s], (k + 1) * 16)
                                    for kt in range(4):
                                        last = pe.matmul(ps[0:2, b, :], cs[:, a, 4 * half + kt, :],
                                                         ring.buf[s][:, kt * BANK:(kt + 1) * BANK],
                                                         start=(half == 0 and kt == 0), stop=(half == 1 and kt == 3))
                                    last.then_inc(ring.used[s], 1)
                            pe.wait_ge(dve_m.sem, dve_m.trips(i))
                            for b in range(3):
                                pe.wait_ge(act_m.sem, act_m.at(f"row{b}", i))
                                for j in range(4):
                                    at = 2 * (4 * b + j)
                                    last = pe.matmul(ps[:, 3, at:at + 2], row[0:2, b, j * P:(j + 1) * P],
                                                     self.con("id", 0, 2)[0:2, :], start=True, stop=True)
                            last.then_inc(*pe_m.did("cols"))

                @block.vector
                def _(dve):
                    dve.wait_ge(s_par, 32)
                    for a in range(3):
                        with dve.Fori(0, NB) as i:
                            dve.wait_ge(pe_m.sem, pe_m.at("cols", i + a * NB))
                            dst = mod[:, a, ds(i * 12, 12), :]
                            b = self.par[:, ds(i * 12 + (COLS["adab"][0] + 48 * a), 12)]
                            nc.vector.tensor_tensor(dst, ps[:, 3, 0:24].rearrange("p (a b) -> p a b", b=2),
                                                    b.unsqueeze(2).broadcast_to([P, 12, 2]),
                                                    ALU.add).then_inc(*dve_m.did("mod"))
                    for i, eps in enumerate((LN_EPS, GN_EPS, RMS_EPS)):
                        V.memset(self.tiny[:, i:i + 1], eps)
                    dve.wait_ge(dve_m.sem, dve_m.trips(3 * NB))
                    for j in (8, 32):
                        nc.vector.tensor_scalar(mod[:, :, j:j + 8, :], mod[:, :, j:j + 8, :], 1.0, None,
                                                ALU.add).then_inc(s_fix, 1)
        ring.end(72, 0)

    def rwkv(self):
        YG = self.B0
        with ExitStack() as mix:
            TW, TA, TG = self.sb(mix, "tw", TOK), self.sb(mix, "ta", TOK), self.sb(mix, "tg", SEQ)
            with ExitStack() as xs:
                xk, xv = self.sb(xs, "xk", KT, TOK), self.sb(xs, "xv", KT, TOK)
                xr = self.sb(xs, "xr", KT, SEQ)
                with ExitStack() as hs:
                    h, xx = self.sb(hs, "h", KT, TOK), self.sb(hs, "xx", KT, TOK)
                    self.token_mix(h, xx, xk, xv, xr, TW, TA, TG)
                self.project_rkv(xk, xv, xr)
            self.pairs(TW, TA, TG, YG)

    def project_rkv(self, xk, xv, xr):
        nc, A, ring, ps = self.nc, self.A, self.ring, self.ps
        S, V = nc.scalar, nc.vector
        N = KT // 2
        pe_m = self.marks("kv_pe", ["kv0", "kv1"], 1)
        act_m, dve_m = self.marks("kv_act", ["k0", "k1"]), self.marks("kv_dve", ["v0", "v1"])
        s_w = [self.sem(f"kv_w{i}") for i in range(2)]
        s_st = [self.sem(f"kv_stored{i}") for i in range(2)]
        s_kvf = [self.sem(f"kv_banks{i}") for i in range(2)]
        s_wr, s_pr, s_er = (self.sem(f"r_{q}") for q in ("w", "pe", "out"))
        s_sr = [self.sem(f"r_stored{i}") for i in range(4)]
        with ExitStack() as st:
            KV = self.sb(st, "kv", 2, 2, TOK)
            with nc.Block() as block:
                @block.gpsimd
                def _(pool):
                    pe_m.begin(pool)
                    for q in (*s_st, *s_kvf):
                        pool.sem_inc(q, 1)

                @block.sync
                def _(sp):
                    with sp.Fori(0, N) as i:
                        for b in range(2):
                            sp.wait_ge(pe_m.sem, pe_m.trips(i))
                            sp.dma_start(ring.buf[b][:, 0:2 * KT * P],
                                         A["w_kv"][ds(2 * i + b, 1)].rearrange("a p n -> (a p) n")).then_inc(s_w[b], 16)
                    for c in range(4):
                        if c >= 1:
                            sp.wait_ge(s_pr, 2 * c)
                        else:
                            sp.wait_ge(pe_m.sem, pe_m.trips(N))
                        sp.dma_start(ring.buf[2][:, 0:2 * KT * P], A["w_r"][c]).then_inc(s_wr, 16)

                @block.tensor
                def _(pe):
                    with pe.Fori(0, N) as i:
                        for b in range(2):
                            pe.wait_ge(s_w[b], (i + 1) * 16)
                            if b == 0:
                                pe.wait_ge(s_kvf[0], 2 * i + 1)
                            else:
                                pe.wait_ge(s_kvf[1], 2 * i + 1)
                            for m, src in enumerate((xk, xv)):
                                for hf in range(2):
                                    for k in range(KT):
                                        at = (2 * k + m) * P
                                        last = pe.matmul(ps[:, 4 * b + 2 * m + hf, 0:HALF], ring.buf[b][:, at:at + P],
                                                         src[:, k, hf * HALF:(hf + 1) * HALF],
                                                         start=(k == 0), stop=(k == KT - 1))
                            last.then_inc(*pe_m.did(f"kv{b}"))
                    pe.wait_ge(act_m.sem, act_m.trips(N))
                    pe.wait_ge(dve_m.sem, dve_m.trips(N))
                    for n in range(KT):
                        if n % 2 == 0:
                            pe.wait_ge(s_wr, (n // 2 + 1) * 16)
                        for k in range(KT):
                            last = pe.matmul(ps[:, n, :], ring.buf[2][:, (2 * k + n % 2) * P:(2 * k + n % 2 + 1) * P],
                                             xr[:, k, :], start=(k == 0), stop=(k == KT - 1))
                        last.then_inc(s_pr, 1)

                @block.scalar
                def _(act):
                    with act.Fori(0, N) as i:
                        for b in range(2):
                            act.wait_ge(pe_m.sem, pe_m.at(f"kv{b}", i))
                            act.wait_ge(s_st[b], i * 16 + 1)
                            S.activation(KV[:, b, 0, :].rearrange("p (a n) -> p a n", a=2), ps[:, 4 * b:4 * b + 2, 0:HALF],
                                         ACT.Copy).then_inc(*act_m.did(f"k{b}"))
                            act.wait_ge(act_m.sem, act_m.at(f"k{b}", i))
                            act.sem_inc(s_kvf[b], 1)
                            act.wait_ge(dve_m.sem, dve_m.at(f"v{b}", i))
                            act.sem_inc(s_kvf[b], 1)
                            act.dma_start(A["kv_rows"][ds(2 * i + b, 1)].rearrange("a p n -> (a p) n"),
                                          KV[:, b, :, :].rearrange("p a n -> p (a n)")).then_inc(s_st[b], 16)
                    for b in range(2):
                        act.wait_ge(s_st[b], 16 * N + 1)
                    for n in range(KT):
                        act.wait_ge(s_pr, n + 1)
                        if n >= 4:
                            act.wait_ge(s_sr[n % 4], 16)
                        R = KV[:, (n // 2) % 2, n % 2, 0:SEQ]
                        S.activation(R, ps[:, n, :], ACT.Copy).then_inc(s_er, 1)
                        act.wait_ge(s_er, n + 1)
                        act.dma_start(A["r_rows"][n], R).then_inc(s_sr[n % 4], 16)
                    for q in s_sr:
                        act.wait_ge(q, 32)

                @block.vector
                def _(dve):
                    with dve.Fori(0, N) as i:
                        for b in range(2):
                            dve.wait_ge(pe_m.sem, pe_m.at(f"kv{b}", i))
                            dve.wait_ge(s_st[b], i * 16 + 1)
                            V.tensor_copy(KV[:, b, 1, :].rearrange("p (a n) -> p a n", a=2),
                                          ps[:, 4 * b + 2:4 * b + 4, 0:HALF]).then_inc(*dve_m.did(f"v{b}"))

    def token_mix(self, h, xx, xk, xv, xr, TW, TA, TG):
        nc, A, ring, ps, mod = self.nc, self.A, self.ring, self.ps, self.mod
        V = nc.vector
        s_x, s_lw = self.sem("x_in"), self.sem("lora_in")
        dve_m = self.marks("mix_dve", ["h", "xw", "xa", "xg", "xk", "xv", "xr"])
        s_h = self.sem("h_steps")
        pe_m = self.marks("mix_pe", ["w", "a", "g"])
        act_m = self.marks("mix_act", ["w", "a", "g"])
        lw = [ring.buf[s][:, 0:KT * P] for s in range(3)]
        with nc.Block() as block:
            @block.sync
            def _(sp):
                sp.dma_start(h[:, :, 0:CTX], A["ctxT"]).then_inc(s_x, 16)
                sp.dma_start(h[:, :, CTX:TOK], A["xT"]).then_inc(s_x, 16)
                for i in range(3):
                    sp.dma_start(lw[i], A["w_lora1"][i]).then_inc(s_lw, 16)

            @block.vector
            def _(dve):
                dve.wait_ge(s_x, 32)
                for k in range(KT):
                    for who, a, b in ((1, 0, CTX), (0, CTX, TOK)):
                        last = V.tensor_scalar(h[:, k, a:b], h[:, k, a:b], mod[:, 0, 8 + k, who:who + 1],
                                               mod[:, 0, k, who:who + 1], ALU.mult, ALU.add)
                        last.then_inc(s_h, 1)
                dve.wait_ge(s_h, 2 * KT)
                V.tensor_scalar(xx[:, :, :], h[:, :, :], -1.0, None, ALU.mult).then_inc(*dve_m.did("h"))
                dve.wait_ge(dve_m.sem, dve_m.at("h"))
                ops = [(slice(0, 4), (1, CTX), (0, CTX - 1)), (slice(4, 8), (0, CTX - 1), (1, CTX))]
                for f, (a, b), (c, d) in ops:
                    V.tensor_tensor(xx[:, f, a:b], h[:, f, c:d], h[:, f, a:b], ALU.subtract).then_inc(s_h, 1)
                R = SEQ // GRID_W
                for f, (r0, c0), (nr, ncol), (rs, cs) in (
                        (slice(0, 2), (0, 1), (R, GRID_W - 1), (0, 0)), (slice(2, 4), (0, 0), (R, GRID_W - 1), (0, 1)),
                        (slice(4, 6), (1, 0), (R - 1, GRID_W), (0, 0)), (slice(6, 8), (0, 0), (R - 1, GRID_W), (1, 0))):
                    for k in range(f.start, f.stop):
                        g = h[:, k, CTX:TOK].rearrange("p (r c) -> p r c", c=GRID_W)
                        o = xx[:, k, CTX:TOK].rearrange("p (r c) -> p r c", c=GRID_W)
                        V.tensor_tensor(o[:, r0:r0 + nr, c0:c0 + ncol], g[:, rs:rs + nr, cs:cs + ncol],
                                        g[:, r0:r0 + nr, c0:c0 + ncol], ALU.subtract).then_inc(s_h, 1)
                dve.wait_ge(s_h, 2 * KT + 2 + KT)
                for name, mu, dst, a, free in (("xw", 1, xk, 0, None), ("xa", 4, xv, 0, None), ("xg", 5, xr, CTX, None),
                                               ("xk", 2, xk, 0, "w"), ("xv", 3, xv, 0, "a"), ("xr", 0, xr, CTX, "g")):
                    if free:
                        dve.wait_ge(pe_m.sem, pe_m.at(free))
                    for k in range(KT):
                        last = V.scalar_tensor_tensor(out=dst[:, k, :], in0=xx[:, k, a:TOK],
                                                      scalar=self.col("mu", mu * 8 + k), in1=h[:, k, a:TOK],
                                                      op0=ALU.mult, op1=ALU.add)
                    last.then_inc(*dve_m.did(name))

            @block.tensor
            def _(pe):
                pe.wait_ge(s_lw, 48)
                for i, (name, src, need) in enumerate((("w", xk, "xw"), ("a", xv, "xa"), ("g", xr, "xg"))):
                    pe.wait_ge(dve_m.sem, dve_m.at(need))
                    spans = [(0, HALF), (HALF, TOK)] if i < 2 else [(0, SEQ)]
                    for b, (c, d) in enumerate(spans):
                        for k in range(KT):
                            last = pe.matmul(ps[:, 2 * i + b, 0:d - c], lw[i][:, k * P:(k + 1) * P], src[:, k, c:d],
                                             start=(k == 0), stop=(k == KT - 1))
                    last.then_inc(*pe_m.did(name))

            @block.scalar
            def _(act):
                for i, (name, dst, f) in enumerate((("w", TW, ACT.Tanh), ("a", TA, ACT.Copy), ("g", TG, ACT.Sigmoid))):
                    act.wait_ge(pe_m.sem, pe_m.at(name))
                    if i < 2:
                        o, src = dst[:, :].rearrange("p (a b) -> p a b", a=2), ps[:, 2 * i:2 * i + 2, 0:HALF]
                    else:
                        o, src = dst[:, :], ps[:, 4, :]
                    nc.scalar.activation(o, src, f).then_inc(*act_m.did(name))

    def pairs(self, TW, TA, TG, YG):
        nc, A, ring, ps = self.nc, self.A, self.ring, self.ps
        V, S = nc.vector, nc.scalar
        N, NQ = KT, NCH // 2
        LAST = 4
        lin = self.marks("lin_pe", ["g", "w0", "w1", "a0", "a1", "norm", "coef"])
        f_act = self.marks("feat_act", ["g", "w0", "w1", "a0", "a1", "root", "Px", "Pi", "P"])
        f_dve = self.marks("feat_dve", ["pj", "omka", "kkr", "sq", "max", "rec", "kk", "scan", "ex", "in1", "A", "kka", "B",
                                        "kd", "kdk", "K", "R", "kds", "rr", "coefin", "bonus"])
        o_pe = self.marks("out_pe", ["mean", "var"])
        o_act = self.marks("out_act", ["root"])
        o_dve = self.marks("out_dve", ["Y", "yc", "sq", "rec", "yn", "affine", "bonus", "gated"])

        def lat(n):
            return n >= CCH

        def steps(q):
            return [2 * q, 2 * q + 1] if 0 <= q < NQ else []

        def chain(n):
            return [f"U{n}", f"Z{n}"] + [f"Y{n}"] * lat(n)

        order = []
        for q in range(NQ + 1):
            ab, pq = steps(q), steps(q - 1)
            order += [f"score{n}" for n in ab] + [f"trans{n}" for n in ab[:1]] + [f"L{n}" for n in ab]
            order += [f"X0.{n}" for n in ab] + [f"trans{n}" for n in ab[1:]] + [f"T0.{n}" for n in ab]
            order += [f"U{n}" for n in pq[:1]]
            order += [f"X1.{n}" for n in ab] + [f"T1.{n}" for n in ab]
            order += [x for n in pq[:1] for x in chain(n)[1:]]
            order += [f"X2.{n}" for n in ab] + [f"T2.{n}" for n in ab]
            order += [f"U{n}" for n in pq[1:]]
            order += [f"X3.{n}" for n in ab] + [f"T3.{n}" for n in ab]
            order += [x for n in pq[1:] for x in chain(n)[1:]]
            order += [f"X4.{n}" for n in ab] + [f"T4.{n}" for n in ab] + [f"akv{n}" for n in ab]
        pe_m = self.marks("rec_pe", order, 1)
        act_of = {"trans": ["trB", "tr"], "U": ["U", "Zs"], "akv": ["akv"], "Y": ["Y"]}
        dve_of = {"score": ["sS", "sK"], "L": ["t0a", "t0b", "t0."], "X": ["x"], "T": ["t"], "Z": ["z"]}

        def follow(table):
            out = []
            for x in order:
                head = x.rstrip("0123456789.")
                for y in table.get(head, ()):
                    if y == "t":
                        out.append(f"t{int(x[1]) + 1}.{x[3:]}")
                    elif y == "x":
                        out.append(f"x{x[1:]}")
                    else:
                        out.append(y + x[len(head):])
            return out

        act_m = self.marks("rec_act", follow(act_of))
        dve_m = self.marks("rec_dve", follow(dve_of))
        pool_m = self.marks("rec_pool", [f"bd{n}" for n in range(NCH)])
        phase, passed, z_init = self.sem("phase"), self.sem("barriers_passed"), self.sem("state_zeroed")
        s_k, s_v, s_w = self.sem("kr_in"), self.sem("v_in"), self.sem("w_pair_in")

        def chunk_at(n, d):
            if d == 0:
                return n * CH
            return (CCH - 1 - n) * CH if n < CCH else (NCH - 1 - (n - CCH)) * CH

        with ExitStack() as st:
            k, v, kk, t1 = (self.sb(st, n, TOK) for n in ("k", "v", "kk", "t1"))
            r, g, bon = (self.sb(st, n, SEQ) for n in ("r", "g", "bon"))
            a, sg, cs, ex, Pi = (self.sb(st, n, 2, TOK) for n in ("a", "sg", "cs", "ex", "Pi"))
            FR, Y = self.sb(st, "FR", 2, SEQ), self.sb(st, "Y", 2, SEQ)
            PJ, W = self.sb(st, "pj", 10), self.sb(st, "w_pair", 5 * P)
            Z, Zs, Us = self.sb(st, "Z", 2, P), self.sb(st, "Zs", 2, P), self.sb(st, "Us", 2, P)
            SETS = 4
            bd = ring.all[:, 0:SETS * 10 * P].rearrange("p (s d i n) -> p s d i n", s=SETS, d=2, i=5)
            off = SETS * 10 * P
            TB = ring.all[:, off:off + SETS * 4 * P].rearrange("p (s d i n) -> p s d i n", s=SETS, d=2, i=2)
            off += SETS * 4 * P
            Xs = ring.all[:, off:off + 4 * P].rearrange("p (s d n) -> p s d n", s=2, d=2)
            tr = self.sb(st, "tr", SETS, 2, 4, P)
            LK = self.sb(st, "lk", SETS, 2, 4, P)
            AT = self.sb(st, "at", SETS, 2, 2, P)
            FB, FK, FA, Pn = sg, Pi, ex, cs

            def barrier(eng, own, j, i):
                for m in own:
                    eng.wait_ge(m.sem, m.trips(j + 1))
                eng.sem_inc(phase, 1)
                eng.wait_ge(phase, 4 * (3 * j + i + 1))
                eng.sem_inc(passed, 1)

            def halves(x):
                return x.rearrange("p (a b) -> p a b", a=2)

            with nc.Block() as block:
                @block.sync
                def _(sp):
                    def row(name, j):
                        x = A[name][0] if j is None else A[name][ds(j, 1)].rearrange("a p n -> (a p) n")
                        return x

                    def loads(j):
                        kv = row("kv_rows", j)
                        sp.dma_start(k[:, :], kv[:, 0:TOK]).then_inc(s_k, 16)
                        sp.dma_start(r[:, :], row("r_rows", j)).then_inc(s_k, 16)
                        sp.dma_start(W[:, :], row("w_pair", j)).then_inc(s_w, 16)
                        return kv

                    kv = loads(None)
                    sp.dma_start(v[:, :], kv[:, TOK:2 * TOK]).then_inc(s_v, 16)
                    with sp.Fori(1, N) as j:
                        sp.wait_ge(phase, 4 * (3 * j - 3 + 1))
                        kv = loads(j)
                        sp.wait_ge(phase, 4 * (3 * j - 3 + 2))
                        sp.dma_start(v[:, :], kv[:, TOK:2 * TOK]).then_inc(s_v, 16)

                @block.gpsimd
                def _(pool):
                    G = nc.gpsimd
                    pe_m.begin(pool)
                    G.memset(bd[:, :, :, :, :], 0.0).then_inc(z_init, 1)
                    pool.wait_ge(z_init, 1)
                    with pool.Fori(0, N) as j:
                        G.memset(Z[:, :, :], 0.0).then_inc(z_init, 1)
                        pool.wait_ge(z_init, j + 2)
                        barrier(pool, [], j, 0)
                        for n in range(NCH):
                            if n >= SETS:
                                pool.wait_ge(pe_m.sem, pe_m.at(chain(n - SETS)[-1], j))
                                pool.sem_inc(passed, 1)
                            for d in range(2):
                                at = chunk_at(n, d)
                                c = slice(at, at + CH)
                                srcs = [(0, FA[:, d, c]), (2, FB[:, d, c]), (3, FK[:, d, c]), (4, v[:, c])]
                                if lat(n):
                                    srcs.append((1, FR[:, d, at - CTX:at - CTX + CH]))
                                for i, src in srcs:
                                    for hh in range(2):
                                        rows = slice(64 * hh, 64 * hh + 64)
                                        last = G.tensor_copy(bd[rows, n % SETS, d, i, rows], src[rows])
                            last.then_inc(*pool_m.did(f"bd{n}"))
                        barrier(pool, [pool_m], j, 1)
                        barrier(pool, [], j, 2)

                @block.tensor
                def _(pe):
                    ident = self.con("id")
                    with pe.Fori(0, N) as j:
                        pe.wait_ge(s_w, (j + 1) * 16)
                        pe.matmul(ps[:, 0, :], W[:, 4 * P:5 * P], TG[:, :], start=True, stop=True).then_inc(*lin.did("g"))
                        for name, i, src, bank in (("w0", 0, TW, 2), ("w1", 1, TW, 4), ("a0", 2, TA, 6), ("a1", 3, TA, 0)):
                            if name == "a1":
                                pe.wait_ge(f_act.sem, f_act.at("g", j))
                            for b in range(2):
                                last = pe.matmul(ps[:, bank + b, 0:HALF], W[:, i * P:(i + 1) * P],
                                                 src[:, b * HALF:(b + 1) * HALF], start=True, stop=True)
                            last.then_inc(*lin.did(name))
                        pe.wait_ge(f_dve.sem, f_dve.at("sq", j))
                        pe.wait_ge(f_act.sem, f_act.at("w0", j))
                        for b in range(2):
                            last = pe.matmul(ps[:, 2 + b, 0:HALF], self.con("hsum"), t1[:, b * HALF:(b + 1) * HALF],
                                             start=True, stop=True)
                        last.then_inc(*lin.did("norm"))
                        pe.wait_ge(f_dve.sem, f_dve.at("coefin", j))
                        pe.wait_ge(f_act.sem, f_act.at("a1", j))
                        pe.matmul(ps[:, 6, :], self.con("hsum"), t1[:, 0:SEQ], start=True, stop=True).then_inc(
                            *lin.did("coef"))
                        barrier(pe, [lin], j, 0)

                        def after(marks, name):
                            pe.wait_ge(marks.sem, marks.at(name, j))

                        def two(bank, lo, mm):
                            for d in range(2):
                                last = mm(ps[:, bank, lo + d * P:lo + (d + 1) * P], d)
                            return last

                        for x in order:
                            head, rest = x.rstrip("0123456789."), x[len(x.rstrip("0123456789.")):]
                            n = int(rest.split(".")[-1])
                            i = int(rest[0]) if "." in rest else 0
                            s, h = n % SETS, n % 2
                            B, TR, SC, TI, X2 = bd[:, s], tr[:, s], LK[:, s], TB[:, s], Xs[:, h]
                            if head == "score":
                                after(pool_m, f"bd{n}")
                                if n >= 2:
                                    after(dve_m, f"t5.{n - 2}")
                                nr = 2 if lat(n) else 1
                                for o, bank in ((2, 2 * h), (3, 2 * h + 1)):
                                    for d in range(2):
                                        last = pe.matmul(ps[:, bank, 256 * d:256 * d + nr * P], B[:, d, o, :],
                                                         B[:, d, 0:nr, :].rearrange("p a b -> p (a b)"),
                                                         start=True, stop=True)
                            elif head == "trans":
                                if h:
                                    after(act_m, f"tr{n - 1}")
                                elif n >= 2:
                                    after(act_m, f"akv{n - 1}")
                                for d in range(2):
                                    for o, src in enumerate((0, 3, 4, 2)):
                                        last = pe.transpose(ps[:, 4 + d, o * P:(o + 1) * P], B[:, d, src, :], ident)
                            elif head == "L":
                                after(dve_m, f"sS{n}")
                                last = two(2 * h, 0, lambda o, d: pe.transpose(o, SC[:, d, 0, :], ident))
                            elif head == "X":
                                after(dve_m, f"t{i}.{n}")
                                last = two(2 * h, 0, lambda o, d: pe.matmul(o, SC[:, d, 0, :], TI[:, d, 0, :],
                                                                            start=True, stop=True))
                            elif head == "T":
                                after(dve_m, f"x{i}.{n}")
                                if i == 0:
                                    after(dve_m, f"sK{n}")
                                for d in range(2):
                                    o = ps[:, 2 * h + 1, 256 * d:256 * d + 2 * P]
                                    if i < LAST:
                                        pe.matmul(o[:, 0:P], TI[:, d, 1, :], X2[:, d, :], start=True, stop=True)
                                    last = pe.matmul(o[:, P:2 * P], X2[:, d, :], TI[:, d, 1, :], start=True, stop=True)
                            elif head == "akv":
                                after(act_m, f"tr{n | 1}")
                                after(dve_m, f"t5.{n}")
                                two(4 + h, 0, lambda o, d: pe.matmul(o, SC[:, d, 2, :], TR[:, d, 2, :], start=True, stop=True))
                                last = two(4 + h, 256, lambda o, d: pe.matmul(o, TR[:, d, 0, :], TI[:, d, 1, :],
                                                                              start=True, stop=True))
                            elif head == "U":
                                after(act_m, f"akv{n}")
                                if n:
                                    after(dve_m, f"z{n - 1}")
                                for d in range(2):
                                    o = ps[:, 6, d * P:(d + 1) * P]
                                    pe.matmul(o, TI[:, d, 1, :], AT[:, s, 0, d, :], start=True, stop=False)
                                    last = pe.matmul(o, AT[:, s, 1, d, :], Z[:, d, :], start=False, stop=True)
                            elif head == "Z":
                                after(act_m, f"U{n}")
                                for d in range(2):
                                    o = ps[:, 6, (2 + d) * P:(3 + d) * P]
                                    pe.matmul(o, TR[:, d, 1, :], TR[:, d, 2, :], start=True, stop=False)
                                    last = pe.matmul(o, TR[:, d, 3, :], Us[:, d, :], start=False, stop=True)
                            elif head == "Y":
                                if n > CCH:
                                    after(act_m, f"Y{n - 1}")
                                for d in range(2):
                                    o = ps[:, 7, d * P:(d + 1) * P]
                                    pe.matmul(o, Z[:, d, :], B[:, d, 1, :], start=True, stop=False)
                                    pe.matmul(o, TR[:, d, 2, :], SC[:, d, 3, :], start=False, stop=False)
                                    last = pe.matmul(o, Us[:, d, :], SC[:, d, 1, :], start=False, stop=True)
                            last.then_inc(*pe_m.did(x))
                        barrier(pe, [pe_m], j, 1)
                        for name, need, src in (("mean", "Y", Y[:, 0, :]), ("var", "sq", t1[:, 0:SEQ])):
                            pe.wait_ge(o_dve.sem, o_dve.at(need, j))
                            pe.matmul(ps[:, 0 if name == "mean" else 1, :], self.con("hmean"), src,
                                      start=True, stop=True).then_inc(*o_pe.did(name))
                        barrier(pe, [o_pe], j, 2)

                @block.scalar
                def _(act):
                    with act.Fori(0, N) as j:
                        act.wait_ge(f_dve.sem, f_dve.at("pj", j))
                        for name, bank, dst, f, pc in (
                                ("g", 0, g, ACT.Copy, None),
                                ("w0", 2, sg[:, 0, :], ACT.Sigmoid, 0), ("w1", 4, sg[:, 1, :], ACT.Sigmoid, 1),
                                ("a0", 6, a[:, 0, :], ACT.Sigmoid, 2), ("a1", 0, a[:, 1, :], ACT.Sigmoid, 3)):
                            act.wait_ge(lin.sem, lin.at(name, j))
                            if name == "g":
                                S.activation(dst[:, :], ps[:, bank, :], f).then_inc(*f_act.did(name))
                            else:
                                S.activation(halves(dst), ps[:, bank:bank + 2, 0:HALF], f,
                                             bias=PJ[:, pc:pc + 1]).then_inc(*f_act.did(name))
                        act.wait_ge(lin.sem, lin.at("norm", j))
                        S.activation(halves(kk[:, :]), ps[:, 2:4, 0:HALF], ACT.Sqrt).then_inc(*f_act.did("root"))
                        act.wait_ge(f_dve.sem, f_dve.at("in1", j))
                        S.activation(ex[:, :, :], ex[:, :, :], ACT.Exp, scale=-DECAY).then_inc(*f_act.did("Px"))
                        S.activation(Pi[:, :, :], cs[:, :, :], ACT.Exp, scale=DECAY).then_inc(*f_act.did("Pi"))
                        act.wait_ge(f_act.sem, f_act.at("Pi", j))
                        S.activation(Pn[:, :, :], cs[:, :, :], ACT.Exp, scale=-DECAY).then_inc(*f_act.did("P"))
                        barrier(act, [f_act], j, 0)
                        for x in order:
                            head = x.rstrip("0123456789.")
                            if head not in act_of:
                                continue
                            n = int(x[len(head):])
                            s, h = n % SETS, n % 2
                            act.wait_ge(pe_m.sem, pe_m.at(x, j))
                            if head == "trans":
                                S.activation(tr[:, s, :, 3, :], ps[:, 4:6, 3 * P:4 * P], ACT.Copy, scale=-1.0).then_inc(
                                    *act_m.did(f"trB{n}"))
                                S.activation(tr[:, s, :, 0:3, :], ps[:, 4:6, 0:3 * P].rearrange("p d (o n) -> p d o n", o=3),
                                             ACT.Copy).then_inc(*act_m.did(f"tr{n}"))
                            elif head == "akv":
                                S.activation(AT[:, s, :, :, :].rearrange("p a d n -> p (a d n)"), ps[:, 4 + h, :],
                                             ACT.Copy).then_inc(*act_m.did(f"akv{n}"))
                            elif head == "U":
                                S.activation(Us[:, :, :].rearrange("p d n -> p (d n)"), ps[:, 6, 0:256],
                                             ACT.Copy).then_inc(*act_m.did(f"U{n}"))
                                for d in range(2):
                                    at = chunk_at(n, d) + (CH - 1 if d == 0 else 0)
                                    last = S.activation(Zs[:, d, :], Z[:, d, :], ACT.Copy, scale=Pn[:, d, at:at + 1])
                                last.then_inc(*act_m.did(f"Zs{n}"))
                            elif head == "Y":
                                for d in range(2):
                                    at = chunk_at(n, d) - CTX
                                    for hh in range(2):
                                        rows = slice(64 * hh, 64 * hh + 64)
                                        last = S.activation(Y[rows, d, at:at + CH],
                                                            ps[rows, 7, d * P + 64 * hh:d * P + 64 * hh + 64], ACT.Copy)
                                last.then_inc(*act_m.did(f"Y{n}"))
                        barrier(act, [act_m], j, 1)
                        act.wait_ge(o_pe.sem, o_pe.at("var", j))
                        S.activation(t1[:, 0:SEQ], ps[:, 1, :], ACT.Sqrt, bias=self.tiny[:, 1:2]).then_inc(*o_act.did("root"))
                        barrier(act, [o_act], j, 2)

                @block.vector
                def _(dve):
                    with dve.Fori(0, N) as j:
                        def own(name):
                            dve.wait_ge(f_dve.sem, f_dve.at(name, j))

                        def sc(name):
                            dve.wait_ge(f_act.sem, f_act.at(name, j))

                        b0 = COLS["pair"][0]
                        V.tensor_copy(PJ[:, 0:9], self.par[:, ds(j * 9 + b0, 9)]).then_inc(*f_dve.did("pj"))
                        own("pj")
                        V.tensor_scalar(PJ[:, 9:10], PJ[:, 5:6], -1.0, 1.0, ALU.mult, ALU.add).then_inc(*f_dve.did("omka"))
                        dve.wait_ge(s_k, (j + 1) * 32)
                        V.tensor_scalar(t1[:, :], k[:, :], PJ[:, 4:5], None, ALU.mult).then_inc(*f_dve.did("kkr"))
                        own("kkr")
                        V.tensor_tensor(t1[:, :], t1[:, :], t1[:, :], ALU.mult).then_inc(*f_dve.did("sq"))
                        sc("root")
                        V.tensor_scalar(kk[:, :], kk[:, :], 1e-12, None, ALU.max).then_inc(*f_dve.did("max"))
                        own("max")
                        V.reciprocal(kk[:, :], kk[:, :]).then_inc(*f_dve.did("rec"))
                        own("rec")
                        V.tensor_tensor(kk[:, :], kk[:, :], k[:, :], ALU.mult)
                        sc("w1")
                        for d in range(2):
                            last = V.tensor_tensor_scan(cs[:, d, :], self.con("scan", 0, TOK), sg[:, d, :], 0.0,
                                                        ALU.mult, ALU.add)
                        last.then_inc(*f_dve.did("kk"))
                        own("kk")
                        V.tensor_scalar(kk[:, :], kk[:, :], PJ[:, 4:5], None, ALU.mult).then_inc(*f_dve.did("scan"))
                        chunks = "p (c t) -> p c t"
                        c1 = cs[:, 1, :].rearrange(chunks, t=CH)
                        V.tensor_tensor(ex[:, 0, :], cs[:, 0, :], sg[:, 0, :], ALU.subtract)
                        V.tensor_tensor(ex[:, 1, :].rearrange(chunks, t=CH), c1[:, :, CH - 1:CH].broadcast_to([P, NCH, CH]), c1,
                                        ALU.subtract).then_inc(*f_dve.did("ex"))
                        own("ex")
                        V.tensor_tensor(cs[:, 1, :], ex[:, 1, :], sg[:, 1, :], ALU.add).then_inc(*f_dve.did("in1"))
                        own("in1")
                        sc("Px")
                        kk2 = kk[:, :].unsqueeze(1).broadcast_to([P, 2, TOK])
                        k2 = k[:, :].unsqueeze(1).broadcast_to([P, 2, TOK])
                        V.tensor_tensor(FA[:, :, :], ex[:, :, :], kk2, ALU.mult).then_inc(*f_dve.did("A"))
                        V.tensor_tensor(FB[:, :, :], a[:, :, :], kk2, ALU.mult).then_inc(*f_dve.did("kka"))
                        own("kka")
                        sc("Pi")
                        V.tensor_tensor(FB[:, :, :], FB[:, :, :], Pi[:, :, :], ALU.mult).then_inc(*f_dve.did("B"))
                        V.tensor_scalar(a[:, :, :], a[:, :, :], PJ[:, 5:6], PJ[:, 9:10], ALU.mult, ALU.add).then_inc(
                            *f_dve.did("kd"))
                        own("kd")
                        V.tensor_tensor(a[:, :, :], a[:, :, :], k2, ALU.mult).then_inc(*f_dve.did("kdk"))
                        own("kdk")
                        V.tensor_tensor(FK[:, :, :], a[:, :, :], Pi[:, :, :], ALU.mult).then_inc(*f_dve.did("K"))
                        sc("P")
                        V.tensor_tensor(FR[:, :, :], Pn[:, :, CTX:TOK], r[:, :].unsqueeze(1).broadcast_to([P, 2, SEQ]),
                                        ALU.mult).then_inc(*f_dve.did("R"))
                        V.tensor_tensor(bon[:, :], a[:, 0, CTX:TOK], a[:, 1, CTX:TOK], ALU.add).then_inc(*f_dve.did("kds"))
                        own("R")
                        V.tensor_scalar(r[:, :], r[:, :], PJ[:, 6:7], None, ALU.mult).then_inc(*f_dve.did("rr"))
                        own("rr")
                        V.tensor_tensor(t1[:, 0:SEQ], r[:, :], bon[:, :], ALU.mult).then_inc(*f_dve.did("coefin"))
                        dve.wait_ge(lin.sem, lin.at("coef", j))
                        dve.wait_ge(s_v, (j + 1) * 16)
                        V.tensor_tensor(bon[:, :], ps[:, 6, :], v[:, CTX:TOK], ALU.mult).then_inc(*f_dve.did("bonus"))
                        barrier(dve, [f_dve], j, 0)

                        def mine(name):
                            dve.wait_ge(dve_m.sem, dve_m.at(name, j))

                        def four(x):
                            return x.rearrange("p (a b n) -> p a b n", a=2, b=2)

                        mL = self.con("mL", 0, 12 * P).rearrange("p (l d n) -> p l d n", l=6, d=2)
                        for x in order:
                            head, rest = x.rstrip("0123456789."), x[len(x.rstrip("0123456789.")):]
                            if head not in dve_of:
                                continue
                            n = int(rest.split(".")[-1])
                            i = int(rest[0]) if "." in rest else 0
                            s, h = n % SETS, n % 2
                            dve.wait_ge(pe_m.sem, pe_m.at(x, j))
                            if head == "score":
                                nr = 2 if lat(n) else 1
                                for name, bank, mask, o in ((f"sS{n}", 2 * h, "mS", 0), (f"sK{n}", 2 * h + 1, "mK", 2)):
                                    V.tensor_tensor(LK[:, s, :, o:o + nr, :], four(ps[:, bank, :])[:, :, 0:nr, :],
                                                    four(self.con(mask, 0, 4 * P))[:, :, 0:nr, :],
                                                    ALU.mult).then_inc(*dve_m.did(name))
                            elif head == "L":
                                V.tensor_tensor(TB[:, s, :, 0, :], ps[:, 2 * h, 0:256].rearrange("p (d n) -> p d n", d=2),
                                                mL[:, 0, :, :], ALU.mult).then_inc(*dve_m.did(f"t0a{n}"))
                                mine(f"sS{n}")
                                for d in range(2):
                                    last = V.tensor_tensor(TB[:, s, d, 1, :], LK[:, s, d, 0, :], mL[:, 0, 1 - d, :], ALU.mult)
                                last.then_inc(*dve_m.did(f"t0b{n}"))
                                mine(f"t0b{n}")
                                V.tensor_tensor(TB[:, s], TB[:, s],
                                                self.con("id").unsqueeze(1).unsqueeze(1).broadcast_to([P, 2, 2, P]),
                                                ALU.add).then_inc(*dve_m.did(f"t0.{n}"))
                            elif head == "X":
                                V.tensor_tensor(Xs[:, h], ps[:, 2 * h, 0:256].rearrange("p (d n) -> p d n", d=2),
                                                mL[:, i + 1, :, :], ALU.mult).then_inc(*dve_m.did(f"x{i}.{n}"))
                            elif head == "T":
                                lo = 0 if i < LAST else 1
                                V.tensor_tensor(TB[:, s, :, lo:2, :], TB[:, s, :, lo:2, :],
                                                four(ps[:, 2 * h + 1, :])[:, :, lo:2, :],
                                                ALU.add).then_inc(*dve_m.did(f"t{i + 1}.{n}"))
                            elif head == "Z":
                                dve.wait_ge(act_m.sem, act_m.at(f"Zs{n}", j))
                                if lat(n):
                                    dve.wait_ge(pe_m.sem, pe_m.at(f"Y{n}", j))
                                for d in range(2):
                                    at = chunk_at(n, d) + (CH - 1 if d == 0 else 0)
                                    last = V.scalar_tensor_tensor(out=Z[:, d, :], in0=ps[:, 6, (2 + d) * P:(3 + d) * P],
                                                                  scalar=Pn[:, d, at:at + 1], in1=Zs[:, d, :],
                                                                  op0=ALU.mult, op1=ALU.add)
                                last.then_inc(*dve_m.did(f"z{n}"))
                        barrier(dve, [dve_m], j, 1)

                        def out(name):
                            dve.wait_ge(o_dve.sem, o_dve.at(name, j))

                        y, t = Y[:, 0, :], t1[:, 0:SEQ]
                        V.tensor_tensor(y, Y[:, 0, :], Y[:, 1, :], ALU.add).then_inc(*o_dve.did("Y"))
                        dve.wait_ge(o_pe.sem, o_pe.at("mean", j))
                        V.tensor_tensor(Y[:, 1, :], y, ps[:, 0, :], ALU.subtract).then_inc(*o_dve.did("yc"))
                        out("yc")
                        V.tensor_tensor(t, Y[:, 1, :], Y[:, 1, :], ALU.mult).then_inc(*o_dve.did("sq"))
                        dve.wait_ge(o_act.sem, o_act.at("root", j))
                        V.reciprocal(t, t).then_inc(*o_dve.did("rec"))
                        out("rec")
                        V.tensor_tensor(t, t, Y[:, 1, :], ALU.mult).then_inc(*o_dve.did("yn"))
                        out("yn")
                        V.tensor_scalar(t, t, PJ[:, 7:8], PJ[:, 8:9], ALU.mult, ALU.add).then_inc(*o_dve.did("affine"))
                        out("affine")
                        V.tensor_tensor(t, t, bon[:, :], ALU.add).then_inc(*o_dve.did("bonus"))
                        out("bonus")
                        V.tensor_tensor(YG[:, ds(j, 1), :].rearrange("p a n -> p (a n)"), t, g[:, :], ALU.mult).then_inc(
                            *o_dve.did("gated"))
                        barrier(dve, [o_dve], j, 2)

    def residual(self, name, src, n, m_tiles, k_tiles, moving, layer, gate, alpha, load_x=None, scale=None):
        nc, ring, ps, X, T = self.nc, self.ring, self.ps, self.X, self.T
        V = nc.vector
        width = m_tiles * k_tiles * P
        s_a = self.sem(name + "_scaled")
        s_x = self.sem(name + "_x_in") if load_x is not None else None
        with nc.Block() as block:
            @block.sync
            def _(sp):
                if load_x is not None:
                    sp.dma_start(X[:, :, :], load_x).then_inc(s_x, 16)
                load_chunks(sp, ring, src, n, width)

            @block.tensor
            def _(pe):
                project(pe, ring, ps, n, m_tiles, k_tiles, moving)

            @block.scalar
            def _(act):
                if load_x is not None:
                    act.wait_ge(s_x, 16)
                nc.scalar.activation(T[:, :, :], X[:, :, :], ACT.Copy, scale=alpha).then_inc(s_a, 1)

            @block.vector
            def _(dve):
                dve.wait_ge(s_a, 1)

                def body(s, trip, c):
                    dve.wait_ge(ring.used[s], ring.used_at(s, trip))
                    for m in range(m_tiles):
                        t = T[:, ds(c * m_tiles + m, 1), :].rearrange("p a n -> p (a n)")
                        g = self.mod[:, layer, ds(c * m_tiles + (gate + m), 1), 0:1].rearrange("p a b -> p (a b)")
                        last = V.scalar_tensor_tensor(out=t, in0=ps[:, 2 * s + m, :], scalar=g, in1=t,
                                                      op0=ALU.mult, op1=ALU.add)
                    last.then_inc(ring.drained[s], 1)

                over_chunks(dve, n, body)
        ring.end(n)

    def norm(self, name, src, gamma, beta, layer, scale, shift, center=True):
        nc, ps, X, H, mod = self.nc, self.ps, self.X, self.H, self.mod
        V, S = nc.vector, nc.scalar
        tiles = range(KT)
        pe_m = self.marks(name + "_pe", ["mean"] * center + ["var"])
        act_m = self.marks(name + "_act", [f"q{k}" for k in tiles] + ["root"] + [f"x{k}" for k in tiles] * center)
        dve_m = self.marks(name + "_dve", [f"c{k}" for k in tiles] * center + ["gs"] * (not center) + ["rec"]
                           + [f"n{k}" for k in tiles] + [f"h{k}" for k in tiles])
        with ExitStack() as st:
            SQ, R = self.sb(st, name + "sq", KT, SEQ), self.sb(st, name + "r", SEQ)
            gs = self.sb(st, name + "gs", KT)
            with nc.Block() as block:
                @block.tensor
                def _(pe):
                    if center:
                        for k in tiles:
                            last = pe.matmul(ps[:, 6, :], self.con("mean"), src[:, k, :], start=(k == 0), stop=(k == KT - 1))
                        last.then_inc(*pe_m.did("mean"))
                    for k in tiles:
                        pe.wait_ge(act_m.sem, act_m.at(f"q{k}"))
                        last = pe.matmul(ps[:, 7, :], self.con("mean"), SQ[:, k, :], start=(k == 0), stop=(k == KT - 1))
                    last.then_inc(*pe_m.did("var"))

                @block.scalar
                def _(act):
                    for k in tiles:
                        if center:
                            act.wait_ge(dve_m.sem, dve_m.at(f"c{k}"))
                        S.activation(SQ[:, k, :], src[:, k, :], ACT.Square).then_inc(*act_m.did(f"q{k}"))
                    act.wait_ge(pe_m.sem, pe_m.at("var"))
                    S.activation(R[:, :], ps[:, 7, :], ACT.Sqrt, bias=self.tiny[:, 0:1] if center else self.tiny[:, 2:3]).then_inc(
                        *act_m.did("root"))
                    if center:
                        for k in tiles:
                            act.wait_ge(dve_m.sem, dve_m.at(f"n{k}"))
                            S.activation(X[:, k, :], src[:, k, :], ACT.Identity, bias=beta[:, k:k + 1],
                                         scale=gamma[:, k:k + 1]).then_inc(*act_m.did(f"x{k}"))

                @block.vector
                def _(dve):
                    if center:
                        dve.wait_ge(pe_m.sem, pe_m.at("mean"))
                        for k in tiles:
                            V.tensor_tensor(src[:, k, :], src[:, k, :], ps[:, 6, :], ALU.subtract).then_inc(
                                *dve_m.did(f"c{k}"))
                    else:
                        V.tensor_tensor(gs[:, :], gamma, mod[:, layer, scale:scale + KT, 0], ALU.mult).then_inc(
                            *dve_m.did("gs"))
                    dve.wait_ge(act_m.sem, act_m.at("root"))
                    V.reciprocal(R[:, :], R[:, :]).then_inc(*dve_m.did("rec"))
                    dve.wait_ge(dve_m.sem, dve_m.at("rec"))
                    for k in tiles:
                        dst = src if center else H
                        V.tensor_tensor(dst[:, k, :], src[:, k, :], R[:, :], ALU.mult).then_inc(*dve_m.did(f"n{k}"))
                    for k in tiles:
                        if center:
                            dve.wait_ge(act_m.sem, act_m.at(f"x{k}"))
                        else:
                            dve.wait_ge(dve_m.sem, dve_m.at(f"n{k}"))
                        V.tensor_scalar(H[:, k, :], X[:, k, :] if center else H[:, k, :],
                                        mod[:, layer, scale + k, 0:1] if center else gs[:, k:k + 1],
                                        mod[:, layer, shift + k, 0:1], ALU.mult, ALU.add).then_inc(*dve_m.did(f"h{k}"))

    def rwkv_out(self):
        self.residual("wo", self.A["w_o"], 4, 2, KT, lambda k: self.B0[:, k, :], 0, 16, ALPHA, load_x=self.A["xT"])
        self.norm("ln00", self.T, self.col("lng", 0, 8), self.col("lnb", 0, 8), 0, 32, 24)

    def ffn(self):
        nc, ring, ps, H = self.nc, self.ring, self.ps, self.H
        silu_m = [self.sem(f"ffn_silu{s}") for s in range(SLOTS)]
        s_zero = self.sem("rows_zeroed")
        with ExitStack() as st:
            HID, G = self.sb(st, "hid", FT, SEQ), self.sb(st, "silu", SLOTS, SEQ)
            with nc.Block() as block:
                @block.sync
                def _(sp):
                    load_chunks(sp, ring, self.A["w_ffn13"], FT, 2 * KT * P)

                @block.gpsimd
                def _(pool):
                    with pool.Fori(0, ITEMS + 2) as i:
                        pool.dma_start(self.A["x_rows"][ds(i * P, P), :], self.A["zeros"]).then_inc(s_zero, 16)
                    with pool.Fori(NE, ITEMS) as i:
                        pool.dma_start(self.A["y_rows"][ds(i * P, P), :], self.A["zeros"]).then_inc(s_zero, 16)
                    pool.wait_ge(s_zero, 16 * (ITEMS + 2 + ITEMS - NE))

                @block.tensor
                def _(pe):
                    project(pe, ring, ps, FT, 2, KT, lambda k: H[:, k, :])

                @block.scalar
                def _(act):
                    def body(s, trip, c):
                        act.wait_ge(ring.used[s], ring.used_at(s, trip))
                        act.wait_ge(ring.drained[s], ring.drained_at(s, trip - 1))
                        nc.scalar.activation(G[:, s, :], ps[:, 2 * s, :], ACT.Silu).then_inc(silu_m[s], 1)

                    over_chunks(act, FT, body)

                @block.vector
                def _(dve):
                    def body(s, trip, c):
                        dve.wait_ge(silu_m[s], trip + 1)
                        nc.vector.tensor_tensor(HID[:, ds(c, 1), :].rearrange("p a n -> p (a n)"), G[:, s, :],
                                                ps[:, 2 * s + 1, :], ALU.mult).then_inc(ring.drained[s], 1)

                    over_chunks(dve, FT, body)
            ring.end(FT)
            self.residual("ffn2", self.A["w_ffn2"], KT, 1, FT, lambda k: HID[:, k, :], 0, 40, ALPHA)
        self.norm("ln01", self.T, self.col("lng", 8, 8), self.col("lnb", 8, 8), 1, 8, 0)

    def pool(self):
        nc, ring, ps, X, T, H = self.nc, self.ring, self.ps, self.X, self.T, self.H
        V = nc.vector
        R, WIDE = SEQ // GRID_W, GRID_W + 2 * PADW
        s_w, s_pe, s_a, s_g = (self.sem(f"pool_{q}") for q in ("w", "done", "scaled", "gate"))
        dve_m = self.marks("pool_dve", ["zero", "pad", "s2", "s4", "s8", "s16", "mean0", "mean1", "mean2", "mean3", "pooled", "gps"])
        Q = self.B0
        with ExitStack() as st:
            pads = [self.sb(st, f"pad{i}", KT, R, WIDE) for i in range(2)]
            gps = self.sb(st, "gps", KT)
            with nc.Block() as block:
                @block.sync
                def _(sp):
                    sp.dma_start(ring.buf[0][:, 0:2048], self.A["w_pool"]).then_inc(s_w, 16)

                @block.scalar
                def _(act):
                    nc.scalar.activation(T[:, :, :], X[:, :, :], ACT.Copy, scale=ALPHA).then_inc(s_a, 1)

                @block.tensor
                def _(pe):
                    pe.wait_ge(s_w, 16)
                    pe.wait_ge(dve_m.sem, dve_m.at("pooled"))
                    for g in range(4):
                        for m in range(2):
                            for k in range(2):
                                at = (g * 4 + k * 2 + m) * P
                                last = pe.matmul(ps[:, 2 * g + m, :], ring.buf[0][:, at:at + P], Q[:, 2 * g + k, :],
                                                 start=(k == 0), stop=(k == 1))
                            last.then_inc(s_pe, 1)

                @block.vector
                def _(dve):
                    def mine(name):
                        dve.wait_ge(dve_m.sem, dve_m.at(name))

                    def grid(x):
                        return x.rearrange("p k (r c) -> p k r c", c=GRID_W)

                    V.memset(pads[0][:, :, :, :], 0.0).then_inc(*dve_m.did("zero"))
                    mine("zero")
                    for k in range(KT):
                        last = V.tensor_copy(pads[0][:, k, :, PADW:PADW + GRID_W],
                                             H[:, k, :].rearrange("p (r c) -> p r c", c=GRID_W))
                    last.then_inc(*dve_m.did("pad"))
                    prev = "pad"
                    for i, (lo, back, ahead) in enumerate(((1, 1, 0), (2, 1, 1), (4, 2, 2), (8, 4, 4))):
                        a, b = pads[i % 2], pads[(i + 1) % 2]
                        hi = WIDE - ahead - (0, 1, 2, 4)[i]
                        mine(prev)
                        for k in range(2 * i, KT):
                            last = V.tensor_tensor(b[:, k, :, lo:hi], a[:, k, :, lo - back:hi - back],
                                                   a[:, k, :, lo + ahead:hi + ahead], ALU.add)
                        prev = f"s{2 ** (i + 1)}"
                        last.then_inc(*dve_m.did(prev))
                        if i == 3:
                            break
                    mine("s16")
                    for g in range(4):
                        src = pads[(g + 1) % 2]
                        for k in (2 * g, 2 * g + 1):
                            o = Q[:, k, :].rearrange("p (r c) -> p r c", c=GRID_W)
                            last = V.tensor_tensor(o, src[:, k, :, PADW:PADW + GRID_W],
                                                   self.con("rcnt", g * GRID_W, GRID_W).unsqueeze(1).broadcast_to(
                                                       [P, R, GRID_W]), ALU.mult)
                        last.then_inc(*dve_m.did(f"mean{g}"))
                    mine("mean3")
                    V.tensor_tensor(Q[:, :, :], Q[:, :, :], H[:, :, :], ALU.subtract).then_inc(*dve_m.did("pooled"))
                    V.tensor_tensor(gps[:, :], self.col("pscale", 0, 8), self.mod[:, 1, 16:24, 0], ALU.mult).then_inc(
                        *dve_m.did("gps"))
                    mine("gps")
                    dve.wait_ge(s_a, 1)
                    for m in range(KT):
                        dve.wait_ge(s_pe, m + 1)
                        V.scalar_tensor_tensor(out=T[:, m, :], in0=ps[:, m, :], scalar=gps[:, m:m + 1], in1=T[:, m, :],
                                               op0=ALU.mult, op1=ALU.add)
        self.norm("ln10", T, self.col("lng", 16, 8), self.col("lnb", 16, 8), 1, 32, 24)

    def moe(self):
        with ExitStack() as st:
            self.row_at = st.enter_context(self.nc.sbuf_tensor("sb_row_at", [P, TT, 2], I32))
            self.items = st.enter_context(self.nc.sbuf_tensor("sb_items", [P, ITEMS + 1], I32))
            self.gates = self.sb(st, "gates", TT, 2)
            self.spread()
            self.experts()
            self.collect()
        self.norm("ln11", self.T, self.col("lng", 24, 8), self.col("lnb", 24, 8), 1, 8, 0)

    def spread(self):
        nc, A, ps, H = self.nc, self.A, self.ps, self.H
        V, S = nc.vector, nc.scalar
        HT = self.T
        s_w, s_l = self.sem("router_in"), self.sem("logits")
        dve_m = self.marks("router_dve", ["lg", "gt", "eq", "eqlow", "beats", "rank", "first", "sel", "second", "max",
                                          "shift", "num", "den", "rec", "gate", "ga0", "ga1", "gb0", "gates",
                                          "pre", "cnt", "gtc", "nt", "excl", "start", "start128", "end", "total",
                                          "ge", "exp_of", "expert", "row", "ra0", "ra1", "rb0", "rb1", "rows"])
        act_m = self.marks("router_act", ["exp"])
        s_pre, s_tr, s_ht = self.sem("prefix"), self.sem("h_turned"), self.sem("h_rows")
        s_spread = self.sem("rows_spread")
        with ExitStack() as st:
            L = self.sb(st, "logit", TT, NE)
            cmp, eq = self.sb(st, "cmp", TT, NE, NE), self.sb(st, "eqs", TT, NE, NE)
            rank, E, Z, mx, first, second, sel, row, tmp = (
                self.sb(st, n, TT, NE) for n in ("rank", "rexp", "rz", "rmx", "sel1", "sel2", "sel", "rrow", "rtmp"))
            tmp2, tmp3, tmp4 = (self.sb(st, n, TT, NE) for n in ("rtmp2", "rtmp3", "rtmp4"))
            rowf = self.sb(st, "rowf", TT, 2)
            rw, rb, low = self.sb(st, "rw", KT * NE), self.sb(st, "rb", NE), self.sb(st, "low", NE * NE)
            before, steps = self.sb(st, "before", P), self.sb(st, "steps", 4 + ITEMS)
            cnt, nt, start, end = (self.sb(st, n, NE) for n in ("rcntx", "rnt", "rstart", "rend"))
            c4, c8 = self.sb(st, "c4", NE, 4), self.sb(st, "c8", NE, NE)
            ge, it = self.sb(st, "rge", ITEMS, NE), self.sb(st, "ritem", ITEMS + 1)
            with nc.Block() as block:
                @block.sync
                def _(sp):
                    sp.dma_start(rw[:, :], A["w_router"]).then_inc(s_w, 16)
                    sp.dma_start(rb[:, :], A["router_b"].broadcast_to([P, NE])).then_inc(s_w, 16)
                    sp.dma_start(low[:, :], A["tie_mask"].broadcast_to([P, NE * NE])).then_inc(s_w, 16)
                    sp.dma_start(before[:, :], A["before"]).then_inc(s_w, 16)
                    sp.dma_start(steps[:, :], A["steps"].broadcast_to([P, 4 + ITEMS])).then_inc(s_w, 16)

                @block.tensor
                def _(pe):
                    pe.wait_ge(s_w, 80)
                    for t in range(TT):
                        for k in range(KT):
                            last = pe.matmul(ps[:, 6, t * NE:(t + 1) * NE], H[:, k, t * P:(t + 1) * P],
                                             rw[:, k * NE:(k + 1) * NE], start=(k == 0), stop=(k == KT - 1))
                    last.then_inc(s_l, 1)
                    for t in range(TT):
                        for g in range(2):
                            n = 2 * t + g
                            if n >= 4:
                                pe.wait_ge(s_ht, n - 3)
                            for k in range(4):
                                last = pe.transpose(ps[:, n % 4, k * P:(k + 1) * P], H[:, 4 * g + k, t * P:(t + 1) * P],
                                                    self.con("id"))
                            last.then_inc(s_tr, 1)
                    pe.wait_ge(dve_m.sem, dve_m.at("sel"))
                    for t in range(TT):
                        for u in range(t + 1):
                            last = pe.matmul(ps[:, 7, t * NE:(t + 1) * NE], before[:, :] if u == t else self.con("ones"),
                                             sel[:, u, :], start=(u == 0), stop=(u == t))
                    for u in range(TT):
                        last = pe.matmul(ps[:, 7, TT * NE:(TT + 1) * NE], self.con("ones"), sel[:, u, :],
                                         start=(u == 0), stop=(u == TT - 1))
                    last.then_inc(s_pre, 1)

                @block.scalar
                def _(act):
                    for n in range(4):
                        act.wait_ge(s_tr, n + 1)
                        S.activation(HT[:, n, :], ps[:, n % 4, :], ACT.Copy).then_inc(s_ht, 1)
                    act.wait_ge(dve_m.sem, dve_m.at("shift"))
                    S.activation(E[:, :, :], Z[:, :, :], ACT.Exp).then_inc(*act_m.did("exp"))
                    for n in range(4, 8):
                        act.wait_ge(s_tr, n + 1)
                        S.activation(HT[:, n, :], ps[:, n % 4, :], ACT.Copy).then_inc(s_ht, 1)

                @block.vector
                def _(dve):
                    def mine(name):
                        dve.wait_ge(dve_m.sem, dve_m.at(name))

                    full = [P, TT, NE, NE]
                    dve.wait_ge(s_l, 1)
                    V.tensor_tensor(L[:, :, :], ps[:, 6, 0:TT * NE].rearrange("p (t e) -> p t e", e=NE),
                                    rb[:, :].unsqueeze(1).broadcast_to([P, TT, NE]), ALU.add).then_inc(*dve_m.did("lg"))
                    mine("lg")
                    other = L[:, :, :].unsqueeze(2).broadcast_to(full)
                    own = L[:, :, :].unsqueeze(3).broadcast_to(full)
                    V.tensor_tensor(cmp[:, :, :, :], other, own, ALU.is_gt).then_inc(*dve_m.did("gt"))
                    V.tensor_tensor(eq[:, :, :, :], other, own, ALU.is_equal).then_inc(*dve_m.did("eq"))
                    mine("eq")
                    tie = low[:, :].rearrange("p (a b) -> p a b", b=NE).unsqueeze(1).broadcast_to(full)
                    V.tensor_tensor(eq[:, :, :, :], eq[:, :, :, :], tie, ALU.mult).then_inc(*dve_m.did("eqlow"))
                    mine("eqlow")
                    V.tensor_tensor(cmp[:, :, :, :], cmp[:, :, :, :], eq[:, :, :, :], ALU.add).then_inc(*dve_m.did("beats"))
                    mine("beats")
                    V.tensor_reduce(rank[:, :, :], cmp[:, :, :, :], AX, ALU.add).then_inc(*dve_m.did("rank"))
                    mine("rank")
                    V.tensor_scalar(first[:, :, :], rank[:, :, :], 0.5, None, ALU.is_lt).then_inc(*dve_m.did("first"))
                    V.tensor_scalar(sel[:, :, :], rank[:, :, :], 1.5, None, ALU.is_lt).then_inc(*dve_m.did("sel"))
                    mine("sel")
                    V.tensor_tensor(second[:, :, :], sel[:, :, :], first[:, :, :], ALU.subtract).then_inc(
                        *dve_m.did("second"))
                    V.tensor_reduce(mx[:, :, 0:1], L[:, :, :], AX, ALU.max).then_inc(*dve_m.did("max"))
                    mine("max")
                    V.tensor_tensor(Z[:, :, :], L[:, :, :], mx[:, :, 0:1].broadcast_to([P, TT, NE]),
                                    ALU.subtract).then_inc(*dve_m.did("shift"))
                    dve.wait_ge(act_m.sem, act_m.at("exp"))
                    V.tensor_tensor(E[:, :, :], E[:, :, :], sel[:, :, :], ALU.mult).then_inc(*dve_m.did("num"))
                    mine("num")
                    V.tensor_reduce(mx[:, :, 1:2], E[:, :, :], AX, ALU.add).then_inc(*dve_m.did("den"))
                    mine("den")
                    V.reciprocal(mx[:, :, 1:2], mx[:, :, 1:2]).then_inc(*dve_m.did("rec"))
                    mine("rec")
                    V.tensor_tensor(E[:, :, :], E[:, :, :], mx[:, :, 1:2].broadcast_to([P, TT, NE]), ALU.mult).then_inc(
                        *dve_m.did("gate"))
                    mine("gate")
                    V.tensor_tensor(tmp[:, :, :], E[:, :, :], first[:, :, :], ALU.mult).then_inc(*dve_m.did("ga0"))
                    V.tensor_tensor(tmp2[:, :, :], E[:, :, :], second[:, :, :], ALU.mult).then_inc(*dve_m.did("ga1"))
                    mine("ga1")
                    V.tensor_reduce(self.gates[:, :, 0:1], tmp[:, :, :], AX, ALU.add).then_inc(*dve_m.did("gb0"))
                    V.tensor_reduce(self.gates[:, :, 1:2], tmp2[:, :, :], AX, ALU.add).then_inc(*dve_m.did("gates"))
                    dve.wait_ge(s_pre, 1)
                    V.tensor_copy(row[:, :, :], ps[:, 7, 0:TT * NE].rearrange("p (t e) -> p t e", e=NE)).then_inc(
                        *dve_m.did("pre"))
                    V.tensor_copy(cnt[:, :], ps[:, 7, TT * NE:(TT + 1) * NE]).then_inc(*dve_m.did("cnt"))
                    mine("cnt")
                    V.tensor_tensor(c4[:, :, :], cnt[:, :].unsqueeze(2).broadcast_to([P, NE, 4]),
                                    steps[:, 0:4].unsqueeze(1).broadcast_to([P, NE, 4]), ALU.is_gt).then_inc(
                        *dve_m.did("gtc"))
                    mine("gtc")
                    V.tensor_reduce(nt[:, :], c4[:, :, :], AX, ALU.add).then_inc(*dve_m.did("nt"))
                    mine("nt")
                    V.tensor_tensor(c8[:, :, :], nt[:, :].unsqueeze(1).broadcast_to([P, NE, NE]),
                                    low[:, :].rearrange("p (a b) -> p a b", b=NE), ALU.mult).then_inc(*dve_m.did("excl"))
                    mine("excl")
                    V.tensor_reduce(start[:, :], c8[:, :, :], AX, ALU.add).then_inc(*dve_m.did("start"))
                    mine("start")
                    V.tensor_scalar(cnt[:, :], start[:, :], float(P), None, ALU.mult).then_inc(*dve_m.did("start128"))
                    V.tensor_tensor(end[:, :], start[:, :], nt[:, :], ALU.add).then_inc(*dve_m.did("end"))
                    V.tensor_reduce(it[:, ITEMS:ITEMS + 1], nt[:, :], AX, ALU.add).then_inc(*dve_m.did("total"))
                    mine("end")
                    V.tensor_tensor(ge[:, :, :], steps[:, 4:4 + ITEMS].unsqueeze(2).broadcast_to([P, ITEMS, NE]),
                                    end[:, :].unsqueeze(1).broadcast_to([P, ITEMS, NE]), ALU.is_ge).then_inc(
                        *dve_m.did("ge"))
                    mine("ge")
                    V.tensor_reduce(it[:, 0:ITEMS], ge[:, :, :], AX, ALU.add).then_inc(*dve_m.did("exp_of"))
                    mine("exp_of")
                    V.tensor_copy(self.items[:, :], it[:, :]).then_inc(*dve_m.did("expert"))
                    mine("start128")
                    V.tensor_tensor(row[:, :, :], row[:, :, :], cnt[:, :].unsqueeze(1).broadcast_to([P, TT, NE]),
                                    ALU.add).then_inc(*dve_m.did("row"))
                    mine("row")
                    V.tensor_tensor(tmp3[:, :, :], row[:, :, :], first[:, :, :], ALU.mult).then_inc(*dve_m.did("ra0"))
                    V.tensor_tensor(tmp4[:, :, :], row[:, :, :], second[:, :, :], ALU.mult).then_inc(*dve_m.did("ra1"))
                    mine("ra1")
                    V.tensor_reduce(rowf[:, :, 0:1], tmp3[:, :, :], AX, ALU.add).then_inc(*dve_m.did("rb0"))
                    V.tensor_reduce(rowf[:, :, 1:2], tmp4[:, :, :], AX, ALU.add).then_inc(*dve_m.did("rb1"))
                    mine("rb1")
                    V.tensor_copy(self.row_at[:, :, :], rowf[:, :, :]).then_inc(*dve_m.did("rows"))

                @block.gpsimd
                def _(pool):
                    pool.wait_ge(dve_m.sem, dve_m.at("rows"))
                    pool.wait_ge(s_ht, 8)
                    for t in range(TT):
                        for c in range(2):
                            nc.gpsimd.indirect_dma_start(
                                A["x_rows"], IndirectOffsetOnAxis(ap=self.row_at[:, t, c:c + 1], axis=0),
                                self.token_rows(HT, t), None).then_inc(s_spread, 16)
                    pool.wait_ge(s_spread, 16 * 2 * TT)

    def token_rows(self, buf, t):
        return buf[:, 2 * t:2 * t + 2, :].rearrange("p a n -> p (a n)")

    def experts(self):
        nc, A, ring, ps = self.nc, self.A, self.ring, self.ps
        V, S = nc.vector, nc.scalar
        UP, DOWN = FE // HCOL, D // YCOL
        ROUND = UP + DOWN
        assert ROUND % SLOTS == 0 and KT * 2 * HCOL == SLOT and ET * YCOL == SLOT
        HTB = (3, 4, 5)
        XB = (2, 7)
        YB = (6, 7)
        loaded = [self.sem(f"moe_w_loaded{s}") for s in range(SLOTS)]
        s_x, s_y = self.sem("moe_x_in"), self.sem("moe_y_out")
        def trip_marks(name, names):
            return self.marks(name, names, len(names))

        pe_m = trip_marks("moe_pe", [f"up{c}" for c in range(UP)] + ["x0", "x1", "t0", "t1", "t2"]
                          + [f"down{j}" for j in range(DOWN)])
        act_m = trip_marks("moe_act", [f"silu{c}" for c in range(UP)] + ["t0", "t1", "t2"] + [f"y{j}" for j in range(DOWN)])
        dve_m = trip_marks("moe_dve", [f"hid{c}" for c in range(UP)] + ["x0", "x1"])
        pool_m = trip_marks("moe_pool", ["y_written"])
        s_first, s_first_t = self.sem("moe_first_turned"), self.sem("moe_first_copied")
        mark_of = [f"up{c}" if c < UP else f"down{c - UP}" for c in range(ROUND)]
        with ExitStack() as st:
            XI, XG = self.sb(st, "x_in", D), self.sb(st, "x_feat", KT, P)
            G, HR = self.sb(st, "esilu", 2, HCOL), self.sb(st, "hid_rows", FE)
            HF, YO = self.sb(st, "hid_feat", 12, P), self.sb(st, "y_rows_out", D)
            with nc.Block() as block:
                def count(eng):
                    return eng.value_load(self.items[0:1, ITEMS:ITEMS + 1], min_val=NE, max_val=ITEMS)

                @block.sync
                def _(sp):
                    n = count(sp)
                    with sp.Fori(0, n) as i:
                        e = sp.value_load(self.items[0:1, ds(i, 1)], min_val=0, max_val=NE - 1)
                        for c in range(ROUND):
                            s = c % SLOTS
                            if c < SLOTS:
                                sp.wait_ge(pe_m.sem, pe_m.at(mark_of[ROUND + c - SLOTS], i - 1))
                            else:
                                sp.wait_ge(pe_m.sem, pe_m.at(mark_of[c - SLOTS], i))
                            src = (A["w_moe_up"][ds(e * UP + c, 1)] if c < UP else
                                   A["w_moe_down"][ds(e * DOWN + (c - UP), 1)])
                            sp.dma_start(ring.buf[s], src.rearrange("a p n -> (a p) n")).then_inc(loaded[s], 16)

                @block.tensor
                def _(pe):
                    def turn_x(half):
                        for k in range(4):
                            at = (4 * half + k) * P
                            last = pe.transpose(ps[:, XB[half], k * P:(k + 1) * P], XI[:, at:at + P], self.con("id"))
                        return last

                    n = count(pe)
                    pe.wait_ge(s_x, 16)
                    for half in range(2):
                        turn_x(half).then_inc(s_first, 1)
                    pe.wait_ge(s_first_t, 2)
                    with pe.Fori(0, n) as i:
                        for c in range(ROUND):
                            s = c % SLOTS
                            pe.wait_ge(loaded[s], (i * (ROUND // SLOTS) + (c // SLOTS + 1)) * 16)
                            if c == 0:
                                pe.wait_ge(dve_m.sem, dve_m.at("x1", i - 1))
                            if c < UP:
                                if c < 2:
                                    pe.wait_ge(dve_m.sem, dve_m.at(f"hid{UP - 2 + c}", i - 1))
                                else:
                                    pe.wait_ge(dve_m.sem, dve_m.at(f"hid{c - 2}", i))
                                for k in range(KT):
                                    last = pe.matmul(ps[:, c % 2, 0:2 * HCOL], XG[:, k, :],
                                                     ring.buf[s][:, k * 2 * HCOL:(k + 1) * 2 * HCOL],
                                                     start=(k == 0), stop=(k == KT - 1))
                                last.then_inc(*pe_m.did(f"up{c}"))
                            else:
                                j = c - UP
                                if j == 0:
                                    pe.wait_ge(s_x, i * 16 + 32)
                                    pe.wait_ge(act_m.sem, act_m.at(f"y{DOWN - 1}", i - 1))
                                    for half in range(2):
                                        turn_x(half).then_inc(*pe_m.did(f"x{half}"))
                                    for b in range(3):
                                        pe.wait_ge(dve_m.sem, dve_m.at(f"hid{min(UP - 1, ((4 * b + 4) * P - 1) // HCOL)}", i))
                                        for k in range(4 * b, min(4 * b + 4, ET)):
                                            last = pe.transpose(ps[:, HTB[b], (k % 4) * P:(k % 4 + 1) * P],
                                                                HR[:, k * P:(k + 1) * P], self.con("id"))
                                        last.then_inc(*pe_m.did(f"t{b}"))
                                if j == 1:
                                    pe.wait_ge(dve_m.sem, dve_m.at("x1", i))
                                if j < 2:
                                    pe.wait_ge(act_m.sem, act_m.at(f"y{DOWN - 2 + j}", i - 1))
                                else:
                                    pe.wait_ge(act_m.sem, act_m.at(f"y{j - 2}", i))
                                for k in range(ET):
                                    if j == 0 and k % 4 == 0:
                                        pe.wait_ge(act_m.sem, act_m.at(f"t{k // 4}", i))
                                    last = pe.matmul(ps[:, YB[j % 2], 0:YCOL], HF[:, k, :],
                                                     ring.buf[s][:, k * YCOL:(k + 1) * YCOL],
                                                     start=(k == 0), stop=(k == ET - 1))
                                last.then_inc(*pe_m.did(f"down{j}"))

                @block.scalar
                def _(act):
                    n = count(act)
                    with act.Fori(0, n) as i:
                        for c in range(UP):
                            act.wait_ge(pe_m.sem, pe_m.at(f"up{c}", i))
                            S.activation(G[:, c % 2, :], ps[:, c % 2, 0:HCOL], ACT.Silu).then_inc(*act_m.did(f"silu{c}"))
                        for b in range(3):
                            act.wait_ge(pe_m.sem, pe_m.at(f"t{b}", i))
                            w = min(4, ET - 4 * b)
                            S.activation(HF[:, 4 * b:4 * b + w, :], ps[:, HTB[b], 0:w * P].rearrange(
                                "p (k n) -> p k n", n=P), ACT.Copy).then_inc(*act_m.did(f"t{b}"))
                        act.wait_ge(pool_m.sem, pool_m.at("y_written", i - 1))
                        for j in range(DOWN):
                            act.wait_ge(pe_m.sem, pe_m.at(f"down{j}", i))
                            S.activation(YO[:, j * YCOL:(j + 1) * YCOL], ps[:, YB[j % 2], 0:YCOL],
                                         ACT.Copy).then_inc(*act_m.did(f"y{j}"))

                @block.vector
                def _(dve):
                    def copy_x(half):
                        return V.tensor_copy(XG[:, 4 * half:4 * half + 4, :],
                                             ps[:, XB[half], :].rearrange("p (k n) -> p k n", n=P))

                    n = count(dve)
                    for half in range(2):
                        dve.wait_ge(s_first, half + 1)
                        copy_x(half).then_inc(s_first_t, 1)
                    with dve.Fori(0, n) as i:
                        for c in range(UP):
                            dve.wait_ge(act_m.sem, act_m.at(f"silu{c}", i))
                            V.tensor_tensor(HR[:, c * HCOL:(c + 1) * HCOL], G[:, c % 2, :], ps[:, c % 2, HCOL:2 * HCOL],
                                            ALU.mult).then_inc(*dve_m.did(f"hid{c}"))
                        for half in range(2):
                            dve.wait_ge(pe_m.sem, pe_m.at(f"x{half}", i))
                            copy_x(half).then_inc(*dve_m.did(f"x{half}"))

                @block.gpsimd
                def _(pool):
                    for m in (pe_m, act_m, dve_m, pool_m):
                        m.begin(pool)
                    n = count(pool)
                    pool.dma_start(XI[:, :], A["x_rows"][0:P, :]).then_inc(s_x, 16)
                    pool.wait_ge(s_first, 2)
                    pool.dma_start(XI[:, :], A["x_rows"][P:2 * P, :]).then_inc(s_x, 16)
                    with pool.Fori(0, n) as i:
                        pool.wait_ge(pe_m.sem, pe_m.at("x1", i))
                        pool.dma_start(XI[:, :], A["x_rows"][ds((i + 2) * P, P), :]).then_inc(s_x, 16)
                        pool.wait_ge(act_m.sem, act_m.at(f"y{DOWN - 1}", i))
                        pool.dma_start(A["y_rows"][ds(i * P, P), :], YO[:, :]).then_inc(s_y, 16)
                        pool.wait_ge(s_x, i * 16 + 48)
                        pool.wait_ge(s_y, i * 16 + 16)
                        pool.sem_inc(*pool_m.did("y_written"))

    def collect(self):
        nc, A, ps, T, X = self.nc, self.A, self.ps, self.T, self.X
        V, S = nc.vector, nc.scalar
        YA, YB = self.B0, self.H
        s_in = [self.sem(f"moe_back{t}") for t in range(TT)]
        s_t, s_pe = self.sem("moe_T"), self.sem("moe_turned")
        dve_m = self.marks("collect_dve", [f"{q}{t}" for t in range(TT) for q in ("a", "b")])
        with nc.Block() as block:
            @block.gpsimd
            def _(pool):
                for t in range(TT):
                    for c, buf in enumerate((YA, YB)):
                        nc.gpsimd.indirect_dma_start(
                            self.token_rows(buf, t), None, A["y_rows"],
                            IndirectOffsetOnAxis(ap=self.row_at[:, t, c:c + 1], axis=0)).then_inc(s_in[t], 16)

            @block.scalar
            def _(act):
                S.activation(T[:, :, :], X[:, :, :], ACT.Copy, scale=ALPHA).then_inc(s_t, 1)

            @block.tensor
            def _(pe):
                for t in range(TT):
                    pe.wait_ge(dve_m.sem, dve_m.at(f"b{t}"))
                    for m in range(KT):
                        last = pe.transpose(ps[:, m, t * P:(t + 1) * P], YA[:, 2 * t + m // 4, (m % 4) * P:(m % 4 + 1) * P],
                                            self.con("id"))
                        if t == TT - 1:
                            last.then_inc(s_pe, 1)

            @block.vector
            def _(dve):
                for t in range(TT):
                    ya, yb = self.token_rows(YA, t), self.token_rows(YB, t)
                    dve.wait_ge(s_in[t], 32)
                    V.tensor_scalar(ya, ya, self.gates[:, t, 0:1], None, ALU.mult).then_inc(*dve_m.did(f"a{t}"))
                    dve.wait_ge(dve_m.sem, dve_m.at(f"a{t}"))
                    V.scalar_tensor_tensor(out=ya, in0=yb, scalar=self.gates[:, t, 1:2], in1=ya,
                                           op0=ALU.mult, op1=ALU.add).then_inc(*dve_m.did(f"b{t}"))
                dve.wait_ge(s_t, 1)
                for m in range(KT):
                    dve.wait_ge(s_pe, m + 1)
                    V.scalar_tensor_tensor(out=T[:, m, :], in0=ps[:, m, :], scalar=self.mod[:, 1, 40 + m, 0:1],
                                           in1=T[:, m, :], op0=ALU.mult, op1=ALU.add)

    def attention(self):
        nc, A, ring, ps, X, T, H, mod = self.nc, self.A, self.ring, self.ps, self.X, self.T, self.H, self.mod
        V, S = nc.vector, nc.scalar
        self.norm("rms1", X, self.col("n1g", 0, 8), None, 2, 8, 0, center=False)
        with ExitStack() as st:
            QK = self.sb(st, "qk", 16, SEQ)
            VV = self.sb(st, "vv", 2, TT, BANK)
            lam = self.sb(st, "lamv", 8)
            self.qkv(QK, VV, lam)
            O = self.B0
            self.heads(QK, VV, lam, O)
        self.residual("wout", A["w_out"], 4, 2, KT, lambda k: self.B0[:, k, :], 2, 16, 1.0)
        self.move_t_to_x("h1")

    def move_t_to_x(self, name):
        s = self.sem(name + "_moved")
        with self.nc.Block() as block:
            @block.scalar
            def _(act):
                self.nc.scalar.activation(self.X[:, :, :], self.T[:, :, :], ACT.Copy).then_inc(s, 1)

    def qkv(self, QK, VV, lam):
        nc, A, ring, ps, H = self.nc, self.A, self.ring, self.ps, self.H
        V, S = nc.vector, nc.scalar
        NV = 4
        s_v, s_vo, s_sq, s_var, s_root, s_rec = (self.sem(f"qkv_{q}") for q in ("v", "vout", "sq", "var", "root", "rec"))
        s_n, s_nn = self.sem("qk_copied"), self.sem("qk_normed")
        lam_d, lam_p, lam_a = self.marks("lam_dve", ["prod", "sub", "lam"]), self.sem("lam_pe"), self.sem("lam_act")
        s_b = [self.sem(f"bias_{q}") for q in ("in", "pe", "act", "out")]
        with ExitStack() as st:
            SQ, R = self.sb(st, "qk_sq", 2, SEQ), self.sb(st, "qk_r", 2, SEQ)
            tab, oh, row = self.sb(st, "tab", 12), self.sb(st, "onehot", 1024), self.sb(st, "biasrow", 1024)
            with nc.Block() as block:
                @block.sync
                def _(sp):
                    sp.dma_start(tab[0:33, :], A["bias_table"]).then_inc(s_b[0], 16)
                    sp.dma_start(oh[0:33, :], A["bucket_onehot"]).then_inc(s_b[0], 16)
                    load_chunks(sp, ring, A["w_qk"], 8, 2 * KT * P)
                    sp.wait_ge(s_b[2], 2)
                    sp.dma_start(A["bias_rows"], row[0:12, :]).then_inc(s_b[3], 16)
                    sp.wait_ge(s_b[3], 16)

                @block.tensor
                def _(pe):
                    pe.wait_ge(s_b[0], 32)
                    for b in range(2):
                        last = pe.matmul(ps[0:12, 6 + b, :], tab[0:33, :], oh[0:33, b * BANK:(b + 1) * BANK],
                                         start=True, stop=True)
                    last.then_inc(s_b[1], 1)
                    pe.wait_ge(lam_d.sem, lam_d.at("prod"))
                    pe.wait_ge(s_b[2], 2)
                    pe.matmul(ps[:, 6, 0:2], self.con("ones"), lam[:, 0:2], start=True, stop=True).then_inc(lam_p, 1)
                    project(pe, ring, ps, 8, 2, KT, lambda k: H[:, k, :])

                @block.scalar
                def _(act):
                    act.wait_ge(s_b[1], 1)
                    for b in range(2):
                        S.activation(row[0:12, b * BANK:(b + 1) * BANK], ps[0:12, 6 + b, :], ACT.Copy).then_inc(s_b[2], 1)
                    act.wait_ge(lam_p, 1)
                    S.activation(lam[:, 2:4], ps[:, 6, 0:2], ACT.Exp).then_inc(lam_a, 1)

                    def body(s, trip, c):
                        act.wait_ge(ring.used[s], ring.used_at(s, trip))
                        S.activation(QK[:, ds(2 * c, 2), :], ps[:, 2 * s:2 * s + 2, :], ACT.Copy).then_inc(ring.drained[s], 1)

                    over_chunks(act, 8, body)

                @block.vector
                def _(dve):
                    V.tensor_tensor(lam[:, 0:2], self.col("lam", 0, 4).rearrange("p (a b) -> p a b", b=2)[:, :, 0],
                                    self.col("lam", 0, 4).rearrange("p (a b) -> p a b", b=2)[:, :, 1],
                                    ALU.mult).then_inc(*lam_d.did("prod"))
                    dve.wait_ge(lam_a, 1)
                    V.tensor_tensor(lam[:, 4:5], lam[:, 2:3], lam[:, 3:4], ALU.subtract).then_inc(*lam_d.did("sub"))
                    dve.wait_ge(lam_d.sem, lam_d.at("sub"))
                    V.tensor_scalar(lam[:, 5:6], lam[:, 4:5], LAMBDA_INIT, None, ALU.add).then_inc(*lam_d.did("lam"))
            ring.end(8)
            with nc.Block() as block:
                @block.sync
                def _(sp):
                    load_chunks(sp, ring, A["w_v"], NV, 4 * BANK)

                @block.tensor
                def _(pe):
                    for c in range(NV):
                        s, kind, half = c % SLOTS, c // 2, c % 2
                        pe.wait_ge(ring.loaded[s], (ring.fills[s] + c // SLOTS + 1) * 16)
                        if c == 2:
                            pe.wait_ge(s_vo, 1)
                        for t in range(TT):
                            for k in range(4):
                                last = pe.matmul(ps[:, t, :], H[:, 4 * half + k, t * P:(t + 1) * P],
                                                 ring.buf[s][:, k * BANK:(k + 1) * BANK],
                                                 start=(half == 0 and k == 0), stop=(half == 1 and k == 3))
                        last.then_inc(ring.used[s], 1)
                    with pe.Fori(0, 16) as i:
                        pe.wait_ge(s_sq, i + 1)
                        pe.wait_ge(s_root, i + 1)
                        pe.matmul(ps[:, 7, :], self.con("hmean"), SQ[:, 0, :], start=True, stop=True).then_inc(s_var, 1)

                @block.scalar
                def _(act):
                    for kind in range(2):
                        s = (2 * kind + 1) % SLOTS
                        act.wait_ge(ring.used[s], ring.used_at(s, (2 * kind + 1) // SLOTS))
                        S.activation(VV[:, kind, :, :], ps[:, 0:TT, :], ACT.Copy).then_inc(s_vo, 1)
                    with act.Fori(0, 16) as i:
                        act.wait_ge(s_var, i + 1)
                        S.activation(SQ[:, 0, :], QK[:, ds(i, 1), :].rearrange("p a n -> p (a n)"), ACT.Square).then_inc(
                            s_sq, 1)
                        act.wait_ge(s_var, i + 2)
                        act.wait_ge(s_nn, i + 1)
                        S.activation(R[:, 0, :], ps[:, 7, :], ACT.Sqrt, bias=self.tiny[:, 2:3]).then_inc(s_root, 1)

                @block.gpsimd
                def _(pool):
                    for q in (s_root, s_var, s_nn):
                        pool.sem_inc(q, 1)

                @block.vector
                def _(dve):
                    with dve.Fori(0, 16) as i:
                        dve.wait_ge(s_root, i + 2)
                        V.reciprocal(R[:, 0, :], R[:, 0, :]).then_inc(s_rec, 1)
                        dve.wait_ge(s_rec, i + 1)
                        x = QK[:, ds(i, 1), :].rearrange("p a n -> p (a n)")
                        V.tensor_tensor(x, x, R[:, 0, :], ALU.mult).then_inc(s_nn, 1)
                    dve.wait_ge(s_nn, 17)
                    for i, name in enumerate(("qna", "kna", "qnb", "knb")):
                        V.tensor_scalar(QK[:, 4 * i:4 * i + 4, :], QK[:, 4 * i:4 * i + 4, :], self.col(name), None, ALU.mult)
            ring.end(NV, 0)

    def heads(self, QK, VV, lam, O):
        nc, A, ps = self.nc, self.A, self.ps
        V, S = nc.vector, nc.scalar
        GW = SEQ + (TT - 1) * P
        units = [(0, h, q) for h in range(2) for q in range(TT)] + [(1, h, q) for q in range(TT) for h in range(2)]
        turns = [i for i, u in enumerate(units) if u[0] == 0 or u[1] == 1]
        U, NTURN = len(units), len(turns)
        U_ = range(U)
        pe_m = self.marks("at_pe", [x for i in range(U + 1) for x in
                                    ([f"s{i}"] if i < U else []) + ([f"t{i - 1}"] if i - 1 in turns else [])
                                    + ([f"pv{0 if i - 1 == 7 else 1}"] if i - 1 in (7, 15) else [])] + ["sub"], 1)
        act_m = self.marks("at_act", [x for i in range(U + 1) for x in
                                      ([f"e{i}"] if i < U else []) + ([f"p{i - 1}"] if i - 1 in turns else [])]
                           + ["oa", "ob", "sq", "root"])
        dve_m = self.marks("at_dve", [x for i in range(U + 1) for x in
                                      ([f"b{i}", f"m{i}"] if i < U else [])
                                      + ([f"r{i - 1}"] + ([f"l{i - 1}"] if units[i - 1][:2] == (1, 1) else [])
                                         + [f"n{i - 1}"] if i >= 1 else [])] + ["rec", "obn", "obg"], 1)
        pool_m = self.marks("at_pool", ["copied"])
        s_half = self.sem("queries_copied")
        s_g, s_z = self.sem("bias_loaded"), self.sem("heads_zero")
        with ExitStack() as st:
            Qz, Ks, Vz = self.sb(st, "qz", 4, SEQ), self.sb(st, "ks", 2, SEQ), self.sb(st, "vz", 3, TT, P)
            GT = self.sb(st, "gt", 3, GW)
            PR = self.sb(st, "pr", 4, SEQ)
            PT, SC = self.H[:, 0:TT, :], self.H[:, TT:TT + 2, :]
            stat = self.sb(st, "stat", U, 4)
            ON, R = self.sb(st, "on", 2, SEQ), self.sb(st, "on_r", SEQ)
            with nc.Block() as block:
                @block.sync
                def _(sp):
                    with sp.Fori(0, 4) as t:
                        sp.wait_ge(dve_m.sem, dve_m.trips(t))
                        for i in range(3):
                            hd = 2 * t + i if i < 2 else t + 8
                            sp.dma_start(GT[:, i, :], self.toeplitz(hd, GW)).then_inc(s_g, 16)

                @block.gpsimd
                def _(pool):
                    G = nc.gpsimd
                    pe_m.begin(pool)
                    dve_m.begin(pool)
                    G.memset(Qz[:, :, :], 0.0).then_inc(s_z, 1)
                    G.memset(Vz[:, :, :, :], 0.0).then_inc(s_z, 1)
                    pool.wait_ge(s_z, 2)
                    with pool.Fori(0, 4) as t:
                        pool.wait_ge(pe_m.sem, pe_m.trips(t))
                        for kind in range(2):
                            for h in range(2):
                                r = slice(64 * h, 64 * h + 64)
                                G.tensor_copy(Qz[r, 2 * kind + h, ::-1], QK[r, ds(8 * kind + t, 1), :].rearrange(
                                    "p a n -> p (a n)")).then_inc(s_half, 1)
                        pool.wait_ge(s_half, 4 * t + 4)
                        for kind in range(2):
                            G.tensor_copy(Ks[:, kind, :], QK[:, ds(8 * kind + 4 + t, 1), :].rearrange("p a n -> p (a n)"))
                        for h in range(2):
                            G.tensor_copy(Vz[:, h, :, 64 * h:64 * h + 64], VV[:, 0, :, ds(t * P + 64 * h, 64)])
                        G.tensor_copy(Vz[:, 2, :, :], VV[:, 1, :, ds(t * P, P)]).then_inc(*pool_m.did("copied"))
                        pool.wait_ge(pool_m.sem, t + 1)

                @block.tensor
                def _(pe):
                    with pe.Fori(0, 4) as t:
                        pe.wait_ge(pool_m.sem, t + 1)
                        for i in range(U + 1):
                            if i < U:
                                kind, h, q = units[i]
                                if i >= 2:
                                    pe.wait_ge(dve_m.sem, dve_m.at(f"b{i - 2}", t))
                                else:
                                    pe.wait_ge(dve_m.sem, dve_m.trips(t))
                                pe.matmul(ps[:, i % 2, :], Qz[:, 2 * kind + h, q * P:(q + 1) * P], Ks[:, kind, :],
                                          start=True, stop=True).then_inc(*pe_m.did(f"s{i}"))
                            if i - 1 in turns:
                                n = turns.index(i - 1)
                                pe.wait_ge(dve_m.sem, dve_m.at(f"n{i - 1}", t))
                                if n >= 2:
                                    pe.wait_ge(act_m.sem, act_m.at(f"p{turns[n - 2]}", t))
                                for k in range(TT):
                                    last = pe.transpose(ps[:, 2 + n % 2, k * P:(k + 1) * P],
                                                        PR[:, (i - 1) % 4, k * P:(k + 1) * P], self.con("id"))
                                last.then_inc(*pe_m.did(f"t{i - 1}"))
                            if i - 1 in (3, 7, 15):
                                pe.wait_ge(act_m.sem, act_m.at(f"p{i - 1}", t))
                                bank = 4 if i - 1 < 8 else 5
                                vi = {3: 0, 7: 1, 15: 2}[i - 1]
                                for k in range(TT):
                                    last = pe.matmul(ps[:, bank, :], Vz[:, vi, k, :], PT[:, k, :],
                                                     start=(k == 0 and vi != 1), stop=(k == TT - 1 and vi != 0))
                                if vi:
                                    last.then_inc(*pe_m.did(f"pv{vi - 1}"))
                        pe.wait_ge(act_m.sem, act_m.at("sq", t))
                        pe.matmul(ps[:, 6, :], self.con("ones"), ON[:, 1, :], start=True, stop=True).then_inc(
                            *pe_m.did("sub"))

                @block.scalar
                def _(act):
                    with act.Fori(0, 4) as t:
                        for i in range(U + 1):
                            if i < U:
                                act.wait_ge(dve_m.sem, dve_m.at(f"m{i}", t))
                                S.activation(PR[:, i % 4, :], SC[:, i % 2, :], ACT.Exp, bias=stat[:, i, 0:1],
                                             accum_out=stat[:, i, 1:2]).then_inc(*act_m.did(f"e{i}"))
                            if i - 1 in turns:
                                q = units[i - 1][2]
                                act.wait_ge(pe_m.sem, pe_m.at(f"t{i - 1}", t))
                                n = turns.index(i - 1)
                                S.activation(PT[:, :, q * P:(q + 1) * P],
                                             ps[:, 2 + n % 2, :].rearrange("p (k c) -> p k c", k=TT),
                                             ACT.Copy).then_inc(*act_m.did(f"p{i - 1}"))
                        act.wait_ge(pe_m.sem, pe_m.at("pv0", t))
                        S.activation(O[:, ds(t, 1), :].rearrange("p a n -> p (a n)"), ps[:, 4, ::-1], ACT.Copy).then_inc(
                            *act_m.did("oa"))
                        act.wait_ge(pe_m.sem, pe_m.at("pv1", t))
                        S.activation(ON[:, 0, :], ps[:, 5, ::-1], ACT.Copy).then_inc(*act_m.did("ob"))
                        act.wait_ge(act_m.sem, act_m.at("ob", t))
                        S.activation(ON[:, 1, :], ON[:, 0, :], ACT.Square).then_inc(*act_m.did("sq"))
                        act.wait_ge(pe_m.sem, pe_m.at("sub", t))
                        S.activation(R[:, :], ps[:, 6, :], ACT.Sqrt, bias=self.tiny[:, 2:3], scale=1.0 / P).then_inc(
                            *act_m.did("root"))

                @block.vector
                def _(dve):
                    with dve.Fori(0, 4) as t:
                        dve.wait_ge(s_g, (t + 1) * 48)

                        def mine(name):
                            dve.wait_ge(dve_m.sem, dve_m.at(name, t))

                        for i in range(U + 1):
                            if i < U:
                                kind, h, q = units[i]
                                dve.wait_ge(pe_m.sem, pe_m.at(f"s{i}", t))
                                if i >= 2:
                                    dve.wait_ge(act_m.sem, act_m.at(f"e{i - 2}", t))
                                lo = q * P
                                gi = h if kind == 0 else 2
                                V.scalar_tensor_tensor(out=SC[:, i % 2, :], in0=ps[:, i % 2, :], scalar=0.125,
                                                       in1=GT[:, gi, lo:lo + SEQ], op0=ALU.mult, op1=ALU.add).then_inc(
                                    *dve_m.did(f"b{i}"))
                                mine(f"b{i}")
                                V.tensor_reduce(stat[:, i, 0:1], SC[:, i % 2, :], AX, ALU.max, negate=True).then_inc(
                                    *dve_m.did(f"m{i}"))
                            if i >= 1:
                                u = i - 1
                                kind, h, q = units[u]
                                dve.wait_ge(act_m.sem, act_m.at(f"e{u}", t))
                                V.reciprocal(stat[:, u, 2:3], stat[:, u, 1:2]).then_inc(*dve_m.did(f"r{u}"))
                                mine(f"r{u}")
                                if kind == 0 or h == 0:
                                    V.tensor_scalar(PR[:, u % 4, :], PR[:, u % 4, :], stat[:, u, 2:3], None,
                                                    ALU.mult).then_inc(*dve_m.did(f"n{u}"))
                                else:
                                    V.tensor_tensor(stat[:, u, 3:4], stat[:, u, 2:3], lam[:, 5:6], ALU.mult).then_inc(
                                        *dve_m.did(f"l{u}"))
                                    mine(f"l{u}")
                                    V.tensor_scalar(PR[:, u % 4, :], PR[:, u % 4, :], stat[:, u, 3:4], None, ALU.mult)
                                    dve.drain()
                                    V.tensor_tensor(PR[:, u % 4, :], PR[:, (u - 1) % 4, :], PR[:, u % 4, :],
                                                    ALU.subtract).then_inc(*dve_m.did(f"n{u}"))
                        dve.wait_ge(act_m.sem, act_m.at("root", t))
                        V.reciprocal(R[:, :], R[:, :]).then_inc(*dve_m.did("rec"))
                        mine("rec")
                        V.tensor_tensor(ON[:, 0, :], ON[:, 0, :], R[:, :], ALU.mult).then_inc(*dve_m.did("obn"))
                        mine("obn")
                        V.tensor_scalar(O[:, ds(t + 4, 1), :].rearrange("p a n -> p (a n)"), ON[:, 0, :], self.col("sub"),
                                        1.0 - LAMBDA_INIT, ALU.mult, ALU.mult).then_inc(*dve_m.did("obg"))

    def toeplitz(self, head, width):
        a = self.A["bias_rows"]
        x = a[ds(head, 1), 0:1]
        return AP(x.tensor, x.offset, [(1, P), (1, width)])

    def convffn(self):
        nc, A, ring, ps, X, T, H = self.nc, self.A, self.ring, self.ps, self.X, self.T, self.H
        V, S = nc.vector, nc.scalar
        self.norm("rms2", X, self.col("n2g", 0, 8), None, 2, 32, 24, center=False)
        W = 2 * KT * P + 8
        up = [self.sem(f"up{s}") for s in range(SLOTS)]
        cv = [self.sem(f"conv{s}") for s in range(SLOTS)]
        hid = [self.sem(f"conv_hid{s}") for s in range(SLOTS)]
        sl = [self.sem(f"conv_silu{s}") for s in range(SLOTS)]
        s_z = self.sem("conv_zero")
        with ExitStack() as st:
            HID = self.sb(st, "chid", FT, SEQ)
            UP = self.sb(st, "up", SLOTS, 2, SEQ + 2)
            CV, PC = self.sb(st, "cv", SLOTS, 2, SEQ), self.sb(st, "convw", FT, 8)
            s_pc = self.sem("convw_in")
            with nc.Block() as block:
                @block.sync
                def _(sp):
                    sp.dma_start(PC[:, :, :], A["conv_cols"]).then_inc(s_pc, 16)
                    load_chunks(sp, ring, A["w_up"], FT, 2 * KT * P)

                @block.tensor
                def _(pe):
                    project(pe, ring, ps, FT, 2, KT, lambda k: H[:, k, :])

                @block.gpsimd
                def _(pool):
                    for q in (*cv, *hid):
                        pool.sem_inc(q, 1)
                    nc.gpsimd.memset(UP[:, :, :, :], 0.0).then_inc(s_z, 1)

                @block.scalar
                def _(act):
                    act.wait_ge(s_z, 1)

                    def body(s, trip, c):
                        act.wait_ge(ring.used[s], ring.used_at(s, trip))
                        act.wait_ge(cv[s], trip * 6 + 1)
                        S.activation(UP[:, s, :, 1:SEQ + 1], ps[:, 2 * s:2 * s + 2, :], ACT.Copy).then_inc(
                            ring.drained[s], 1)
                        act.wait_ge(cv[s], trip * 6 + 7)
                        S.activation(CV[:, s, 1, :], CV[:, s, 1, :], ACT.Silu).then_inc(sl[s], 1)

                    over_chunks(act, FT, body)

                @block.vector
                def _(dve):
                    dve.wait_ge(s_pc, 16)
                    def body(s, trip, c):
                        dve.wait_ge(ring.drained[s], ring.drained_at(s, trip))
                        dve.wait_ge(hid[s], trip + 1)

                        def w(i):
                            return PC[:, ds(c, 1), i:i + 1].rearrange("p a b -> p (a b)")

                        for m in range(2):
                            V.tensor_scalar(CV[:, s, m, :], UP[:, s, m, 1:SEQ + 1], w(4 * m + 1), w(4 * m + 3), ALU.mult,
                                            ALU.add).then_inc(cv[s], 1)
                        for n, tap in enumerate((0, 2)):
                            dve.wait_ge(cv[s], trip * 6 + 2 * n + 3)
                            for m in range(2):
                                V.scalar_tensor_tensor(out=CV[:, s, m, :], in0=UP[:, s, m, tap:tap + SEQ], scalar=w(4 * m + tap),
                                                       in1=CV[:, s, m, :], op0=ALU.mult, op1=ALU.add).then_inc(cv[s], 1)
                        dve.wait_ge(sl[s], trip + 1)
                        V.tensor_tensor(HID[:, ds(c, 1), :].rearrange("p a n -> p (a n)"), CV[:, s, 0, :], CV[:, s, 1, :],
                                        ALU.mult).then_inc(hid[s], 1)

                    over_chunks(dve, FT, body)
            ring.end(FT)
            self.residual("down", A["w_down"], KT, 1, FT, lambda k: HID[:, k, :], 2, 40, 1.0)
        s_o = self.sem("stored")
        with nc.Block() as block:
            @block.sync
            def _(sp):
                sp.dma_start(A["out"], T[:, :, :]).then_inc(s_o, 16)
                sp.wait_ge(s_o, 16)


def _blocks(w, width, dtype=np.float32):
    k, m = w.shape
    return np.ascontiguousarray(w.reshape(k // P, P, m // width, width).transpose(2, 1, 0, 3)).reshape(
        m // width, P, (k // P) * width)


def _cols(v):
    return np.asarray(v).reshape(-1, P).T


def _constants():
    c = np.zeros((P, NCONST), np.float32)

    def put(name, a):
        lo, hi = CONST[name]
        c[:, lo:hi] = a.reshape(P, hi - lo)

    i = np.arange(P)
    same = (i[:, None] // CH) == (i[None, :] // CH)
    put("id", np.eye(P))
    put("hsum", same.astype(np.float32))
    put("hmean", same / float(CH))
    put("ones", np.ones((P, P)))
    put("mean", np.full((P, P), 1.0 / D))
    a, b = i[:, None] % CH, i[None, :] % CH
    strict = [same & (a < b), same & (a > b)]
    incl = [same & (a <= b), same & (a >= b)]
    put("mS", np.stack([np.stack([strict[d] * 1.0, incl[d] * -1.0], 1) for d in range(2)], 1))
    put("mK", np.stack([np.stack([strict[d] * 1.0, incl[d] * 1.0], 1) for d in range(2)], 1))
    lv = []
    for m in LEVELS:
        low = same & (a // (2 * m) == b // (2 * m)) & (a % (2 * m) >= m) & (b % (2 * m) < m)
        lv.append(np.stack([low * -1.0, low.T * -1.0], 1))
    put("mL", np.stack(lv, 1))
    t = np.arange(TOK)
    put("scan", np.broadcast_to((t % CH != 0) * 1.0, (P, TOK)))
    pos = np.arange(GRID_W)
    cnt = [np.clip(pos + w // 2, 0, GRID_W) - np.clip(pos - w // 2, 0, GRID_W) for w in WINDOWS]
    put("rcnt", np.broadcast_to(1.0 / np.stack(cnt), (P, 4, GRID_W)))
    return c


def _layout(z):
    g = {k: np.asarray(v) for k, v in z.items()}
    par = np.zeros((P, NCOL), np.float32)

    def put(name, a):
        lo, hi = COLS[name]
        par[0:a.shape[0], lo:hi] = a

    put("c", np.concatenate([_cols(g["c"][0]), _cols(g["c"][0]), _cols(g["c_2"][0])], 1))
    put("cc", np.concatenate([_cols(g["c_ctx"]), _cols(g["c"][0]), _cols(g["c_2"][0])], 1))
    put("adab", np.concatenate([_cols(g["ada_b"][0]), _cols(g["ada_b"][1]), _cols(g["b_ada_2"][0])], 1))
    put("lng", _cols(g["ln_g"].reshape(-1)))
    put("lnb", _cols(g["ln_b"].reshape(-1)))
    put("mu", _cols(g["rk_mu"][0].reshape(-1)))
    pair = [g["rk_w0"][0, 0], g["rk_w0"][0, 1], g["rk_a0"][0, 0], g["rk_a0"][0, 1], g["rk_k_k"][0], g["rk_k_a"][0],
            g["rk_r_k"][0].reshape(-1), g["rk_lnx_g"][0], g["rk_lnx_b"][0]]
    put("pair", np.stack([_cols(v) for v in pair], 2).reshape(P, 72))
    put("pscale", _cols(g["pool_scale"][0]))
    put("n1g", _cols(g["norm1_g_2"][0]))
    put("n2g", _cols(g["norm2_g_2"][0]))
    for n, k in (("qna", "q_norm_a_2"), ("kna", "k_norm_a_2"), ("qnb", "q_norm_b_2"), ("knb", "k_norm_b_2")):
        put(n, np.tile(g[k][0], 2)[:, None])
    put("sub", g["subln_g_2"][0][:, None])
    put("lam", np.stack([g[k][0] for k in ("lambda_q1_2", "lambda_k1_2", "lambda_q2_2", "lambda_k2_2")], 1))

    a = {"params": par, "consts": _constants()}
    a["xT"] = np.ascontiguousarray(g["x"][0].T.reshape(KT, P, SEQ).transpose(1, 0, 2))
    a["ctxT"] = np.ascontiguousarray(g["ctx"][0].T.reshape(KT, P, CTX).transpose(1, 0, 2))
    ada = np.stack([g["ada_w"][0], g["ada_w"][1], g["w_ada_2"][0]])
    a["w_ada"] = np.ascontiguousarray(ada.reshape(3, 2, 4, P, 12, 512).transpose(0, 4, 1, 3, 2, 5)).reshape(72, P, 2048)
    w1 = np.concatenate([g["rk_w1"][0, 0], g["rk_w1"][0, 1]], 1)
    a1 = np.concatenate([g["rk_a1"][0, 0], g["rk_a1"][0, 1]], 1)
    a["w_lora1"] = np.stack([_blocks(w, P)[0] for w in (w1, a1, g["rk_g1"][0])])
    zero = np.zeros((64, D), np.float32)
    second = [np.concatenate([g["rk_w2"][0, 0], zero]), np.concatenate([zero, g["rk_w2"][0, 1]]),
              np.concatenate([g["rk_a2"][0, 0], zero]), np.concatenate([zero, g["rk_a2"][0, 1]]), g["rk_g2"][0]]
    a["w_pair"] = np.concatenate([_blocks(w, P) for w in second], 2)
    a["w_o"] = _blocks(g["rk_w_o"][0], 2 * P)

    def side(x, y):
        bx, by = _blocks(x, P), _blocks(y, P)
        n = bx.shape[0]
        return np.stack([bx.reshape(n, P, -1, P), by.reshape(n, P, -1, P)], 3).reshape(n, P, -1)

    a["w_kv"] = side(g["rk_w_rkv"][0, 1], g["rk_w_rkv"][0, 2])
    a["w_r"] = _blocks(g["rk_w_rkv"][0, 0], 2 * P)
    a["w_ffn13"] = side(g["ffn_w1"][0], g["ffn_w3"][0])
    a["w_ffn2"] = _blocks(g["ffn_w2"][0], P)
    a["w_pool"] = np.concatenate([_blocks(w, 2 * P)[0] for w in g["pool_w"][0]], 1)
    a["w_router"] = _blocks(g["moe_router_w"][0], NE)[0]
    a["router_b"] = g["moe_router_b"][0:1]
    a["tie_mask"] = np.tril(np.ones((NE, NE), np.float32), -1).reshape(1, NE * NE)
    a["before"] = np.triu(np.ones((P, P), np.float32), 1)
    a["steps"] = np.concatenate([np.arange(4) * P, np.arange(ITEMS)]).astype(np.float32)[None]
    a["zeros"] = np.zeros((P, D), np.float32)
    up = np.stack([g["moe_w1"][0], g["moe_w3"][0]], 2).reshape(NE, KT, P, 2, FE // HCOL, HCOL)
    a["w_moe_up"] = np.ascontiguousarray(up.transpose(0, 4, 2, 1, 3, 5)).reshape(NE * (FE // HCOL), P, SLOT)
    a["w_moe_down"] = np.concatenate([_blocks(g["moe_w2"][0, e], YCOL) for e in range(NE)])
    w = g["w_in_2"][0]
    a["w_qk"] = _blocks(np.concatenate([w[:, 0:1024], w[:, 1536:2560]], 1), 2 * P)
    v = np.stack([w[:, 1024:1536], w[:, 2560:3072]])
    a["w_v"] = np.ascontiguousarray(v.reshape(2, 2, 4, P, 512).transpose(0, 1, 3, 2, 4)).reshape(4, P, 2048)
    a["w_out"] = _blocks(g["w_out_2"][0], 2 * P)
    extra = np.zeros((1, 12), np.float32)
    extra[0, :8] = 1.0
    a["bias_table"] = np.concatenate([g["rel_bias_2"], extra])
    a["bucket_onehot"] = _buckets()
    up = g["w_up_2"][0]
    a["w_up"] = side(up[:, :FF], up[:, FF:])
    cw = np.concatenate([g["conv_w_2"][0], g["conv_b_2"]])
    a["conv_cols"] = np.ascontiguousarray(cw.reshape(4, 2, FT, P).transpose(3, 2, 1, 0)).reshape(P, FT, 8)
    a["w_down"] = _blocks(g["w_down_2"][0], P)
    return a


def _buckets():
    rel = np.arange(-511, 513)
    n = np.abs(rel)
    edge = [8, 16, 32, 64, 128, 256, 512]
    large = 7 + np.searchsorted(edge, n, side="right")
    b = np.where(rel > 0, 16, 0) + np.where(n < 8, n, np.minimum(large, 15))
    out = np.zeros((33, 1024), np.float32)
    out[b, np.arange(1024)] = 1.0
    cnt = sum(((rel % d == 0) & (n <= w // 2)).astype(int) for w, d in ((128, 1), (512, 4), (2048, 16)))
    out[32] = np.where(cnt > 0, np.log(np.maximum(cnt, 1)), -1e30)
    return out


def scratch(nc):
    return {n: nc.dram_tensor(n, s, F32).ap() for n, s in (
        ("bias_rows", (12, 1024)), ("kv_rows", (KT, P, 2 * TOK)), ("r_rows", (KT, P, SEQ)),
        ("x_rows", ((ITEMS + 2) * P, D)), ("y_rows", (ITEMS * P, D)))}


def kernel(**inputs):
    import concourse.bacc as bacc
    from concourse.bass_utils import run_bass_kernel_spmd

    nc = bacc.Bacc("TRN2", target_bir_lowering=False, num_devices=1)
    arrays = _layout(inputs)
    A = {n: nc.dram_tensor(n, a.shape, mybir.dt.from_np(a.dtype), kind="ExternalInput").ap()
         for n, a in arrays.items()}
    A.update(scratch(nc))
    A["out"] = nc.dram_tensor("out", (P, KT, SEQ), F32, kind="ExternalOutput").ap()
    Kernel(nc, A).build()
    r = run_bass_kernel_spmd(nc, [arrays], core_ids=[0])
    y = r.results[0]["out"]
    return np.ascontiguousarray(y.transpose(1, 0, 2).reshape(D, SEQ).T)[None]
```

```python
from contextlib import ExitStack

import numpy as np
from concourse import mybir
from concourse.bass import AP, IndirectOffsetOnAxis, ds

F32 = mybir.dt.float32
I32 = mybir.dt.int32
F32R = mybir.dt.float32r
ALU = mybir.AluOpType
ACT = mybir.ActivationFunctionType
AX = mybir.AxisListType.X

P = 128
D = 1024
KT = D // P
SEQ = 512
CTX = 256
TOK = CTX + SEQ
HALF = TOK // 2
BANK = 512
FF = 2816
FT = FF // P
NE = 8
FE = 1408
ET = FE // P
TT = SEQ // P
ITEMS = 2 * SEQ // P + NE - 1
HCOL, YCOL = 176, 256
ALPHA = float((2 * 2) ** 0.25)
LN_EPS = 1e-5
GN_EPS = 64e-5
RMS_EPS = 1e-6
DECAY = float(np.exp(-0.5))
LAMBDA_INIT = 0.8 - 0.6
GRID_W = 64
CH = 64
NCH = TOK // CH
CCH = CTX // CH
SLOTS = 3
SLOT = FT * P
WINDOWS = (2, 4, 8, 16)
PADW = 8
LEVELS = (1, 2, 4, 8, 16, 32)

COLS = {}
_at = 0
for _name, _n in (("c", 24), ("cc", 24), ("adab", 144), ("lng", 32), ("lnb", 32), ("mu", 48), ("pair", 72),
                  ("pscale", 8), ("n1g", 8), ("n2g", 8), ("qna", 1), ("kna", 1), ("qnb", 1), ("knb", 1),
                  ("sub", 1), ("lam", 4)):
    COLS[_name] = (_at, _at + _n)
    _at += _n
NCOL = _at
CONST = {}
_at = 0
for _name, _n in (("id", P), ("hsum", P), ("hmean", P), ("mean", P), ("ones", P), ("rcnt", 4 * GRID_W),
                  ("mS", 4 * P), ("mK", 4 * P), ("mL", 12 * P), ("scan", TOK)):
    CONST[_name] = (_at, _at + _n)
    _at += _n
NCONST = _at
KEPT = CONST["mS"][0]


class Marks:

    def __init__(self, sem, names, first=0):
        self.sem, self.names, self.next, self.first = sem, list(names), 0, first
        assert len(set(self.names)) == len(self.names)

    def at(self, name, it=0):
        return it * len(self.names) + self.names.index(name) + (1 + self.first)

    def trips(self, it):
        return it * len(self.names) + self.first

    def begin(self, eng):
        eng.sem_inc(self.sem, self.first)

    def did(self, name):
        assert self.names[self.next % len(self.names)] == name, (name, self.names[self.next % len(self.names)])
        self.next += 1
        return self.sem, 1


class Ring:

    def __init__(self, nc, ctx):
        self.all = ctx.enter_context(nc.sbuf_tensor("w_ring", [P, SLOTS * SLOT], F32))
        self.buf = [self.all[:, s * SLOT:(s + 1) * SLOT] for s in range(SLOTS)]
        self.loaded = [ctx.enter_context(nc.semaphore(f"w_loaded{s}")) for s in range(SLOTS)]
        self.used = [ctx.enter_context(nc.semaphore(f"w_used{s}")) for s in range(SLOTS)]
        self.drained = [ctx.enter_context(nc.semaphore(f"ps_drained{s}")) for s in range(SLOTS)]
        self.rounded = [ctx.enter_context(nc.semaphore(f"w_rounded{s}")) for s in range(SLOTS)]
        self.split = [ctx.enter_context(nc.semaphore(f"w_split{s}")) for s in range(SLOTS)]
        self.splits = [0] * SLOTS
        self.fills = [0] * SLOTS
        self.drains = [0] * SLOTS

    def used_at(self, s, k):
        return self.fills[s] + k + 2

    def drained_at(self, s, k):
        return self.drains[s] + k + 2

    def end(self, n, drains_per_chunk=1):
        for s in range(SLOTS):
            k = n // SLOTS + (s < n % SLOTS)
            self.fills[s] += k
            self.drains[s] += k * drains_per_chunk


class Split:

    def __init__(self, nc, ctx, ring, name, width):
        self.nc, self.ring, self.width = nc, ring, width
        hi, lo = (ctx.enter_context(nc.sbuf_tensor(f"sb_{q}_{name}", [P, SLOTS, width], F32R)) for q in ("hi", "lo"))
        self.hi, self.lo = ([t[:, s, :] for s in range(SLOTS)] for t in (hi, lo))

    def leading(self, act, s, trip):
        act.wait_ge(self.ring.loaded[s], (self.ring.fills[s] + trip + 1) * 16)
        self.nc.scalar.activation(self.hi[s], self.ring.buf[s][:, 0:self.width], ACT.Copy).then_inc(
            self.ring.rounded[s], 1)

    def rest(self, dve, s, trip):
        dve.wait_ge(self.ring.rounded[s], self.ring.splits[s] + trip + 1)
        w = self.ring.buf[s][:, 0:self.width]
        self.nc.vector.tensor_tensor(self.lo[s], w, self.hi[s].bitcast(F32), ALU.subtract).then_inc(self.ring.split[s], 1)

    def project(self, pe, ps, n, m_tiles, k_tiles, hi, lo):
        ring = self.ring

        def body(s, trip, c):
            pe.wait_ge(ring.split[s], ring.splits[s] + trip + 1)
            pe.wait_ge(ring.drained[s], ring.drained_at(s, trip - 1))
            for m in range(m_tiles):
                out = ps[:, 2 * s + m, :]
                for k in range(k_tiles):
                    at = (k * m_tiles + m) * P
                    w_hi = self.hi[s][:, at:at + P]
                    w_lo = self.lo[s][:, at:at + P]
                    pe.matmul(out, w_hi, lo(k), start=(k == 0), stop=False)
                    pe.matmul(out, w_lo, hi(k), start=False, stop=False)
                    last = pe.matmul(out, w_hi, hi(k), start=False, stop=(k == k_tiles - 1))
            last.then_inc(ring.used[s], 1)

        over_chunks(pe, n, body)

    def end(self, n):
        for s in range(SLOTS):
            self.ring.splits[s] += n // SLOTS + (s < n % SLOTS)
        self.ring.end(n)


def with_next(n, s, trip, c, f):
    if not isinstance(c, int) or c + 1 < n:
        f((s + 1) % SLOTS, trip + (s == SLOTS - 1))


def over_chunks(eng, n, body):
    trips = n // SLOTS
    if trips:
        with eng.Fori(0, trips) as i:
            for s in range(SLOTS):
                body(s, i, i * SLOTS + s)
    for s in range(n % SLOTS):
        body(s, trips, trips * SLOTS + s)


def load_chunks(sp, ring, src, n, width):

    def body(s, trip, c):
        sp.wait_ge(ring.used[s], ring.used_at(s, trip - 1))
        sp.dma_start(ring.buf[s][:, 0:width], src[ds(c, 1), :, :].rearrange("a p n -> (a p) n")).then_inc(
            ring.loaded[s], 16)

    over_chunks(sp, n, body)


def project(pe, ring, ps, n, m_tiles, k_tiles, moving, width=BANK, between=None):

    def body(s, trip, c):
        pe.wait_ge(ring.loaded[s], (ring.fills[s] + trip + 1) * 16)
        pe.wait_ge(ring.drained[s], ring.drained_at(s, trip - 1))
        for m in range(m_tiles):
            for k in range(k_tiles):
                at = (k * m_tiles + m) * P
                last = pe.matmul(ps[:, 2 * s + m, 0:width], ring.buf[s][:, at:at + P], moving(k),
                                 start=(k == 0), stop=(k == k_tiles - 1))
        last.then_inc(ring.used[s], 1)

    over_chunks(pe, n, body)


class Kernel:
    def __init__(self, nc, A):
        self.nc, self.A = nc, A
        self.ctx = ExitStack()

    def sb(self, ctx, name, *shape):
        return ctx.enter_context(self.nc.sbuf_tensor("sb_" + name, [P, *shape], F32))

    def right(self, ctx, name):
        return ctx.enter_context(self.nc.sbuf_tensor("sb_" + name, [P, KT, SEQ], F32, side="right"))

    def marks(self, name, names, first=0):
        return Marks(self.ctx.enter_context(self.nc.semaphore(name)), names, first)

    def sem(self, name):
        return self.ctx.enter_context(self.nc.semaphore(name))

    def col(self, name, i=0, n=1):
        a = COLS[name][0] + i
        return self.par[:, a:a + n]

    def con(self, name, i=0, n=P):
        a = CONST[name][0] + i
        return self.cst[:, a:a + n] if a < KEPT else self.masks[:, a - KEPT:a - KEPT + n]

    def build(self):
        nc = self.nc
        with self.ctx:
            ctx = self.ctx
            self.ring = Ring(nc, ctx)
            self.par = self.sb(ctx, "params", NCOL)
            self.cst = self.sb(ctx, "consts", KEPT)
            self.mod = self.sb(ctx, "mod", 3, 48, 2)
            self.tiny = self.sb(ctx, "tiny", 8)
            self.ps = ctx.enter_context(nc.psum_tensor("ps", [P, 8, BANK], F32))
            self.s_hi, self.s_lo, self.parted = self.sem("parts_leading"), self.sem("parts_rest"), 0
            self.adaln()
            b0 = ctx.enter_context(ExitStack())
            self.B0 = self.right(b0, "b0")
            self.rwkv()
            self.X = self.sb(ctx, "x", KT, SEQ)
            self.h, self.t = ctx.enter_context(ExitStack()), ctx.enter_context(ExitStack())
            self.H, self.T = self.sb(self.h, "hm", KT, SEQ), self.sb(self.t, "t", KT, SEQ)
            for stage in (self.rwkv_out, self.ffn, self.pool, self.moe, self.attention, self.convffn):
                if stage == self.ffn:
                    b0.close()
                    self.t.close()
                if stage == self.pool:
                    self.B0 = self.right(b0, "b0_again")
                if stage == self.convffn:
                    b0.close()
                    self.t.close()
                    self.h.close()
                    self.H = self.right(self.h, "hm_again")
                stage()

    def adaln(self):
        nc, A, ring, ps, mod = self.nc, self.A, self.ring, self.ps, self.mod
        s_par = self.sem("params_in")
        V = nc.vector
        NB = 4
        pe_m = self.marks("ada_pe", ["cols"], 1)
        act_m = self.marks("ada_act", ["row0", "row1", "row2"])
        dve_m = self.marks("ada_dve", ["mod"], 1)
        s_silu = self.sem("silu_c")
        s_fix = self.sem("mod_plus_one")
        with ExitStack() as st:
            cs = self.sb(st, "c_silu", 3, KT, 2)
            row = self.sb(st, "ada_row", 3, BANK)
            with nc.Block() as block:
                @block.gpsimd
                def _(pool):
                    for q in (*ring.used, *ring.drained, pe_m.sem, dve_m.sem):
                        pool.sem_inc(q, 1)

                @block.sync
                def _(sp):
                    sp.dma_start(self.par[:, :], A["params"]).then_inc(s_par, 16)
                    sp.dma_start(self.cst[:, :], A["consts"][:, 0:KEPT]).then_inc(s_par, 16)
                    load_chunks(sp, ring, A["w_ada"], 72, 2048)

                @block.scalar
                def _(act):
                    act.wait_ge(s_par, 32)
                    for v in range(2):
                        last = nc.scalar.activation(cs[:, :, :, v],
                                                    self.col(("c", "cc")[v], 0, 24).rearrange("p (a k) -> p a k", a=3),
                                                    ACT.Silu)
                        last.then_inc(s_silu, 1)
                    for a in range(3):
                        with act.Fori(a * NB, (a + 1) * NB) as i:
                            act.wait_ge(pe_m.sem, pe_m.trips(i))
                            for b in range(3):
                                act.wait_ge(ring.used[(2 * b + 1) % SLOTS],
                                            ring.used_at((2 * b + 1) % SLOTS, 2 * i + (2 * b + 1) // SLOTS))
                                nc.scalar.activation(row[0:2, b, :], ps[0:2, b, :], ACT.Copy).then_inc(
                                    *act_m.did(f"row{b}"))

                @block.tensor
                def _(pe):
                    pe.wait_ge(s_silu, 2)
                    pe.wait_ge(s_par, 32)
                    for a in range(3):
                        with pe.Fori(a * NB, (a + 1) * NB) as i:
                            for b in range(3):
                                for half in range(2):
                                    ch = 2 * b + half
                                    s = ch % SLOTS
                                    k = 2 * i + ch // SLOTS
                                    pe.wait_ge(ring.loaded[s], (k + 1) * 16)
                                    for kt in range(4):
                                        last = pe.matmul(ps[0:2, b, :], cs[:, a, 4 * half + kt, :],
                                                         ring.buf[s][:, kt * BANK:(kt + 1) * BANK],
                                                         start=(half == 0 and kt == 0), stop=(half == 1 and kt == 3))
                                    last.then_inc(ring.used[s], 1)
                            pe.wait_ge(dve_m.sem, dve_m.trips(i))
                            for b in range(3):
                                pe.wait_ge(act_m.sem, act_m.at(f"row{b}", i))
                                for j in range(4):
                                    at = 2 * (4 * b + j)
                                    last = pe.matmul(ps[:, 3, at:at + 2], row[0:2, b, j * P:(j + 1) * P],
                                                     self.con("id", 0, 2)[0:2, :], start=True, stop=True)
                            last.then_inc(*pe_m.did("cols"))

                @block.vector
                def _(dve):
                    dve.wait_ge(s_par, 32)
                    for a in range(3):
                        with dve.Fori(0, NB) as i:
                            dve.wait_ge(pe_m.sem, pe_m.at("cols", i + a * NB))
                            dst = mod[:, a, ds(i * 12, 12), :]
                            b = self.par[:, ds(i * 12 + (COLS["adab"][0] + 48 * a), 12)]
                            nc.vector.tensor_tensor(dst, ps[:, 3, 0:24].rearrange("p (a b) -> p a b", b=2),
                                                    b.unsqueeze(2).broadcast_to([P, 12, 2]),
                                                    ALU.add).then_inc(*dve_m.did("mod"))
                    for i, eps in enumerate((LN_EPS, GN_EPS, RMS_EPS)):
                        V.memset(self.tiny[:, i:i + 1], eps)
                    dve.wait_ge(dve_m.sem, dve_m.trips(3 * NB))
                    for j in (8, 32):
                        nc.vector.tensor_scalar(mod[:, :, j:j + 8, :], mod[:, :, j:j + 8, :], 1.0, None,
                                                ALU.add).then_inc(s_fix, 1)
        ring.end(72, 0)

    def rwkv(self):
        YG = self.B0
        with ExitStack() as mix:
            TW, TA, TG = self.sb(mix, "tw", TOK), self.sb(mix, "ta", TOK), self.sb(mix, "tg", SEQ)
            with ExitStack() as xs:
                xk, xv = self.sb(xs, "xk", KT, TOK), self.sb(xs, "xv", KT, TOK)
                xr = self.sb(xs, "xr", KT, SEQ)
                with ExitStack() as hs:
                    h, xx = self.sb(hs, "h", KT, TOK), self.sb(hs, "xx", KT, TOK)
                    self.token_mix(h, xx, xk, xv, xr, TW, TA, TG)
                self.project_rkv(xk, xv, xr)
            self.pairs(TW, TA, TG, YG)

    def project_rkv(self, xk, xv, xr):
        nc, A, ring, ps = self.nc, self.A, self.ring, self.ps
        S, V = nc.scalar, nc.vector
        N = KT // 2
        pe_m = self.marks("kv_pe", ["kv0", "kv1"], 1)
        act_m, dve_m = self.marks("kv_act", ["k0", "k1"]), self.marks("kv_dve", ["v0", "v1"])
        s_w = [self.sem(f"kv_w{i}") for i in range(2)]
        s_pad = self.sem("kv_padded")
        s_st = [self.sem(f"kv_stored{i}") for i in range(2)]
        s_kvf = [self.sem(f"kv_banks{i}") for i in range(2)]
        s_wr, s_pr, s_er = (self.sem(f"r_{q}") for q in ("w", "pe", "out"))
        s_sr = [self.sem(f"r_stored{i}") for i in range(4)]
        with ExitStack() as st:
            KV = self.sb(st, "kv", 2, 2, TOK)
            with nc.Block() as block:
                @block.gpsimd
                def _(pool):
                    pe_m.begin(pool)
                    for q in (*s_st, *s_kvf):
                        pool.sem_inc(q, 1)
                    pool.dma_start(A["kv_rows"][KT], A["zeros"]).then_inc(s_pad, 16)
                    pool.dma_start(A["r_rows"][KT], A["zeros"][:, 0:SEQ]).then_inc(s_pad, 16)
                    pool.wait_ge(s_pad, 32)

                @block.sync
                def _(sp):
                    with sp.Fori(0, N) as i:
                        for b in range(2):
                            sp.wait_ge(pe_m.sem, pe_m.trips(i))
                            sp.dma_start(ring.buf[b][:, 0:2 * KT * P],
                                         A["w_kv"][ds(2 * i + b, 1)].rearrange("a p n -> (a p) n")).then_inc(s_w[b], 16)
                    for c in range(4):
                        if c >= 1:
                            sp.wait_ge(s_pr, 2 * c)
                        else:
                            sp.wait_ge(pe_m.sem, pe_m.trips(N))
                        sp.dma_start(ring.buf[2][:, 0:2 * KT * P], A["w_r"][c]).then_inc(s_wr, 16)

                @block.tensor
                def _(pe):
                    with pe.Fori(0, N) as i:
                        for b in range(2):
                            pe.wait_ge(s_w[b], (i + 1) * 16)
                            if b == 0:
                                pe.wait_ge(s_kvf[0], 2 * i + 1)
                            else:
                                pe.wait_ge(s_kvf[1], 2 * i + 1)
                            for m, src in enumerate((xk, xv)):
                                for hf in range(2):
                                    for k in range(KT):
                                        at = (2 * k + m) * P
                                        last = pe.matmul(ps[:, 4 * b + 2 * m + hf, 0:HALF], ring.buf[b][:, at:at + P],
                                                         src[:, k, hf * HALF:(hf + 1) * HALF],
                                                         start=(k == 0), stop=(k == KT - 1))
                            last.then_inc(*pe_m.did(f"kv{b}"))
                    pe.wait_ge(act_m.sem, act_m.trips(N))
                    pe.wait_ge(dve_m.sem, dve_m.trips(N))
                    for n in range(KT):
                        if n % 2 == 0:
                            pe.wait_ge(s_wr, (n // 2 + 1) * 16)
                        for k in range(KT):
                            last = pe.matmul(ps[:, n, :], ring.buf[2][:, (2 * k + n % 2) * P:(2 * k + n % 2 + 1) * P],
                                             xr[:, k, :], start=(k == 0), stop=(k == KT - 1))
                        last.then_inc(s_pr, 1)

                @block.scalar
                def _(act):
                    with act.Fori(0, N) as i:
                        for b in range(2):
                            act.wait_ge(pe_m.sem, pe_m.at(f"kv{b}", i))
                            act.wait_ge(s_st[b], i * 16 + 1)
                            S.activation(KV[:, b, 0, :].rearrange("p (a n) -> p a n", a=2), ps[:, 4 * b:4 * b + 2, 0:HALF],
                                         ACT.Copy).then_inc(*act_m.did(f"k{b}"))
                            act.wait_ge(act_m.sem, act_m.at(f"k{b}", i))
                            act.sem_inc(s_kvf[b], 1)
                            act.wait_ge(dve_m.sem, dve_m.at(f"v{b}", i))
                            act.sem_inc(s_kvf[b], 1)
                            act.dma_start(A["kv_rows"][ds(2 * i + b, 1)].rearrange("a p n -> (a p) n"),
                                          KV[:, b, :, :].rearrange("p a n -> p (a n)")).then_inc(s_st[b], 16)
                    for b in range(2):
                        act.wait_ge(s_st[b], 16 * N + 1)
                    for n in range(KT):
                        act.wait_ge(s_pr, n + 1)
                        if n >= 4:
                            act.wait_ge(s_sr[n % 4], 16)
                        R = KV[:, (n // 2) % 2, n % 2, 0:SEQ]
                        S.activation(R, ps[:, n, :], ACT.Copy).then_inc(s_er, 1)
                        act.wait_ge(s_er, n + 1)
                        act.dma_start(A["r_rows"][n], R).then_inc(s_sr[n % 4], 16)
                    for q in s_sr:
                        act.wait_ge(q, 32)

                @block.vector
                def _(dve):
                    with dve.Fori(0, N) as i:
                        for b in range(2):
                            dve.wait_ge(pe_m.sem, pe_m.at(f"kv{b}", i))
                            dve.wait_ge(s_st[b], i * 16 + 1)
                            V.tensor_copy(KV[:, b, 1, :].rearrange("p (a n) -> p a n", a=2),
                                          ps[:, 4 * b + 2:4 * b + 4, 0:HALF]).then_inc(*dve_m.did(f"v{b}"))

    def token_mix(self, h, xx, xk, xv, xr, TW, TA, TG):
        nc, A, ring, ps, mod = self.nc, self.A, self.ring, self.ps, self.mod
        V = nc.vector
        s_x, s_lw = self.sem("x_in"), self.sem("lora_in")
        dve_m = self.marks("mix_dve", ["h", "xw", "xa", "xg", "xk", "xv", "xr"])
        s_h = self.sem("h_steps")
        pe_m = self.marks("mix_pe", ["w", "a", "g"])
        act_m = self.marks("mix_act", ["w", "a", "g"])
        lw = [ring.buf[s][:, 0:KT * P] for s in range(3)]
        with nc.Block() as block:
            @block.sync
            def _(sp):
                sp.dma_start(h[:, :, 0:CTX], A["ctxT"]).then_inc(s_x, 16)
                sp.dma_start(h[:, :, CTX:TOK], A["xT"]).then_inc(s_x, 16)
                for i in range(3):
                    sp.dma_start(lw[i], A["w_lora1"][i]).then_inc(s_lw, 16)

            @block.vector
            def _(dve):
                dve.wait_ge(s_x, 32)
                for k in range(KT):
                    for who, a, b in ((1, 0, CTX), (0, CTX, TOK)):
                        last = V.tensor_scalar(h[:, k, a:b], h[:, k, a:b], mod[:, 0, 8 + k, who:who + 1],
                                               mod[:, 0, k, who:who + 1], ALU.mult, ALU.add)
                        last.then_inc(s_h, 1)
                dve.wait_ge(s_h, 2 * KT)
                V.tensor_scalar(xx[:, :, :], h[:, :, :], -1.0, None, ALU.mult).then_inc(*dve_m.did("h"))
                dve.wait_ge(dve_m.sem, dve_m.at("h"))
                ops = [(slice(0, 4), (1, CTX), (0, CTX - 1)), (slice(4, 8), (0, CTX - 1), (1, CTX))]
                for f, (a, b), (c, d) in ops:
                    V.tensor_tensor(xx[:, f, a:b], h[:, f, c:d], h[:, f, a:b], ALU.subtract).then_inc(s_h, 1)
                R = SEQ // GRID_W
                for f, (r0, c0), (nr, ncol), (rs, cs) in (
                        (slice(0, 2), (0, 1), (R, GRID_W - 1), (0, 0)), (slice(2, 4), (0, 0), (R, GRID_W - 1), (0, 1)),
                        (slice(4, 6), (1, 0), (R - 1, GRID_W), (0, 0)), (slice(6, 8), (0, 0), (R - 1, GRID_W), (1, 0))):
                    for k in range(f.start, f.stop):
                        g = h[:, k, CTX:TOK].rearrange("p (r c) -> p r c", c=GRID_W)
                        o = xx[:, k, CTX:TOK].rearrange("p (r c) -> p r c", c=GRID_W)
                        V.tensor_tensor(o[:, r0:r0 + nr, c0:c0 + ncol], g[:, rs:rs + nr, cs:cs + ncol],
                                        g[:, r0:r0 + nr, c0:c0 + ncol], ALU.subtract).then_inc(s_h, 1)
                dve.wait_ge(s_h, 2 * KT + 2 + KT)
                for name, mu, dst, a, free in (("xw", 1, xk, 0, None), ("xa", 4, xv, 0, None), ("xg", 5, xr, CTX, None),
                                               ("xk", 2, xk, 0, "w"), ("xv", 3, xv, 0, "a"), ("xr", 0, xr, CTX, "g")):
                    if free:
                        dve.wait_ge(pe_m.sem, pe_m.at(free))
                    for k in range(KT):
                        last = V.scalar_tensor_tensor(out=dst[:, k, :], in0=xx[:, k, a:TOK],
                                                      scalar=self.col("mu", mu * 8 + k), in1=h[:, k, a:TOK],
                                                      op0=ALU.mult, op1=ALU.add)
                    last.then_inc(*dve_m.did(name))

            @block.tensor
            def _(pe):
                pe.wait_ge(s_lw, 48)
                for i, (name, src, need) in enumerate((("w", xk, "xw"), ("a", xv, "xa"), ("g", xr, "xg"))):
                    pe.wait_ge(dve_m.sem, dve_m.at(need))
                    spans = [(0, HALF), (HALF, TOK)] if i < 2 else [(0, SEQ)]
                    for b, (c, d) in enumerate(spans):
                        for k in range(KT):
                            last = pe.matmul(ps[:, 2 * i + b, 0:d - c], lw[i][:, k * P:(k + 1) * P], src[:, k, c:d],
                                             start=(k == 0), stop=(k == KT - 1))
                    last.then_inc(*pe_m.did(name))

            @block.scalar
            def _(act):
                for i, (name, dst, f) in enumerate((("w", TW, ACT.Tanh), ("a", TA, ACT.Copy), ("g", TG, ACT.Sigmoid))):
                    act.wait_ge(pe_m.sem, pe_m.at(name))
                    if i < 2:
                        o, src = dst[:, :].rearrange("p (a b) -> p a b", a=2), ps[:, 2 * i:2 * i + 2, 0:HALF]
                    else:
                        o, src = dst[:, :], ps[:, 4, :]
                    nc.scalar.activation(o, src, f).then_inc(*act_m.did(name))

    def pair_tile(self, p):
        return 4 + p // 2 if p % 2 == 0 else (p + 1) // 2 % 4

    def pairs(self, TW, TA, TG, YG):
        nc, A, ring, ps = self.nc, self.A, self.ring, self.ps
        V, S = nc.vector, nc.scalar
        N, NQ = KT, NCH // 2
        LAST = 4
        feats = ["Dpj", "Domka", "Dkkr", "Dsq", "Pnorm0", "Aroot0", "Pnorm1", "Aroot1", "Dmax", "Drec", "Dkkn",
                 "Pw0.0", "Aw0.0", "Pw0.1", "Aw0.1", "Dkk", "Dscan0", "Pw1.0", "Aw1.0", "Pw1.1", "Aw1.1", "Dex0",
                 "Dscan1", "Pa0.0", "Aa0.0", "Pa0.1", "Aa0.1", "Dex1", "Pa1.0", "Aa1.0", "Pa1.1", "Aa1.1", "Din1",
                 "Pg", "Ag", "APx0", "APi0", "APx1", "APi1", "AP0", "AP1", "AP", "DA0", "DA1", "Dkka0", "Dkka1", "DB0", "DB1",
                 "Dkd0", "Dkd1", "Dkdk0", "Dkdk1", "DK0", "DK1", "DR0", "DR1", "Drr", "Dkds", "Dcoefin", "Pcoef",
                 "Dbonus"]
        lin = self.marks("lin_pe", [x[1:] for x in feats if x[0] == "P"])
        f_act = self.marks("feat_act", [x[1:] for x in feats if x[0] == "A"])
        f_dve = self.marks("feat_dve", [x[1:] for x in feats if x[0] == "D"])
        outs = ["DY", "Pmean", "Dyc", "Dsq", "Pvar", "Aroot", "Drec", "Dyn", "Daffine", "Dbonus", "Dgated"]
        o_pe = self.marks("out_pe", [x[1:] for x in outs if x[0] == "P"])
        o_act = self.marks("out_act", [x[1:] for x in outs if x[0] == "A"])
        o_dve = self.marks("out_dve", [x[1:] for x in outs if x[0] == "D"])

        def lat(n):
            return n >= CCH

        def steps(q):
            return [2 * q, 2 * q + 1] if 0 <= q < NQ else []

        def chain(n):
            return [f"U{n}", f"Z{n}"] + [f"Y{n}"] * lat(n)

        order = []
        for q in range(NQ + 1):
            ab, pq = steps(q), steps(q - 1)
            order += [f"score{n}" for n in ab] + [f"trans{n}" for n in ab[:1]] + [f"L{n}" for n in ab]
            order += [f"X0.{n}" for n in ab] + [f"trans{n}" for n in ab[1:]] + [f"T0.{n}" for n in ab]
            order += [f"U{n}" for n in pq[:1]]
            order += [f"X1.{n}" for n in ab] + [f"T1.{n}" for n in ab]
            order += [x for n in pq[:1] for x in chain(n)[1:]]
            order += [f"X2.{n}" for n in ab] + [f"T2.{n}" for n in ab]
            order += [f"U{n}" for n in pq[1:]]
            order += [f"X3.{n}" for n in ab] + [f"T3.{n}" for n in ab]
            order += [x for n in pq[1:] for x in chain(n)[1:]]
            order += [f"X4.{n}" for n in ab] + [f"T4.{n}" for n in ab] + [f"akv{n}" for n in ab]
        first, stop = 2, order.index(f"Y{CCH}") - 2
        plan, done = [], 0
        extra = [("output", x) for x in outs] + [("feature", x) for x in feats]
        for i, x in enumerate(order):
            due = len(extra) * min(max(i - first, 0), stop - first) // (stop - first)
            plan += extra[done:due] + [("rec", x)]
            done = due
        pe_m = self.marks("rec_pe", order, len(order))
        act_of = {"trans": ["trB", "tr"], "U": ["U", "Zs"], "akv": ["akv"], "Y": ["Y"]}
        dve_of = {"score": ["sS", "sK"], "L": ["t0a", "t0b", "t0."], "X": ["x"], "T": ["t"], "Z": ["z"]}

        def follow(table):
            out = []
            for x in order:
                head = x.rstrip("0123456789.")
                for y in table.get(head, ()):
                    if y == "t":
                        out.append(f"t{int(x[1]) + 1}.{x[3:]}")
                    elif y == "x":
                        out.append(f"x{x[1:]}")
                    else:
                        out.append(y + x[len(head):])
            return out

        act_m = self.marks("rec_act", follow(act_of), len(follow(act_of)))
        dve_m = self.marks("rec_dve", follow(dve_of), len(follow(dve_of)))
        pool_m = self.marks("rec_pool", [f"bd{n}" for n in range(NCH)], 1)
        passed, z_init, s_mask = self.sem("waits_passed"), self.sem("blocks_zeroed"), self.sem("masks_in")
        s_blank = self.sem("blank_pair")
        s_restart = self.sem("state_restarted")
        s_k, s_v, s_w = self.sem("kr_in"), self.sem("v_in"), self.sem("w_pair_in")

        def chunk_at(n, d):
            if d == 0:
                return n * CH
            return (CCH - 1 - n) * CH if n < CCH else (NCH - 1 - (n - CCH)) * CH

        with ExitStack() as st:
            k, kk, t1 = (self.sb(st, n, TOK) for n in ("k", "kk", "t1"))
            r = self.sb(st, "r", SEQ)
            a, cs = self.sb(st, "a", 2, TOK), self.sb(st, "cs", 2, TOK)
            V2, BON, GT = self.sb(st, "v", 2, TOK), self.sb(st, "bon", 2, SEQ), self.sb(st, "g", 2, SEQ)
            SG, EX, PI = (self.sb(st, n, 2, 2, TOK) for n in ("sg", "ex", "Pi"))
            FR2, PJ2, PE2 = self.sb(st, "FR", 2, 2, SEQ), self.sb(st, "pj", 2, 10), self.sb(st, "pend", 2, 2, NCH)
            Y, W = self.sb(st, "Y", 2, SEQ), self.sb(st, "w_pair", 5 * P)
            Z, Zs, Us = self.sb(st, "Z", 2, P), self.sb(st, "Zs", 2, P), self.sb(st, "Us", 2, P)
            self.masks = self.sb(st, "masks", NCONST - KEPT)
            SETS = 4
            bd = ring.all[:, 0:SETS * 10 * P].rearrange("p (s d i n) -> p s d i n", s=SETS, d=2, i=5)
            off = SETS * 10 * P
            TB = ring.all[:, off:off + SETS * 4 * P].rearrange("p (s d i n) -> p s d i n", s=SETS, d=2, i=2)
            off += SETS * 4 * P
            Xs = ring.all[:, off:off + 4 * P].rearrange("p (s d n) -> p s d n", s=2, d=2)
            tr = self.sb(st, "tr", SETS, 2, 4, P)
            LK = self.sb(st, "lk", SETS, 2, 4, P)
            AT = self.sb(st, "at", SETS, 2, 2, P)
            def halves(x):
                return x.rearrange("p (a b) -> p a b", a=2)

            with nc.Block() as block:
                @block.sync
                def _(sp):
                    def row(name, j):
                        x = A[name][0] if j is None else A[name][ds(j, 1)].rearrange("a p n -> (a p) n")
                        return x

                    def loads(j):
                        kv = row("kv_rows", j)
                        sp.dma_start(k[:, :], kv[:, 0:TOK]).then_inc(s_k, 16)
                        sp.dma_start(r[:, :], row("r_rows", j)).then_inc(s_k, 16)
                        sp.dma_start(W[:, :], row("w_pair", j)).then_inc(s_w, 16)
                        return kv

                    sp.dma_start(self.masks[:, :], A["consts"][:, KEPT:NCONST]).then_inc(s_mask, 16)
                    kv = loads(None)
                    sp.dma_start(V2[:, 0, :], kv[:, TOK:2 * TOK]).then_inc(s_v, 16)
                    with sp.Fori(0, N // 2) as jj:
                        for u in range(2):
                            j = jj * 2 + u
                            for m, n in ((f_dve, j + 1), (lin, j + 1), (pool_m, j)):
                                sp.wait_ge(m.sem, m.trips(n))
                                sp.sem_inc(passed, 1)
                            kv = loads(j + 1)
                            sp.dma_start(V2[:, 1 - u, :], kv[:, TOK:2 * TOK]).then_inc(s_v, 16)
                    sp.wait_ge(s_k, (N + 1) * 32)
                    sp.wait_ge(s_w, (N + 1) * 16)
                    sp.wait_ge(s_v, (N + 1) * 16)

                @block.gpsimd
                def _(pool):
                    G = nc.gpsimd
                    for m in (pe_m, act_m, dve_m, pool_m):
                        m.begin(pool)
                    G.memset(bd[:, :, :, :, :], 0.0).then_inc(z_init, 1)
                    pool.wait_ge(z_init, 1)
                    with pool.Fori(0, N // 2) as jj:
                      for u in range(2):
                        j = jj * 2 + u
                        FA, FB, FK, FR, v = EX[:, u], SG[:, u], PI[:, u], FR2[:, u], V2[:, u]
                        pool.wait_ge(f_dve.sem, f_dve.trips(j + 1))
                        pool.sem_inc(passed, 1)
                        for n in range(NCH):
                            if n >= SETS:
                                pool.wait_ge(pe_m.sem, pe_m.at(chain(n - SETS)[-1], j))
                            else:
                                pool.wait_ge(pe_m.sem, pe_m.at(chain(NCH - SETS + n)[-1], j - 1))
                            pool.sem_inc(passed, 1)
                            for d in range(2):
                                at = chunk_at(n, d)
                                c = slice(at, at + CH)
                                srcs = [(0, FA[:, d, c]), (2, FB[:, d, c]), (3, FK[:, d, c]), (4, v[:, c])]
                                if lat(n):
                                    srcs.append((1, FR[:, d, at - CTX:at - CTX + CH]))
                                for i, src in srcs:
                                    for hh in range(2):
                                        rows = slice(64 * hh, 64 * hh + 64)
                                        last = G.tensor_copy(bd[rows, n % SETS, d, i, rows], src[rows])
                            last.then_inc(*pool_m.did(f"bd{n}"))

                @block.tensor
                def _(pe):
                    ident = self.con("id")

                    def output(x, j):
                        if x == "mean":
                            pe.wait_ge(act_m.sem, act_m.at(f"Y{NCH - 1}", j - 1))
                            pe.wait_ge(o_dve.sem, o_dve.at("Y", j))
                            return pe.matmul(ps[:, 7, :], self.con("hmean"), Y[:, 0, :], start=True, stop=True)
                        pe.wait_ge(o_dve.sem, o_dve.at("sq", j))
                        return pe.matmul(ps[:, 7, :], self.con("hmean"), t1[:, 0:SEQ], start=True, stop=True)

                    def feature(x, j, first=False):
                        def evacuated(name):
                            pe.wait_ge(f_act.sem, f_act.at(name, j))

                        def lora(i, b, src):
                            return pe.matmul(ps[:, 7, 0:HALF], W[:, i * P:(i + 1) * P], src[:, b * HALF:(b + 1) * HALF],
                                             start=True, stop=True)

                        if x == "norm0":
                            pe.wait_ge(s_w, (j + 1) * 16)
                            pe.wait_ge(f_dve.sem, f_dve.at("sq", j))
                            if not first:
                                pe.wait_ge(o_act.sem, o_act.at("root", j - 1))
                            return pe.matmul(ps[:, 7, 0:HALF], self.con("hsum"), t1[:, 0:HALF], start=True, stop=True)
                        if x == "norm1":
                            evacuated("root0")
                            return pe.matmul(ps[:, 7, 0:HALF], self.con("hsum"), t1[:, HALF:TOK], start=True, stop=True)
                        if x == "w0.0":
                            evacuated("root1")
                            return lora(0, 0, TW)
                        if x == "w0.1":
                            evacuated("w0.0")
                            return lora(0, 1, TW)
                        if x == "w1.0":
                            evacuated("w0.1")
                            return lora(1, 0, TW)
                        if x == "w1.1":
                            evacuated("w1.0")
                            return lora(1, 1, TW)
                        if x == "a0.0":
                            evacuated("w1.1")
                            return lora(2, 0, TA)
                        if x == "a0.1":
                            evacuated("a0.0")
                            return lora(2, 1, TA)
                        if x == "a1.0":
                            evacuated("a0.1")
                            return lora(3, 0, TA)
                        if x == "a1.1":
                            evacuated("a1.0")
                            return lora(3, 1, TA)
                        if x == "g":
                            evacuated("a1.1")
                            return pe.matmul(ps[:, 7, :], W[:, 4 * P:5 * P], TG[:, :], start=True, stop=True)
                        evacuated("g")
                        pe.wait_ge(f_dve.sem, f_dve.at("coefin", j))
                        return pe.matmul(ps[:, 7, :], self.con("hsum"), t1[:, 0:SEQ], start=True, stop=True)

                    for x in feats:
                        if x[0] == "P":
                            feature(x[1:], 0, True).then_inc(*lin.did(x[1:]))
                    with pe.Fori(0, N // 2) as jj:
                      for u in range(2):
                        j = jj * 2 + u

                        def after(marks, name):
                            pe.wait_ge(marks.sem, marks.at(name, j))

                        def two(bank, lo, mm):
                            for d in range(2):
                                last = mm(ps[:, bank, lo + d * P:lo + (d + 1) * P], d)
                            return last

                        for kind, x in plan:
                            if kind == "feature":
                                if x[0] == "P":
                                    feature(x[1:], j + 1).then_inc(*lin.did(x[1:]))
                                continue
                            if kind == "output":
                                if x[0] == "P":
                                    output(x[1:], j).then_inc(*o_pe.did(x[1:]))
                                continue
                            head, rest = x.rstrip("0123456789."), x[len(x.rstrip("0123456789.")):]
                            n = int(rest.split(".")[-1])
                            i = int(rest[0]) if "." in rest else 0
                            s, h = n % SETS, n % 2
                            B, TR, SC, TI, X2 = bd[:, s], tr[:, s], LK[:, s], TB[:, s], Xs[:, h]
                            if head == "score":
                                after(pool_m, f"bd{n}")
                                pe.wait_ge(dve_m.sem, dve_m.at(f"t5.{(n - 2) % NCH}", j if n >= 2 else j - 1))
                                nr = 2 if lat(n) else 1
                                for o, bank in ((2, 2 * h), (3, 2 * h + 1)):
                                    for d in range(2):
                                        last = pe.matmul(ps[:, bank, 256 * d:256 * d + nr * P], B[:, d, o, :],
                                                         B[:, d, 0:nr, :].rearrange("p a b -> p (a b)"),
                                                         start=True, stop=True)
                            elif head == "trans":
                                if h:
                                    after(act_m, f"tr{n - 1}")
                                else:
                                    pe.wait_ge(act_m.sem, act_m.at(f"akv{(n - 1) % NCH}", j if n else j - 1))
                                for d in range(2):
                                    for o, src in enumerate((0, 3, 4, 2)):
                                        last = pe.transpose(ps[:, 4 + d, o * P:(o + 1) * P], B[:, d, src, :], ident)
                            elif head == "L":
                                after(dve_m, f"sS{n}")
                                last = two(2 * h, 0, lambda o, d: pe.transpose(o, SC[:, d, 0, :], ident))
                            elif head == "X":
                                after(dve_m, f"t{i}.{n}")
                                last = two(2 * h, 0, lambda o, d: pe.matmul(o, SC[:, d, 0, :], TI[:, d, 0, :],
                                                                            start=True, stop=True))
                            elif head == "T":
                                after(dve_m, f"x{i}.{n}")
                                if i == 0:
                                    after(dve_m, f"sK{n}")
                                for d in range(2):
                                    o = ps[:, 2 * h + 1, 256 * d:256 * d + 2 * P]
                                    if i < LAST:
                                        pe.matmul(o[:, 0:P], TI[:, d, 1, :], X2[:, d, :], start=True, stop=True)
                                    last = pe.matmul(o[:, P:2 * P], X2[:, d, :], TI[:, d, 1, :], start=True, stop=True)
                            elif head == "akv":
                                after(act_m, f"tr{n | 1}")
                                after(dve_m, f"t5.{n}")
                                two(4 + h, 0, lambda o, d: pe.matmul(o, SC[:, d, 2, :], TR[:, d, 2, :], start=True, stop=True))
                                last = two(4 + h, 256, lambda o, d: pe.matmul(o, TR[:, d, 0, :], TI[:, d, 1, :],
                                                                              start=True, stop=True))
                            elif head == "U":
                                after(act_m, f"akv{n}")
                                if n:
                                    after(dve_m, f"z{n - 1}")
                                else:
                                    pe.wait_ge(s_restart, j + 1)
                                for d in range(2):
                                    o = ps[:, 6, d * P:(d + 1) * P]
                                    pe.matmul(o, TI[:, d, 1, :], AT[:, s, 0, d, :], start=True, stop=False)
                                    last = pe.matmul(o, AT[:, s, 1, d, :], Z[:, d, :], start=False, stop=True)
                            elif head == "Z":
                                after(act_m, f"U{n}")
                                for d in range(2):
                                    o = ps[:, 6, (2 + d) * P:(3 + d) * P]
                                    pe.matmul(o, TR[:, d, 1, :], TR[:, d, 2, :], start=True, stop=False)
                                    last = pe.matmul(o, TR[:, d, 3, :], Us[:, d, :], start=False, stop=True)
                            elif head == "Y":
                                if n > CCH:
                                    after(act_m, f"Y{n - 1}")
                                else:
                                    pe.wait_ge(f_dve.sem, f_dve.at("bonus", j + 1))
                                for d in range(2):
                                    o = ps[:, 7, d * P:(d + 1) * P]
                                    pe.matmul(o, Z[:, d, :], B[:, d, 1, :], start=True, stop=False)
                                    pe.matmul(o, TR[:, d, 2, :], SC[:, d, 3, :], start=False, stop=False)
                                    last = pe.matmul(o, Us[:, d, :], SC[:, d, 1, :], start=False, stop=True)
                            last.then_inc(*pe_m.did(x))

                    output("mean", N).then_inc(*o_pe.did("mean"))
                    output("var", N).then_inc(*o_pe.did("var"))

                @block.scalar
                def _(act):
                    def output(j):
                        act.wait_ge(o_pe.sem, o_pe.at("var", j))
                        return S.activation(t1[:, 0:SEQ], ps[:, 7, :], ACT.Sqrt, bias=self.tiny[:, 1:2])

                    def feature(x, j, u):
                        PJ, sg, ex, Pi = PJ2[:, u], SG[:, u], EX[:, u], PI[:, u]
                        if x[:2] in ("w0", "w1", "a0", "a1"):
                            act.wait_ge(lin.sem, lin.at(x, j))
                            i, b = ("w0", "w1", "a0", "a1").index(x[:2]), int(x[-1])
                            return S.activation((sg, a)[i // 2][:, i % 2, b * HALF:(b + 1) * HALF], ps[:, 7, 0:HALF],
                                                ACT.Sigmoid, bias=PJ[:, i:i + 1])
                        if x == "g":
                            act.wait_ge(lin.sem, lin.at("g", j))
                            return S.activation(GT[:, u], ps[:, 7, :], ACT.Copy)
                        if x.startswith("root"):
                            b = int(x[-1])
                            act.wait_ge(lin.sem, lin.at(f"norm{b}", j))
                            return S.activation(kk[:, b * HALF:(b + 1) * HALF], ps[:, 7, 0:HALF], ACT.Sqrt)
                        if x == "AP" or x == "P":
                            act.wait_ge(f_act.sem, f_act.at("P1", j))
                            S.activation(PE2[:, u, 0, :], cs[:, 0, :].rearrange("p (c t) -> p c t", t=CH)[:, :, CH - 1],
                                         ACT.Copy)
                            return S.activation(PE2[:, u, 1, :], cs[:, 1, :].rearrange("p (c t) -> p c t", t=CH)[:, :, 0],
                                                ACT.Copy)
                        d = int(x[-1])
                        act.wait_ge(f_dve.sem, f_dve.at("in1", j))
                        if x.startswith("Px"):
                            return S.activation(ex[:, d, :], ex[:, d, :], ACT.Exp, scale=-DECAY)
                        if x.startswith("Pi"):
                            return S.activation(Pi[:, d, :], cs[:, d, :], ACT.Exp, scale=DECAY)
                        act.wait_ge(f_act.sem, f_act.at("Pi1", j))
                        return S.activation(cs[:, d, :], cs[:, d, :], ACT.Exp, scale=-DECAY)

                    act.wait_ge(f_dve.sem, f_dve.at("pj"))
                    for x in feats:
                        if x[0] == "A":
                            feature(x[1:], 0, 0).then_inc(*f_act.did(x[1:]))
                    with act.Fori(0, N // 2) as jj:
                      for u in range(2):
                        j = jj * 2 + u
                        Pn = PE2[:, u]
                        for kind, x in plan:
                            if kind == "feature":
                                if x == "Aroot0":
                                    act.wait_ge(pool_m.sem, pool_m.trips(j))
                                    act.wait_ge(dve_m.sem, dve_m.trips(j))
                                if x == "Ag":
                                    act.wait_ge(o_dve.sem, o_dve.at("gated", j))
                                if x[0] == "A":
                                    feature(x[1:], j + 1, 1 - u).then_inc(*f_act.did(x[1:]))
                                continue
                            if kind == "output":
                                if x[0] == "A":
                                    output(j).then_inc(*o_act.did("root"))
                                continue
                            head = x.rstrip("0123456789.")
                            if head not in act_of:
                                continue
                            n = int(x[len(head):])
                            s, h = n % SETS, n % 2
                            act.wait_ge(pe_m.sem, pe_m.at(x, j))
                            if head == "trans":
                                S.activation(tr[:, s, :, 3, :], ps[:, 4:6, 3 * P:4 * P], ACT.Copy, scale=-1.0).then_inc(
                                    *act_m.did(f"trB{n}"))
                                S.activation(tr[:, s, :, 0:3, :], ps[:, 4:6, 0:3 * P].rearrange("p d (o n) -> p d o n", o=3),
                                             ACT.Copy).then_inc(*act_m.did(f"tr{n}"))
                            elif head == "akv":
                                S.activation(AT[:, s, :, :, :].rearrange("p a d n -> p (a d n)"), ps[:, 4 + h, :],
                                             ACT.Copy).then_inc(*act_m.did(f"akv{n}"))
                            elif head == "U":
                                S.activation(Us[:, :, :].rearrange("p d n -> p (d n)"), ps[:, 6, 0:256],
                                             ACT.Copy).then_inc(*act_m.did(f"U{n}"))
                                for d in range(2):
                                    at = chunk_at(n, d) // CH
                                    last = S.activation(Zs[:, d, :], Z[:, d, :], ACT.Copy, scale=Pn[:, d, at:at + 1])
                                last.then_inc(*act_m.did(f"Zs{n}"))
                            elif head == "Y":
                                if n == CCH:
                                    act.wait_ge(o_dve.sem, o_dve.at("gated", j))
                                for d in range(2):
                                    at = chunk_at(n, d) - CTX
                                    for hh in range(2):
                                        rows = slice(64 * hh, 64 * hh + 64)
                                        last = S.activation(Y[rows, d, at:at + CH],
                                                            ps[rows, 7, d * P + 64 * hh:d * P + 64 * hh + 64], ACT.Copy)
                                last.then_inc(*act_m.did(f"Y{n}"))
                    output(N).then_inc(*o_act.did("root"))

                @block.vector
                def _(dve):
                    chunks = "p (c t) -> p c t"

                    def feature(x, j, u, par):
                        PJ, sg, ex, Pi, bon = PJ2[:, u], SG[:, u], EX[:, u], PI[:, u], BON[:, u]
                        FB, FK, FA, v = sg, Pi, ex, V2[:, u]

                        def own(name):
                            dve.wait_ge(f_dve.sem, f_dve.at(name, j))

                        def sc(name):
                            dve.wait_ge(f_act.sem, f_act.at(name, j))

                        d = int(x[-1]) if x[-1] in "01" else 0
                        if x == "pj":
                            return V.tensor_copy(PJ[:, 0:9], par)
                        if x == "omka":
                            own("pj")
                            return V.tensor_scalar(PJ[:, 9:10], PJ[:, 5:6], -1.0, 1.0, ALU.mult, ALU.add)
                        if x == "kkr":
                            dve.wait_ge(s_k, (j + 1) * 32)
                            return V.tensor_scalar(t1[:, :], k[:, :], PJ[:, 4:5], None, ALU.mult)
                        if x == "sq":
                            own("kkr")
                            return V.tensor_tensor(t1[:, :], t1[:, :], t1[:, :], ALU.mult)
                        if x == "max":
                            sc("root1")
                            return V.tensor_scalar(kk[:, :], kk[:, :], 1e-12, None, ALU.max)
                        if x == "rec":
                            own("max")
                            return V.reciprocal(kk[:, :], kk[:, :])
                        if x == "kkn":
                            own("rec")
                            return V.tensor_tensor(kk[:, :], kk[:, :], k[:, :], ALU.mult)
                        if x == "kk":
                            own("kkn")
                            return V.tensor_scalar(kk[:, :], kk[:, :], PJ[:, 4:5], None, ALU.mult)
                        if x in ("scan0", "scan1"):
                            sc(f"w{d}.1")
                            return V.tensor_tensor_scan(cs[:, d, :], self.con("scan", 0, TOK), sg[:, d, :], 0.0,
                                                        ALU.mult, ALU.add)
                        if x == "ex0":
                            own("scan0")
                            return V.tensor_tensor(ex[:, 0, :], cs[:, 0, :], sg[:, 0, :], ALU.subtract)
                        if x == "ex1":
                            own("scan1")
                            c1 = cs[:, 1, :].rearrange(chunks, t=CH)
                            return V.tensor_tensor(ex[:, 1, :].rearrange(chunks, t=CH),
                                                   c1[:, :, CH - 1:CH].broadcast_to([P, NCH, CH]), c1, ALU.subtract)
                        if x == "in1":
                            own("ex1")
                            return V.tensor_tensor(cs[:, 1, :], ex[:, 1, :], sg[:, 1, :], ALU.add)
                        if x in ("A0", "A1"):
                            sc(f"Px{d}")
                            return V.tensor_tensor(FA[:, d, :], ex[:, d, :], kk[:, :], ALU.mult)
                        if x in ("kka0", "kka1"):
                            own("in1")
                            return V.tensor_tensor(FB[:, d, :], a[:, d, :], kk[:, :], ALU.mult)
                        if x in ("B0", "B1"):
                            own(f"kka{d}")
                            sc(f"Pi{d}")
                            return V.tensor_tensor(FB[:, d, :], FB[:, d, :], Pi[:, d, :], ALU.mult)
                        if x in ("kd0", "kd1"):
                            own(f"kka{d}")
                            return V.tensor_scalar(a[:, d, :], a[:, d, :], PJ[:, 5:6], PJ[:, 9:10], ALU.mult, ALU.add)
                        if x in ("kdk0", "kdk1"):
                            own(f"kd{d}")
                            return V.tensor_tensor(a[:, d, :], a[:, d, :], k[:, :], ALU.mult)
                        if x in ("K0", "K1"):
                            own(f"kdk{d}")
                            own(f"B{d}")
                            return V.tensor_tensor(FK[:, d, :], a[:, d, :], Pi[:, d, :], ALU.mult)
                        if x in ("R0", "R1"):
                            sc("P")
                            return V.tensor_tensor(FR2[:, u, d, :], cs[:, d, CTX:TOK], r[:, :], ALU.mult)
                        if x == "rr":
                            own("R1")
                            return V.tensor_scalar(r[:, :], r[:, :], PJ[:, 6:7], None, ALU.mult)
                        if x == "kds":
                            return V.tensor_tensor(bon, a[:, 0, CTX:TOK], a[:, 1, CTX:TOK], ALU.add)
                        if x == "coefin":
                            own("kds")
                            return V.tensor_tensor(t1[:, 0:SEQ], r[:, :], bon, ALU.mult)
                        assert x == "bonus"
                        dve.wait_ge(lin.sem, lin.at("coef", j))
                        dve.wait_ge(s_v, (j + 1) * 16)
                        return V.tensor_tensor(bon, ps[:, 7, :], v[:, CTX:TOK], ALU.mult)

                    def output(x, j, u, dst):
                        PJ, bon = PJ2[:, 1 - u], BON[:, 1 - u]
                        y, t = Y[:, 0, :], t1[:, 0:SEQ]

                        def out(name):
                            dve.wait_ge(o_dve.sem, o_dve.at(name, j))

                        if x == "Y":
                            dve.wait_ge(act_m.sem, act_m.at(f"Y{NCH - 1}", j - 1))
                            return V.tensor_tensor(y, Y[:, 0, :], Y[:, 1, :], ALU.add)
                        if x == "yc":
                            dve.wait_ge(o_pe.sem, o_pe.at("mean", j))
                            return V.tensor_tensor(Y[:, 1, :], y, ps[:, 7, :], ALU.subtract)
                        if x == "sq":
                            out("yc")
                            return V.tensor_tensor(t, Y[:, 1, :], Y[:, 1, :], ALU.mult)
                        if x == "rec":
                            dve.wait_ge(o_act.sem, o_act.at("root", j))
                            return V.reciprocal(t, t)
                        if x == "yn":
                            out("rec")
                            return V.tensor_tensor(t, t, Y[:, 1, :], ALU.mult)
                        if x == "affine":
                            out("yn")
                            return V.tensor_scalar(t, t, PJ[:, 7:8], PJ[:, 8:9], ALU.mult, ALU.add)
                        if x == "bonus":
                            out("affine")
                            return V.tensor_tensor(t, t, bon, ALU.add)
                        out("bonus")
                        return V.tensor_tensor(dst, t, GT[:, 1 - u], ALU.mult)

                    for x in (Y[:, :, :], GT[:, 1], BON[:, 1], PJ2[:, 1]):
                        V.memset(x, 0.0).then_inc(s_blank, 1)
                    dve.wait_ge(s_blank, 4)
                    b0 = COLS["pair"][0]
                    dve.wait_ge(s_mask, 16)
                    for x in feats:
                        if x[0] == "D":
                            feature(x[1:], 0, 0, self.par[:, b0:b0 + 9]).then_inc(*f_dve.did(x[1:]))
                    with dve.Fori(0, N // 2) as jj:
                      for u in range(2):
                        j = jj * 2 + u
                        Pn, PJ, bon = PE2[:, u], PJ2[:, u], BON[:, u]

                        def mine(name):
                            dve.wait_ge(dve_m.sem, dve_m.at(name, j))

                        def four(x):
                            return x.rearrange("p (a b n) -> p a b n", a=2, b=2)

                        mL = self.con("mL", 0, 12 * P).rearrange("p (l d n) -> p l d n", l=6, d=2)
                        for kind, x in plan:
                            if kind == "feature":
                                if x == "Dpj":
                                    dve.wait_ge(pool_m.sem, pool_m.trips(j))
                                if x[0] == "D":
                                    feature(x[1:], j + 1, 1 - u, self.par[:, ds((j + 1) * 9 + b0, 9)]).then_inc(
                                        *f_dve.did(x[1:]))
                                continue
                            if kind == "output":
                                if x[0] == "D":
                                    output(x[1:], j, u, YG[:, ds(jj + 4 * u, 1), :].rearrange(
                                        "p a n -> p (a n)")).then_inc(*o_dve.did(x[1:]))
                                continue
                            head, rest = x.rstrip("0123456789."), x[len(x.rstrip("0123456789.")):]
                            if head not in dve_of:
                                continue
                            n = int(rest.split(".")[-1])
                            i = int(rest[0]) if "." in rest else 0
                            s, h = n % SETS, n % 2
                            if x == "score0":
                                dve.wait_ge(pe_m.sem, pe_m.at(order[-1], j - 1))
                                dve.wait_ge(act_m.sem, act_m.trips(j))
                                dve.wait_ge(dve_m.sem, dve_m.trips(j))
                                V.memset(Z[:, :, :], 0.0).then_inc(s_restart, 1)
                            dve.wait_ge(pe_m.sem, pe_m.at(x, j))
                            if head == "score":
                                nr = 2 if lat(n) else 1
                                for name, bank, mask, o in ((f"sS{n}", 2 * h, "mS", 0), (f"sK{n}", 2 * h + 1, "mK", 2)):
                                    V.tensor_tensor(LK[:, s, :, o:o + nr, :], four(ps[:, bank, :])[:, :, 0:nr, :],
                                                    four(self.con(mask, 0, 4 * P))[:, :, 0:nr, :],
                                                    ALU.mult).then_inc(*dve_m.did(name))
                            elif head == "L":
                                V.tensor_tensor(TB[:, s, :, 0, :], ps[:, 2 * h, 0:256].rearrange("p (d n) -> p d n", d=2),
                                                mL[:, 0, :, :], ALU.mult).then_inc(*dve_m.did(f"t0a{n}"))
                                mine(f"sS{n}")
                                for d in range(2):
                                    last = V.tensor_tensor(TB[:, s, d, 1, :], LK[:, s, d, 0, :], mL[:, 0, 1 - d, :], ALU.mult)
                                last.then_inc(*dve_m.did(f"t0b{n}"))
                                mine(f"t0b{n}")
                                V.tensor_tensor(TB[:, s], TB[:, s],
                                                self.con("id").unsqueeze(1).unsqueeze(1).broadcast_to([P, 2, 2, P]),
                                                ALU.add).then_inc(*dve_m.did(f"t0.{n}"))
                            elif head == "X":
                                V.tensor_tensor(Xs[:, h], ps[:, 2 * h, 0:256].rearrange("p (d n) -> p d n", d=2),
                                                mL[:, i + 1, :, :], ALU.mult).then_inc(*dve_m.did(f"x{i}.{n}"))
                            elif head == "T":
                                lo = 0 if i < LAST else 1
                                V.tensor_tensor(TB[:, s, :, lo:2, :], TB[:, s, :, lo:2, :],
                                                four(ps[:, 2 * h + 1, :])[:, :, lo:2, :],
                                                ALU.add).then_inc(*dve_m.did(f"t{i + 1}.{n}"))
                            elif head == "Z":
                                dve.wait_ge(act_m.sem, act_m.at(f"Zs{n}", j))
                                if lat(n):
                                    dve.wait_ge(pe_m.sem, pe_m.at(f"Y{n}", j))
                                for d in range(2):
                                    at = chunk_at(n, d) // CH
                                    last = V.scalar_tensor_tensor(out=Z[:, d, :], in0=ps[:, 6, (2 + d) * P:(3 + d) * P],
                                                                  scalar=Pn[:, d, at:at + 1], in1=Zs[:, d, :],
                                                                  op0=ALU.mult, op1=ALU.add)
                                last.then_inc(*dve_m.did(f"z{n}"))

                    for x in outs:
                        if x[0] == "D":
                            output(x[1:], N, 0, YG[:, 0, :]).then_inc(*o_dve.did(x[1:]))

    def residual(self, name, src, n, m_tiles, k_tiles, moving, layer, gate, alpha, load_x=None, scale=None):
        nc, ring, ps, X = self.nc, self.ring, self.ps, self.X
        T = X if alpha is None else self.T
        V = nc.vector
        width = m_tiles * k_tiles * P
        s_a = self.sem(name + "_scaled") if alpha is not None else None
        s_x = self.sem(name + "_x_in") if load_x is not None else None
        with nc.Block() as block:
            @block.sync
            def _(sp):
                if load_x is not None:
                    sp.dma_start(X[:, :, :], load_x).then_inc(s_x, 16)
                load_chunks(sp, ring, src, n, width)

            @block.tensor
            def _(pe):
                project(pe, ring, ps, n, m_tiles, k_tiles, moving)

            @block.scalar
            def _(act):
                if load_x is not None:
                    act.wait_ge(s_x, 16)
                if alpha is not None:
                    nc.scalar.activation(T[:, :, :], X[:, :, :], ACT.Copy, scale=alpha).then_inc(s_a, 1)

            @block.vector
            def _(dve):
                if alpha is not None:
                    dve.wait_ge(s_a, 1)

                def body(s, trip, c):
                    dve.wait_ge(ring.used[s], ring.used_at(s, trip))
                    for m in range(m_tiles):
                        t = T[:, ds(c * m_tiles + m, 1), :].rearrange("p a n -> p (a n)")
                        g = self.mod[:, layer, ds(c * m_tiles + (gate + m), 1), 0:1].rearrange("p a b -> p (a b)")
                        last = V.scalar_tensor_tensor(out=t, in0=ps[:, 2 * s + m, :], scalar=g, in1=t,
                                                      op0=ALU.mult, op1=ALU.add)
                    last.then_inc(ring.drained[s], 1)

                over_chunks(dve, n, body)
        ring.end(n)

    def split_features(self, act, dve, HH, HL):
        H = self.H
        for k in range(KT):
            if act is not None:
                self.nc.scalar.activation(HH[:, k, :], H[:, k, :], ACT.Copy).then_inc(self.s_hi, 1)
            if dve is not None:
                dve.wait_ge(self.s_hi, self.parted + k + 1)
                self.nc.vector.tensor_tensor(HL[:, k, :], H[:, k, :], HH[:, k, :].bitcast(F32), ALU.subtract).then_inc(
                    self.s_lo, 1)

    def norm(self, name, src, gamma, beta, layer, scale, shift, center=True):
        nc, ps, X, H, mod = self.nc, self.ps, self.X, self.H, self.mod
        V, S = nc.vector, nc.scalar
        tiles = range(KT)
        pe_m = self.marks(name + "_pe", ["mean"] * center + ["var"])
        act_m = self.marks(name + "_act", [f"q{k}" for k in tiles] + ["root"] + [f"x{k}" for k in tiles] * center)
        dve_m = self.marks(name + "_dve", [f"c{k}" for k in tiles] * center + ["gs"] * (not center) + ["rec"]
                           + [f"n{k}" for k in tiles] + [f"h{k}" for k in tiles])
        with ExitStack() as st:
            SQ, R = self.sb(st, name + "sq", KT, SEQ), self.sb(st, name + "r", SEQ)
            gs = self.sb(st, name + "gs", KT)
            with nc.Block() as block:
                @block.tensor
                def _(pe):
                    if center:
                        for k in tiles:
                            last = pe.matmul(ps[:, 6, :], self.con("mean"), src[:, k, :], start=(k == 0), stop=(k == KT - 1))
                        last.then_inc(*pe_m.did("mean"))
                    for k in tiles:
                        pe.wait_ge(act_m.sem, act_m.at(f"q{k}"))
                        last = pe.matmul(ps[:, 7, :], self.con("mean"), SQ[:, k, :], start=(k == 0), stop=(k == KT - 1))
                    last.then_inc(*pe_m.did("var"))

                @block.scalar
                def _(act):
                    for k in tiles:
                        if center:
                            act.wait_ge(dve_m.sem, dve_m.at(f"c{k}"))
                        S.activation(SQ[:, k, :], src[:, k, :], ACT.Square).then_inc(*act_m.did(f"q{k}"))
                    act.wait_ge(pe_m.sem, pe_m.at("var"))
                    S.activation(R[:, :], ps[:, 7, :], ACT.Sqrt, bias=self.tiny[:, 0:1] if center else self.tiny[:, 2:3]).then_inc(
                        *act_m.did("root"))
                    if center:
                        for k in tiles:
                            act.wait_ge(dve_m.sem, dve_m.at(f"n{k}"))
                            S.activation(X[:, k, :], src[:, k, :], ACT.Identity, bias=beta[:, k:k + 1],
                                         scale=gamma[:, k:k + 1]).then_inc(*act_m.did(f"x{k}"))

                @block.vector
                def _(dve):
                    if center:
                        dve.wait_ge(pe_m.sem, pe_m.at("mean"))
                        for k in tiles:
                            V.tensor_tensor(src[:, k, :], src[:, k, :], ps[:, 6, :], ALU.subtract).then_inc(
                                *dve_m.did(f"c{k}"))
                    else:
                        V.tensor_tensor(gs[:, :], gamma, mod[:, layer, scale:scale + KT, 0], ALU.mult).then_inc(
                            *dve_m.did("gs"))
                    dve.wait_ge(act_m.sem, act_m.at("root"))
                    V.reciprocal(R[:, :], R[:, :]).then_inc(*dve_m.did("rec"))
                    dve.wait_ge(dve_m.sem, dve_m.at("rec"))
                    for k in tiles:
                        dst = src if center else H
                        V.tensor_tensor(dst[:, k, :], src[:, k, :], R[:, :], ALU.mult).then_inc(*dve_m.did(f"n{k}"))
                    for k in tiles:
                        if center:
                            dve.wait_ge(act_m.sem, act_m.at(f"x{k}"))
                        else:
                            dve.wait_ge(dve_m.sem, dve_m.at(f"n{k}"))
                        V.tensor_scalar(H[:, k, :], X[:, k, :] if center else H[:, k, :],
                                        mod[:, layer, scale + k, 0:1] if center else gs[:, k:k + 1],
                                        mod[:, layer, shift + k, 0:1], ALU.mult, ALU.add).then_inc(*dve_m.did(f"h{k}"))

    def rwkv_out(self):
        self.residual("wo", self.A["w_o"], 4, 2, KT, lambda k: self.B0[:, self.pair_tile(k), :], 0, 16, ALPHA, load_x=self.A["xT"])
        self.norm("ln00", self.T, self.col("lng", 0, 8), self.col("lnb", 0, 8), 0, 32, 24)

    def ffn(self):
        nc, ring, ps, H = self.nc, self.ring, self.ps, self.H
        silu_m = [self.sem(f"ffn_silu{s}") for s in range(SLOTS)]
        s_zero = self.sem("rows_zeroed")
        with ExitStack() as st:
            HID, G = self.sb(st, "hid", FT, SEQ), self.sb(st, "silu", SLOTS, SEQ)
            up_split = ExitStack()
            split = Split(nc, up_split, ring, "ffn_up", 2 * KT * P)
            HH, HL = (up_split.enter_context(nc.sbuf_tensor(f"sb_ffn_{q}", [P, KT, SEQ], F32R)) for q in ("hh", "hl"))
            with nc.Block() as block:
                @block.sync
                def _(sp):
                    load_chunks(sp, ring, self.A["w_ffn13"], FT, 2 * KT * P)

                @block.gpsimd
                def _(pool):
                    with pool.Fori(0, ITEMS + 2) as i:
                        pool.dma_start(self.A["x_rows"][ds(i * P, P), :], self.A["zeros"][:, 0:D]).then_inc(s_zero, 16)
                    with pool.Fori(NE, ITEMS) as i:
                        pool.dma_start(self.A["y_rows"][ds(i * P, P), :], self.A["zeros"][:, 0:D]).then_inc(s_zero, 16)
                    pool.wait_ge(s_zero, 16 * (ITEMS + 2 + ITEMS - NE))

                @block.tensor
                def _(pe):
                    pe.wait_ge(self.s_lo, self.parted + KT)
                    split.project(pe, ps, FT, 2, KT, lambda k: HH[:, k, :], lambda k: HL[:, k, :])

                @block.scalar
                def _(act):
                    self.split_features(act, None, HH, HL)
                    split.leading(act, 0, 0)

                    def body(s, trip, c):
                        with_next(FT, s, trip, c, lambda s1, t1: split.leading(act, s1, t1))
                        act.wait_ge(ring.used[s], ring.used_at(s, trip))
                        act.wait_ge(ring.drained[s], ring.drained_at(s, trip - 1))
                        nc.scalar.activation(G[:, s, :], ps[:, 2 * s, :], ACT.Silu).then_inc(silu_m[s], 1)

                    over_chunks(act, FT, body)

                @block.vector
                def _(dve):
                    self.split_features(None, dve, HH, HL)
                    split.rest(dve, 0, 0)

                    def body(s, trip, c):
                        with_next(FT, s, trip, c, lambda s1, t1: split.rest(dve, s1, t1))
                        dve.wait_ge(silu_m[s], trip + 1)
                        nc.vector.tensor_tensor(HID[:, ds(c, 1), :].rearrange("p a n -> p (a n)"), G[:, s, :],
                                                ps[:, 2 * s + 1, :], ALU.mult).then_inc(ring.drained[s], 1)

                    over_chunks(dve, FT, body)
            up_split.close()
            split.end(FT)
            self.parted += KT
            self.T = self.right(self.t, "t_again")
            self.residual("ffn2", self.A["w_ffn2"], KT, 1, FT, lambda k: HID[:, k, :], 0, 40, ALPHA)
        self.norm("ln01", self.T, self.col("lng", 8, 8), self.col("lnb", 8, 8), 1, 8, 0)

    def pool(self):
        nc, ring, ps, X, T, H = self.nc, self.ring, self.ps, self.X, self.T, self.H
        V = nc.vector
        R, WIDE = SEQ // GRID_W, GRID_W + 2 * PADW
        s_w, s_pe, s_a, s_g = (self.sem(f"pool_{q}") for q in ("w", "done", "scaled", "gate"))
        dve_m = self.marks("pool_dve", ["zero", "pad", "s2", "s4", "s8", "s16", "mean0", "mean1", "mean2", "mean3", "pooled", "gps"])
        Q = self.B0
        with ExitStack() as st:
            pads = [self.sb(st, f"pad{i}", KT, R, WIDE) for i in range(2)]
            gps = self.sb(st, "gps", KT)
            with nc.Block() as block:
                @block.sync
                def _(sp):
                    sp.dma_start(ring.buf[0][:, 0:2048], self.A["w_pool"]).then_inc(s_w, 16)

                @block.scalar
                def _(act):
                    nc.scalar.activation(T[:, :, :], X[:, :, :], ACT.Copy, scale=ALPHA).then_inc(s_a, 1)

                @block.tensor
                def _(pe):
                    pe.wait_ge(s_w, 16)
                    pe.wait_ge(dve_m.sem, dve_m.at("pooled"))
                    for g in range(4):
                        for m in range(2):
                            for k in range(2):
                                at = (g * 4 + k * 2 + m) * P
                                last = pe.matmul(ps[:, 2 * g + m, :], ring.buf[0][:, at:at + P], Q[:, 2 * g + k, :],
                                                 start=(k == 0), stop=(k == 1))
                            last.then_inc(s_pe, 1)

                @block.vector
                def _(dve):
                    def mine(name):
                        dve.wait_ge(dve_m.sem, dve_m.at(name))

                    def grid(x):
                        return x.rearrange("p k (r c) -> p k r c", c=GRID_W)

                    V.memset(pads[0][:, :, :, :], 0.0).then_inc(*dve_m.did("zero"))
                    mine("zero")
                    for k in range(KT):
                        last = V.tensor_copy(pads[0][:, k, :, PADW:PADW + GRID_W],
                                             H[:, k, :].rearrange("p (r c) -> p r c", c=GRID_W))
                    last.then_inc(*dve_m.did("pad"))
                    prev = "pad"
                    for i, (lo, back, ahead) in enumerate(((1, 1, 0), (2, 1, 1), (4, 2, 2), (8, 4, 4))):
                        a, b = pads[i % 2], pads[(i + 1) % 2]
                        hi = WIDE - ahead - (0, 1, 2, 4)[i]
                        mine(prev)
                        for k in range(2 * i, KT):
                            last = V.tensor_tensor(b[:, k, :, lo:hi], a[:, k, :, lo - back:hi - back],
                                                   a[:, k, :, lo + ahead:hi + ahead], ALU.add)
                        prev = f"s{2 ** (i + 1)}"
                        last.then_inc(*dve_m.did(prev))
                        if i == 3:
                            break
                    mine("s16")
                    for g in range(4):
                        src = pads[(g + 1) % 2]
                        for k in (2 * g, 2 * g + 1):
                            o = Q[:, k, :].rearrange("p (r c) -> p r c", c=GRID_W)
                            last = V.tensor_tensor(o, src[:, k, :, PADW:PADW + GRID_W],
                                                   self.con("rcnt", g * GRID_W, GRID_W).unsqueeze(1).broadcast_to(
                                                       [P, R, GRID_W]), ALU.mult)
                        last.then_inc(*dve_m.did(f"mean{g}"))
                    mine("mean3")
                    V.tensor_tensor(Q[:, :, :], Q[:, :, :], H[:, :, :], ALU.subtract).then_inc(*dve_m.did("pooled"))
                    V.tensor_tensor(gps[:, :], self.col("pscale", 0, 8), self.mod[:, 1, 16:24, 0], ALU.mult).then_inc(
                        *dve_m.did("gps"))
                    mine("gps")
                    dve.wait_ge(s_a, 1)
                    for m in range(KT):
                        dve.wait_ge(s_pe, m + 1)
                        V.scalar_tensor_tensor(out=T[:, m, :], in0=ps[:, m, :], scalar=gps[:, m:m + 1], in1=T[:, m, :],
                                               op0=ALU.mult, op1=ALU.add)
        self.norm("ln10", T, self.col("lng", 16, 8), self.col("lnb", 16, 8), 1, 32, 24)

    def moe(self):
        with ExitStack() as st:
            self.row_at = st.enter_context(self.nc.sbuf_tensor("sb_row_at", [P, TT, 2], I32))
            self.items = st.enter_context(self.nc.sbuf_tensor("sb_items", [P, ITEMS + 1], I32))
            self.gates = self.sb(st, "gates", TT, 2)
            self.spread()
            self.experts()
            self.collect()
        self.norm("ln11", self.T, self.col("lng", 24, 8), self.col("lnb", 24, 8), 1, 8, 0)

    def spread(self):
        nc, A, ps, H = self.nc, self.A, self.ps, self.H
        V, S = nc.vector, nc.scalar
        HT = self.T
        s_w, s_l = self.sem("router_in"), self.sem("logits")
        dve_m = self.marks("router_dve", ["lg", "gt", "eq", "eqlow", "beats", "rank", "first", "sel", "second", "max",
                                          "shift", "num", "den", "rec", "gate", "ga0", "ga1", "gb0", "gates",
                                          "pre", "cnt", "gtc", "nt", "excl", "start", "start128", "end", "total",
                                          "ge", "exp_of", "expert", "row", "ra0", "ra1", "rb0", "rb1", "rows"])
        act_m = self.marks("router_act", ["exp"])
        s_pre, s_tr, s_ht = self.sem("prefix"), self.sem("h_turned"), self.sem("h_rows")
        s_spread = self.sem("rows_spread")
        with ExitStack() as st:
            L = self.sb(st, "logit", TT, NE)
            cmp, eq = self.sb(st, "cmp", TT, NE, NE), self.sb(st, "eqs", TT, NE, NE)
            rank, E, Z, mx, first, second, sel, row, tmp = (
                self.sb(st, n, TT, NE) for n in ("rank", "rexp", "rz", "rmx", "sel1", "sel2", "sel", "rrow", "rtmp"))
            tmp2, tmp3, tmp4 = (self.sb(st, n, TT, NE) for n in ("rtmp2", "rtmp3", "rtmp4"))
            rowf = self.sb(st, "rowf", TT, 2)
            rw, rb, low = self.sb(st, "rw", KT * NE), self.sb(st, "rb", NE), self.sb(st, "low", NE * NE)
            before, steps = self.sb(st, "before", P), self.sb(st, "steps", 4 + ITEMS)
            cnt, nt, start, end = (self.sb(st, n, NE) for n in ("rcntx", "rnt", "rstart", "rend"))
            c4, c8 = self.sb(st, "c4", NE, 4), self.sb(st, "c8", NE, NE)
            ge, it = self.sb(st, "rge", ITEMS, NE), self.sb(st, "ritem", ITEMS + 1)
            with nc.Block() as block:
                @block.sync
                def _(sp):
                    sp.dma_start(rw[:, :], A["w_router"]).then_inc(s_w, 16)
                    sp.dma_start(rb[:, :], A["router_b"].broadcast_to([P, NE])).then_inc(s_w, 16)
                    sp.dma_start(low[:, :], A["tie_mask"].broadcast_to([P, NE * NE])).then_inc(s_w, 16)
                    sp.dma_start(before[:, :], A["before"]).then_inc(s_w, 16)
                    sp.dma_start(steps[:, :], A["steps"].broadcast_to([P, 4 + ITEMS])).then_inc(s_w, 16)

                @block.tensor
                def _(pe):
                    pe.wait_ge(s_w, 80)
                    for t in range(TT):
                        for k in range(KT):
                            last = pe.matmul(ps[:, 6, t * NE:(t + 1) * NE], H[:, k, t * P:(t + 1) * P],
                                             rw[:, k * NE:(k + 1) * NE], start=(k == 0), stop=(k == KT - 1))
                    last.then_inc(s_l, 1)
                    for t in range(TT):
                        for g in range(2):
                            n = 2 * t + g
                            if n >= 4:
                                pe.wait_ge(s_ht, n - 3)
                            for k in range(4):
                                last = pe.transpose(ps[:, n % 4, k * P:(k + 1) * P], H[:, 4 * g + k, t * P:(t + 1) * P],
                                                    self.con("id"))
                            last.then_inc(s_tr, 1)
                    pe.wait_ge(dve_m.sem, dve_m.at("sel"))
                    for t in range(TT):
                        for u in range(t + 1):
                            last = pe.matmul(ps[:, 7, t * NE:(t + 1) * NE], before[:, :] if u == t else self.con("ones"),
                                             sel[:, u, :], start=(u == 0), stop=(u == t))
                    for u in range(TT):
                        last = pe.matmul(ps[:, 7, TT * NE:(TT + 1) * NE], self.con("ones"), sel[:, u, :],
                                         start=(u == 0), stop=(u == TT - 1))
                    last.then_inc(s_pre, 1)

                @block.scalar
                def _(act):
                    for n in range(4):
                        act.wait_ge(s_tr, n + 1)
                        S.activation(HT[:, n, :], ps[:, n % 4, :], ACT.Copy).then_inc(s_ht, 1)
                    act.wait_ge(dve_m.sem, dve_m.at("shift"))
                    S.activation(E[:, :, :], Z[:, :, :], ACT.Exp).then_inc(*act_m.did("exp"))
                    for n in range(4, 8):
                        act.wait_ge(s_tr, n + 1)
                        S.activation(HT[:, n, :], ps[:, n % 4, :], ACT.Copy).then_inc(s_ht, 1)

                @block.vector
                def _(dve):
                    def mine(name):
                        dve.wait_ge(dve_m.sem, dve_m.at(name))

                    full = [P, TT, NE, NE]
                    dve.wait_ge(s_l, 1)
                    V.tensor_tensor(L[:, :, :], ps[:, 6, 0:TT * NE].rearrange("p (t e) -> p t e", e=NE),
                                    rb[:, :].unsqueeze(1).broadcast_to([P, TT, NE]), ALU.add).then_inc(*dve_m.did("lg"))
                    mine("lg")
                    other = L[:, :, :].unsqueeze(2).broadcast_to(full)
                    own = L[:, :, :].unsqueeze(3).broadcast_to(full)
                    V.tensor_tensor(cmp[:, :, :, :], other, own, ALU.is_gt).then_inc(*dve_m.did("gt"))
                    V.tensor_tensor(eq[:, :, :, :], other, own, ALU.is_equal).then_inc(*dve_m.did("eq"))
                    mine("eq")
                    tie = low[:, :].rearrange("p (a b) -> p a b", b=NE).unsqueeze(1).broadcast_to(full)
                    V.tensor_tensor(eq[:, :, :, :], eq[:, :, :, :], tie, ALU.mult).then_inc(*dve_m.did("eqlow"))
                    mine("eqlow")
                    V.tensor_tensor(cmp[:, :, :, :], cmp[:, :, :, :], eq[:, :, :, :], ALU.add).then_inc(*dve_m.did("beats"))
                    mine("beats")
                    V.tensor_reduce(rank[:, :, :], cmp[:, :, :, :], AX, ALU.add).then_inc(*dve_m.did("rank"))
                    mine("rank")
                    V.tensor_scalar(first[:, :, :], rank[:, :, :], 0.5, None, ALU.is_lt).then_inc(*dve_m.did("first"))
                    V.tensor_scalar(sel[:, :, :], rank[:, :, :], 1.5, None, ALU.is_lt).then_inc(*dve_m.did("sel"))
                    mine("sel")
                    V.tensor_tensor(second[:, :, :], sel[:, :, :], first[:, :, :], ALU.subtract).then_inc(
                        *dve_m.did("second"))
                    V.tensor_reduce(mx[:, :, 0:1], L[:, :, :], AX, ALU.max).then_inc(*dve_m.did("max"))
                    mine("max")
                    V.tensor_tensor(Z[:, :, :], L[:, :, :], mx[:, :, 0:1].broadcast_to([P, TT, NE]),
                                    ALU.subtract).then_inc(*dve_m.did("shift"))
                    dve.wait_ge(act_m.sem, act_m.at("exp"))
                    V.tensor_tensor(E[:, :, :], E[:, :, :], sel[:, :, :], ALU.mult).then_inc(*dve_m.did("num"))
                    mine("num")
                    V.tensor_reduce(mx[:, :, 1:2], E[:, :, :], AX, ALU.add).then_inc(*dve_m.did("den"))
                    mine("den")
                    V.reciprocal(mx[:, :, 1:2], mx[:, :, 1:2]).then_inc(*dve_m.did("rec"))
                    mine("rec")
                    V.tensor_tensor(E[:, :, :], E[:, :, :], mx[:, :, 1:2].broadcast_to([P, TT, NE]), ALU.mult).then_inc(
                        *dve_m.did("gate"))
                    mine("gate")
                    V.tensor_tensor(tmp[:, :, :], E[:, :, :], first[:, :, :], ALU.mult).then_inc(*dve_m.did("ga0"))
                    V.tensor_tensor(tmp2[:, :, :], E[:, :, :], second[:, :, :], ALU.mult).then_inc(*dve_m.did("ga1"))
                    mine("ga1")
                    V.tensor_reduce(self.gates[:, :, 0:1], tmp[:, :, :], AX, ALU.add).then_inc(*dve_m.did("gb0"))
                    V.tensor_reduce(self.gates[:, :, 1:2], tmp2[:, :, :], AX, ALU.add).then_inc(*dve_m.did("gates"))
                    dve.wait_ge(s_pre, 1)
                    V.tensor_copy(row[:, :, :], ps[:, 7, 0:TT * NE].rearrange("p (t e) -> p t e", e=NE)).then_inc(
                        *dve_m.did("pre"))
                    V.tensor_copy(cnt[:, :], ps[:, 7, TT * NE:(TT + 1) * NE]).then_inc(*dve_m.did("cnt"))
                    mine("cnt")
                    V.tensor_tensor(c4[:, :, :], cnt[:, :].unsqueeze(2).broadcast_to([P, NE, 4]),
                                    steps[:, 0:4].unsqueeze(1).broadcast_to([P, NE, 4]), ALU.is_gt).then_inc(
                        *dve_m.did("gtc"))
                    mine("gtc")
                    V.tensor_reduce(nt[:, :], c4[:, :, :], AX, ALU.add).then_inc(*dve_m.did("nt"))
                    mine("nt")
                    V.tensor_tensor(c8[:, :, :], nt[:, :].unsqueeze(1).broadcast_to([P, NE, NE]),
                                    low[:, :].rearrange("p (a b) -> p a b", b=NE), ALU.mult).then_inc(*dve_m.did("excl"))
                    mine("excl")
                    V.tensor_reduce(start[:, :], c8[:, :, :], AX, ALU.add).then_inc(*dve_m.did("start"))
                    mine("start")
                    V.tensor_scalar(cnt[:, :], start[:, :], float(P), None, ALU.mult).then_inc(*dve_m.did("start128"))
                    V.tensor_tensor(end[:, :], start[:, :], nt[:, :], ALU.add).then_inc(*dve_m.did("end"))
                    V.tensor_reduce(it[:, ITEMS:ITEMS + 1], nt[:, :], AX, ALU.add).then_inc(*dve_m.did("total"))
                    mine("end")
                    V.tensor_tensor(ge[:, :, :], steps[:, 4:4 + ITEMS].unsqueeze(2).broadcast_to([P, ITEMS, NE]),
                                    end[:, :].unsqueeze(1).broadcast_to([P, ITEMS, NE]), ALU.is_ge).then_inc(
                        *dve_m.did("ge"))
                    mine("ge")
                    V.tensor_reduce(it[:, 0:ITEMS], ge[:, :, :], AX, ALU.add).then_inc(*dve_m.did("exp_of"))
                    mine("exp_of")
                    V.tensor_copy(self.items[:, :], it[:, :]).then_inc(*dve_m.did("expert"))
                    mine("start128")
                    V.tensor_tensor(row[:, :, :], row[:, :, :], cnt[:, :].unsqueeze(1).broadcast_to([P, TT, NE]),
                                    ALU.add).then_inc(*dve_m.did("row"))
                    mine("row")
                    V.tensor_tensor(tmp3[:, :, :], row[:, :, :], first[:, :, :], ALU.mult).then_inc(*dve_m.did("ra0"))
                    V.tensor_tensor(tmp4[:, :, :], row[:, :, :], second[:, :, :], ALU.mult).then_inc(*dve_m.did("ra1"))
                    mine("ra1")
                    V.tensor_reduce(rowf[:, :, 0:1], tmp3[:, :, :], AX, ALU.add).then_inc(*dve_m.did("rb0"))
                    V.tensor_reduce(rowf[:, :, 1:2], tmp4[:, :, :], AX, ALU.add).then_inc(*dve_m.did("rb1"))
                    mine("rb1")
                    V.tensor_copy(self.row_at[:, :, :], rowf[:, :, :]).then_inc(*dve_m.did("rows"))

                @block.gpsimd
                def _(pool):
                    pool.wait_ge(dve_m.sem, dve_m.at("rows"))
                    pool.wait_ge(s_ht, 8)
                    for t in range(TT):
                        for c in range(2):
                            nc.gpsimd.indirect_dma_start(
                                A["x_rows"], IndirectOffsetOnAxis(ap=self.row_at[:, t, c:c + 1], axis=0),
                                self.token_rows(HT, t), None).then_inc(s_spread, 16)
                    pool.wait_ge(s_spread, 16 * 2 * TT)

    def token_rows(self, buf, t):
        return buf[:, 2 * t:2 * t + 2, :].rearrange("p a n -> p (a n)")

    def experts(self):
        nc, A, ring, ps = self.nc, self.A, self.ring, self.ps
        V, S = nc.vector, nc.scalar
        UP, DOWN = FE // HCOL, D // YCOL
        ROUND = UP + DOWN
        assert ROUND % SLOTS == 0 and KT * 2 * HCOL == SLOT and ET * YCOL == SLOT
        HTB = (3, 4, 5)
        XB = (2, 7)
        YB = (6, 7)
        loaded = [self.sem(f"moe_w_loaded{s}") for s in range(SLOTS)]
        s_x, s_y = self.sem("moe_x_in"), self.sem("moe_y_out")
        def trip_marks(name, names):
            return self.marks(name, names, len(names))

        pe_m = trip_marks("moe_pe", [f"up{c}" for c in range(UP)] + ["x0", "x1", "t0", "t1", "t2"]
                          + [f"down{j}" for j in range(DOWN)])
        act_m = trip_marks("moe_act", [f"silu{c}" for c in range(UP)] + ["t0", "t1", "t2"] + [f"y{j}" for j in range(DOWN)])
        dve_m = trip_marks("moe_dve", [f"hid{c}" for c in range(UP)] + ["x0", "x1"])
        pool_m = trip_marks("moe_pool", ["y_written"])
        s_first, s_first_t = self.sem("moe_first_turned"), self.sem("moe_first_copied")
        mark_of = [f"up{c}" if c < UP else f"down{c - UP}" for c in range(ROUND)]
        with ExitStack() as st:
            XI, XG = self.sb(st, "x_in", D), self.sb(st, "x_feat", KT, P)
            G, HR = self.sb(st, "esilu", 2, HCOL), self.sb(st, "hid_rows", FE)
            HF, YO = self.sb(st, "hid_feat", 12, P), self.sb(st, "y_rows_out", D)
            with nc.Block() as block:
                def count(eng):
                    return eng.value_load(self.items[0:1, ITEMS:ITEMS + 1], min_val=NE, max_val=ITEMS)

                @block.sync
                def _(sp):
                    n = count(sp)
                    with sp.Fori(0, n) as i:
                        e = sp.value_load(self.items[0:1, ds(i, 1)], min_val=0, max_val=NE - 1)
                        for c in range(ROUND):
                            s = c % SLOTS
                            if c < SLOTS:
                                sp.wait_ge(pe_m.sem, pe_m.at(mark_of[ROUND + c - SLOTS], i - 1))
                            else:
                                sp.wait_ge(pe_m.sem, pe_m.at(mark_of[c - SLOTS], i))
                            src = (A["w_moe_up"][ds(e * UP + c, 1)] if c < UP else
                                   A["w_moe_down"][ds(e * DOWN + (c - UP), 1)])
                            sp.dma_start(ring.buf[s], src.rearrange("a p n -> (a p) n")).then_inc(loaded[s], 16)

                @block.tensor
                def _(pe):
                    def turn_x(half):
                        for k in range(4):
                            at = (4 * half + k) * P
                            last = pe.transpose(ps[:, XB[half], k * P:(k + 1) * P], XI[:, at:at + P], self.con("id"))
                        return last

                    n = count(pe)
                    pe.wait_ge(s_x, 16)
                    for half in range(2):
                        turn_x(half).then_inc(s_first, 1)
                    pe.wait_ge(s_first_t, 2)
                    with pe.Fori(0, n) as i:
                        for c in range(ROUND):
                            s = c % SLOTS
                            pe.wait_ge(loaded[s], (i * (ROUND // SLOTS) + (c // SLOTS + 1)) * 16)
                            if c == 0:
                                pe.wait_ge(dve_m.sem, dve_m.at("x1", i - 1))
                            if c < UP:
                                if c < 2:
                                    pe.wait_ge(dve_m.sem, dve_m.at(f"hid{UP - 2 + c}", i - 1))
                                else:
                                    pe.wait_ge(dve_m.sem, dve_m.at(f"hid{c - 2}", i))
                                for k in range(KT):
                                    last = pe.matmul(ps[:, c % 2, 0:2 * HCOL], XG[:, k, :],
                                                     ring.buf[s][:, k * 2 * HCOL:(k + 1) * 2 * HCOL],
                                                     start=(k == 0), stop=(k == KT - 1))
                                last.then_inc(*pe_m.did(f"up{c}"))
                            else:
                                j = c - UP
                                if j == 0:
                                    pe.wait_ge(s_x, i * 16 + 32)
                                    pe.wait_ge(act_m.sem, act_m.at(f"y{DOWN - 1}", i - 1))
                                    for half in range(2):
                                        turn_x(half).then_inc(*pe_m.did(f"x{half}"))
                                    for b in range(3):
                                        pe.wait_ge(dve_m.sem, dve_m.at(f"hid{min(UP - 1, ((4 * b + 4) * P - 1) // HCOL)}", i))
                                        for k in range(4 * b, min(4 * b + 4, ET)):
                                            last = pe.transpose(ps[:, HTB[b], (k % 4) * P:(k % 4 + 1) * P],
                                                                HR[:, k * P:(k + 1) * P], self.con("id"))
                                        last.then_inc(*pe_m.did(f"t{b}"))
                                if j == 1:
                                    pe.wait_ge(dve_m.sem, dve_m.at("x1", i))
                                if j < 2:
                                    pe.wait_ge(act_m.sem, act_m.at(f"y{DOWN - 2 + j}", i - 1))
                                else:
                                    pe.wait_ge(act_m.sem, act_m.at(f"y{j - 2}", i))
                                for k in range(ET):
                                    if j == 0 and k % 4 == 0:
                                        pe.wait_ge(act_m.sem, act_m.at(f"t{k // 4}", i))
                                    last = pe.matmul(ps[:, YB[j % 2], 0:YCOL], HF[:, k, :],
                                                     ring.buf[s][:, k * YCOL:(k + 1) * YCOL],
                                                     start=(k == 0), stop=(k == ET - 1))
                                last.then_inc(*pe_m.did(f"down{j}"))

                @block.scalar
                def _(act):
                    n = count(act)
                    with act.Fori(0, n) as i:
                        for c in range(UP):
                            act.wait_ge(pe_m.sem, pe_m.at(f"up{c}", i))
                            S.activation(G[:, c % 2, :], ps[:, c % 2, 0:HCOL], ACT.Silu).then_inc(*act_m.did(f"silu{c}"))
                        for b in range(3):
                            act.wait_ge(pe_m.sem, pe_m.at(f"t{b}", i))
                            w = min(4, ET - 4 * b)
                            S.activation(HF[:, 4 * b:4 * b + w, :], ps[:, HTB[b], 0:w * P].rearrange(
                                "p (k n) -> p k n", n=P), ACT.Copy).then_inc(*act_m.did(f"t{b}"))
                        act.wait_ge(pool_m.sem, pool_m.at("y_written", i - 1))
                        for j in range(DOWN):
                            act.wait_ge(pe_m.sem, pe_m.at(f"down{j}", i))
                            S.activation(YO[:, j * YCOL:(j + 1) * YCOL], ps[:, YB[j % 2], 0:YCOL],
                                         ACT.Copy).then_inc(*act_m.did(f"y{j}"))

                @block.vector
                def _(dve):
                    def copy_x(half):
                        return V.tensor_copy(XG[:, 4 * half:4 * half + 4, :],
                                             ps[:, XB[half], :].rearrange("p (k n) -> p k n", n=P))

                    n = count(dve)
                    for half in range(2):
                        dve.wait_ge(s_first, half + 1)
                        copy_x(half).then_inc(s_first_t, 1)
                    with dve.Fori(0, n) as i:
                        for c in range(UP):
                            dve.wait_ge(act_m.sem, act_m.at(f"silu{c}", i))
                            V.tensor_tensor(HR[:, c * HCOL:(c + 1) * HCOL], G[:, c % 2, :], ps[:, c % 2, HCOL:2 * HCOL],
                                            ALU.mult).then_inc(*dve_m.did(f"hid{c}"))
                        for half in range(2):
                            dve.wait_ge(pe_m.sem, pe_m.at(f"x{half}", i))
                            copy_x(half).then_inc(*dve_m.did(f"x{half}"))

                @block.gpsimd
                def _(pool):
                    for m in (pe_m, act_m, dve_m, pool_m):
                        m.begin(pool)
                    n = count(pool)
                    pool.dma_start(XI[:, :], A["x_rows"][0:P, :]).then_inc(s_x, 16)
                    pool.wait_ge(s_first, 2)
                    pool.dma_start(XI[:, :], A["x_rows"][P:2 * P, :]).then_inc(s_x, 16)
                    with pool.Fori(0, n) as i:
                        pool.wait_ge(pe_m.sem, pe_m.at("x1", i))
                        pool.dma_start(XI[:, :], A["x_rows"][ds((i + 2) * P, P), :]).then_inc(s_x, 16)
                        pool.wait_ge(act_m.sem, act_m.at(f"y{DOWN - 1}", i))
                        pool.dma_start(A["y_rows"][ds(i * P, P), :], YO[:, :]).then_inc(s_y, 16)
                        pool.wait_ge(s_x, i * 16 + 48)
                        pool.wait_ge(s_y, i * 16 + 16)
                        pool.sem_inc(*pool_m.did("y_written"))

    def collect(self):
        nc, A, ps, T, X = self.nc, self.A, self.ps, self.T, self.X
        V, S = nc.vector, nc.scalar
        YA, YB = self.B0, self.H
        s_in = [self.sem(f"moe_back{t}") for t in range(TT)]
        s_t, s_pe = self.sem("moe_T"), self.sem("moe_turned")
        dve_m = self.marks("collect_dve", [f"{q}{t}" for t in range(TT) for q in ("a", "b")])
        with nc.Block() as block:
            @block.gpsimd
            def _(pool):
                for t in range(TT):
                    for c, buf in enumerate((YA, YB)):
                        nc.gpsimd.indirect_dma_start(
                            self.token_rows(buf, t), None, A["y_rows"],
                            IndirectOffsetOnAxis(ap=self.row_at[:, t, c:c + 1], axis=0)).then_inc(s_in[t], 16)

            @block.scalar
            def _(act):
                S.activation(T[:, :, :], X[:, :, :], ACT.Copy, scale=ALPHA).then_inc(s_t, 1)

            @block.tensor
            def _(pe):
                for t in range(TT):
                    pe.wait_ge(dve_m.sem, dve_m.at(f"b{t}"))
                    for m in range(KT):
                        last = pe.transpose(ps[:, m, t * P:(t + 1) * P], YA[:, 2 * t + m // 4, (m % 4) * P:(m % 4 + 1) * P],
                                            self.con("id"))
                        if t == TT - 1:
                            last.then_inc(s_pe, 1)

            @block.vector
            def _(dve):
                for t in range(TT):
                    ya, yb = self.token_rows(YA, t), self.token_rows(YB, t)
                    dve.wait_ge(s_in[t], 32)
                    V.tensor_scalar(ya, ya, self.gates[:, t, 0:1], None, ALU.mult).then_inc(*dve_m.did(f"a{t}"))
                    dve.wait_ge(dve_m.sem, dve_m.at(f"a{t}"))
                    V.scalar_tensor_tensor(out=ya, in0=yb, scalar=self.gates[:, t, 1:2], in1=ya,
                                           op0=ALU.mult, op1=ALU.add).then_inc(*dve_m.did(f"b{t}"))
                dve.wait_ge(s_t, 1)
                for m in range(KT):
                    dve.wait_ge(s_pe, m + 1)
                    V.scalar_tensor_tensor(out=T[:, m, :], in0=ps[:, m, :], scalar=self.mod[:, 1, 40 + m, 0:1],
                                           in1=T[:, m, :], op0=ALU.mult, op1=ALU.add)

    def attention(self):
        nc, A, ring, ps, X, T, H, mod = self.nc, self.A, self.ring, self.ps, self.X, self.T, self.H, self.mod
        V, S = nc.vector, nc.scalar
        self.norm("rms1", X, self.col("n1g", 0, 8), None, 2, 8, 0, center=False)
        with ExitStack() as st:
            QK = self.sb(st, "qk", 16, SEQ)
            VV = self.sb(st, "vv", 2, TT, BANK)
            lam = self.sb(st, "lamv", 8)
            self.qkv(QK, VV, lam)
            O = self.B0
            self.heads(QK, VV, lam, O)
        self.residual("wout", A["w_out"], 4, 2, KT, lambda k: self.B0[:, k, :], 2, 16, 1.0)
        self.move_t_to_x("h1")

    def move_t_to_x(self, name):
        s = self.sem(name + "_moved")
        with self.nc.Block() as block:
            @block.scalar
            def _(act):
                self.nc.scalar.activation(self.X[:, :, :], self.T[:, :, :], ACT.Copy).then_inc(s, 1)

    def qkv(self, QK, VV, lam):
        nc, A, ring, ps, H = self.nc, self.A, self.ring, self.ps, self.H
        V, S = nc.vector, nc.scalar
        NV = 4
        s_vo, s_sq, s_var, s_root, s_rec = (self.sem(f"qkv_{q}") for q in ("vout", "sq", "var", "root", "rec"))
        s_sel, s_sp, s_nn = self.sem("head_sums_in"), self.sem("qk_spread"), self.sem("qk_normed")
        lam_d, lam_p, lam_a = self.marks("lam_dve", ["prod", "sub", "lam"]), self.sem("lam_pe"), self.sem("lam_act")
        s_b = [self.sem(f"bias_{q}") for q in ("in", "pe", "act", "out")]
        with ExitStack() as st:
            SQ, R = (self.T, self.B0), self.sb(st, "qk_r", SEQ)
            sums, spread = self.sb(st, "head_sums", 16, 32), self.sb(st, "head_spread", 16, P)
            tab, oh, row = self.sb(st, "tab", 12), self.sb(st, "onehot", 1024), self.sb(st, "biasrow", 1024)
            with nc.Block() as block:
                @block.sync
                def _(sp):
                    sp.dma_start(tab[0:33, :], A["bias_table"]).then_inc(s_b[0], 16)
                    sp.dma_start(oh[0:33, :], A["bucket_onehot"]).then_inc(s_b[0], 16)
                    load_chunks(sp, ring, A["w_qk"], 8, 2 * KT * P)
                    sp.wait_ge(s_b[2], 2)
                    sp.dma_start(A["bias_rows"], row[0:12, :]).then_inc(s_b[3], 16)
                    sp.wait_ge(s_b[3], 16)

                @block.tensor
                def _(pe):
                    pe.wait_ge(s_b[0], 32)
                    for b in range(2):
                        last = pe.matmul(ps[0:12, 6 + b, :], tab[0:33, :], oh[0:33, b * BANK:(b + 1) * BANK],
                                         start=True, stop=True)
                    last.then_inc(s_b[1], 1)
                    pe.wait_ge(lam_d.sem, lam_d.at("prod"))
                    pe.wait_ge(s_b[2], 2)
                    pe.matmul(ps[:, 6, 0:2], self.con("ones"), lam[:, 0:2], start=True, stop=True).then_inc(lam_p, 1)
                    project(pe, ring, ps, 8, 2, KT, lambda k: H[:, k, :])

                @block.scalar
                def _(act):
                    act.wait_ge(s_b[1], 1)
                    for b in range(2):
                        S.activation(row[0:12, b * BANK:(b + 1) * BANK], ps[0:12, 6 + b, :], ACT.Copy).then_inc(s_b[2], 1)
                    act.wait_ge(lam_p, 1)
                    S.activation(lam[:, 2:4], ps[:, 6, 0:2], ACT.Exp).then_inc(lam_a, 1)

                    def body(s, trip, c):
                        act.wait_ge(ring.used[s], ring.used_at(s, trip))
                        S.activation(QK[:, ds(2 * c, 2), :], ps[:, 2 * s:2 * s + 2, :], ACT.Copy).then_inc(ring.drained[s], 1)

                    over_chunks(act, 8, body)

                @block.vector
                def _(dve):
                    V.tensor_tensor(lam[:, 0:2], self.col("lam", 0, 4).rearrange("p (a b) -> p a b", b=2)[:, :, 0],
                                    self.col("lam", 0, 4).rearrange("p (a b) -> p a b", b=2)[:, :, 1],
                                    ALU.mult).then_inc(*lam_d.did("prod"))
                    dve.wait_ge(lam_a, 1)
                    V.tensor_tensor(lam[:, 4:5], lam[:, 2:3], lam[:, 3:4], ALU.subtract).then_inc(*lam_d.did("sub"))
                    dve.wait_ge(lam_d.sem, lam_d.at("sub"))
                    V.tensor_scalar(lam[:, 5:6], lam[:, 4:5], LAMBDA_INIT, None, ALU.add).then_inc(*lam_d.did("lam"))
            ring.end(8)
            with nc.Block() as block:
                @block.sync
                def _(sp):
                    load_chunks(sp, ring, A["w_v"], NV, 4 * BANK)
                    sp.dma_start(sums[:, :, :], A["head_sums"]).then_inc(s_sel, 16)
                    sp.dma_start(spread[0:32, :, :], A["head_spread"]).then_inc(s_sel, 16)

                @block.tensor
                def _(pe):
                    def value_chunk(c):
                        s, half = c % SLOTS, c % 2
                        pe.wait_ge(ring.loaded[s], (ring.fills[s] + c // SLOTS + 1) * 16)
                        for t in range(TT):
                            for k in range(4):
                                last = pe.matmul(ps[:, t, :], H[:, 4 * half + k, t * P:(t + 1) * P],
                                                 ring.buf[s][:, k * BANK:(k + 1) * BANK],
                                                 start=(half == 0 and k == 0), stop=(half == 1 and k == 3))
                        last.then_inc(ring.used[s], 1)

                    value_chunk(0)
                    value_chunk(1)
                    pe.wait_ge(s_sel, 32)
                    for i in range(16):
                        pe.wait_ge(s_sq, i + 1)
                        last = pe.matmul(ps[0:32, 7, :], sums[:, i, :], SQ[i // KT][:, i % KT, :], start=(i == 0),
                                         stop=(i == 15))
                    last.then_inc(s_var, 1)
                    pe.wait_ge(s_vo, 1)
                    value_chunk(2)
                    value_chunk(3)
                    pe.wait_ge(s_rec, 1)
                    for i in range(16):
                        if i >= 3:
                            pe.wait_ge(s_nn, i - 2)
                        pe.matmul(ps[:, 4 + i % 3, :], spread[0:32, i, :], R[0:32, :], start=True, stop=True).then_inc(
                            s_sp, 1)

                @block.scalar
                def _(act):
                    for i in range(16):
                        S.activation(SQ[i // KT][:, i % KT, :], QK[:, i, :], ACT.Square).then_inc(s_sq, 1)
                        if i == 7:
                            act.wait_ge(ring.used[1], ring.used_at(1, 0))
                            S.activation(VV[:, 0, :, :], ps[:, 0:TT, :], ACT.Copy).then_inc(s_vo, 1)
                    act.wait_ge(s_var, 1)
                    S.activation(R[0:32, :], ps[0:32, 7, :], ACT.Sqrt, bias=self.tiny[0:32, 2:3]).then_inc(s_root, 1)
                    act.wait_ge(ring.used[0], ring.used_at(0, 1))
                    S.activation(VV[:, 1, :, :], ps[:, 0:TT, :], ACT.Copy).then_inc(s_vo, 1)

                @block.vector
                def _(dve):
                    dve.wait_ge(s_root, 1)
                    V.reciprocal(R[0:32, :], R[0:32, :]).then_inc(s_rec, 1)
                    for i in range(16):
                        dve.wait_ge(s_sp, i + 1)
                        V.scalar_tensor_tensor(out=QK[:, i, :], in0=ps[:, 4 + i % 3, :],
                                               scalar=self.col(("qna", "kna", "qnb", "knb")[i // 4]), in1=QK[:, i, :],
                                               op0=ALU.mult, op1=ALU.mult).then_inc(s_nn, 1)
            ring.end(NV, 0)

    def heads(self, QK, VV, lam, O):
        nc, A, ps = self.nc, self.A, self.ps
        V, S = nc.vector, nc.scalar
        GW = SEQ + (TT - 1) * P
        units = [(0, h, q) for h in range(2) for q in range(TT)] + [(1, h, q) for q in range(TT) for h in range(2)]
        turns = [i for i, u in enumerate(units) if u[0] == 0 or u[1] == 1]
        U, NTURN = len(units), len(turns)
        U_ = range(U)
        pe_m = self.marks("at_pe", [x for i in range(U + 1) for x in
                                    ([f"s{i}"] if i < U else []) + ([f"t{i - 1}"] if i - 1 in turns else [])
                                    + ([f"pv{0 if i - 1 == 7 else 1}"] if i - 1 in (7, 15) else [])] + ["sub"], 1)
        act_m = self.marks("at_act", [x for i in range(U + 1) for x in
                                      ([f"e{i}"] if i < U else []) + ([f"p{i - 1}"] if i - 1 in turns else [])]
                           + ["oa", "ob", "sq", "root"])
        dve_m = self.marks("at_dve", [x for i in range(U + 1) for x in
                                      ([f"b{i}", f"m{i}"] if i < U else [])
                                      + ([f"r{i - 1}"] + ([f"l{i - 1}"] if units[i - 1][:2] == (1, 1) else [])
                                         + [f"n{i - 1}"] if i >= 1 else [])] + ["rec", "obn", "obg"], 1)
        pool_m = self.marks("at_pool", ["copied"])
        s_half = self.sem("queries_copied")
        s_g, s_z = self.sem("bias_loaded"), self.sem("heads_zero")
        with ExitStack() as st:
            Qz, Ks, Vz = self.sb(st, "qz", 4, SEQ), self.sb(st, "ks", 2, SEQ), self.sb(st, "vz", 3, TT, P)
            GT = self.sb(st, "gt", 3, GW)
            PR = self.sb(st, "pr", 4, SEQ)
            PT, SC = self.H[:, 0:TT, :], self.H[:, TT:TT + 2, :]
            stat = self.sb(st, "stat", U, 4)
            ON, R = self.sb(st, "on", 2, SEQ), self.sb(st, "on_r", SEQ)
            with nc.Block() as block:
                @block.sync
                def _(sp):
                    with sp.Fori(0, 4) as t:
                        sp.wait_ge(dve_m.sem, dve_m.trips(t))
                        for i in range(3):
                            hd = 2 * t + i if i < 2 else t + 8
                            sp.dma_start(GT[:, i, :], self.toeplitz(hd, GW)).then_inc(s_g, 16)

                @block.gpsimd
                def _(pool):
                    G = nc.gpsimd
                    pe_m.begin(pool)
                    dve_m.begin(pool)
                    G.memset(Qz[:, :, :], 0.0).then_inc(s_z, 1)
                    G.memset(Vz[:, :, :, :], 0.0).then_inc(s_z, 1)
                    pool.wait_ge(s_z, 2)
                    with pool.Fori(0, 4) as t:
                        pool.wait_ge(pe_m.sem, pe_m.trips(t))
                        for kind in range(2):
                            for h in range(2):
                                r = slice(64 * h, 64 * h + 64)
                                G.tensor_copy(Qz[r, 2 * kind + h, ::-1], QK[r, ds(8 * kind + t, 1), :].rearrange(
                                    "p a n -> p (a n)")).then_inc(s_half, 1)
                        pool.wait_ge(s_half, 4 * t + 4)
                        for kind in range(2):
                            G.tensor_copy(Ks[:, kind, :], QK[:, ds(8 * kind + 4 + t, 1), :].rearrange("p a n -> p (a n)"))
                        for h in range(2):
                            G.tensor_copy(Vz[:, h, :, 64 * h:64 * h + 64], VV[:, 0, :, ds(t * P + 64 * h, 64)])
                        G.tensor_copy(Vz[:, 2, :, :], VV[:, 1, :, ds(t * P, P)]).then_inc(*pool_m.did("copied"))
                        pool.wait_ge(pool_m.sem, t + 1)

                @block.tensor
                def _(pe):
                    with pe.Fori(0, 4) as t:
                        pe.wait_ge(pool_m.sem, t + 1)
                        for i in range(U + 1):
                            if i < U:
                                kind, h, q = units[i]
                                if i >= 2:
                                    pe.wait_ge(dve_m.sem, dve_m.at(f"b{i - 2}", t))
                                else:
                                    pe.wait_ge(dve_m.sem, dve_m.trips(t))
                                pe.matmul(ps[:, i % 2, :], Qz[:, 2 * kind + h, q * P:(q + 1) * P], Ks[:, kind, :],
                                          start=True, stop=True).then_inc(*pe_m.did(f"s{i}"))
                            if i - 1 in turns:
                                n = turns.index(i - 1)
                                pe.wait_ge(dve_m.sem, dve_m.at(f"n{i - 1}", t))
                                if n >= 2:
                                    pe.wait_ge(act_m.sem, act_m.at(f"p{turns[n - 2]}", t))
                                for k in range(TT):
                                    last = pe.transpose(ps[:, 2 + n % 2, k * P:(k + 1) * P],
                                                        PR[:, (i - 1) % 4, k * P:(k + 1) * P], self.con("id"))
                                last.then_inc(*pe_m.did(f"t{i - 1}"))
                            if i - 1 in (3, 7, 15):
                                pe.wait_ge(act_m.sem, act_m.at(f"p{i - 1}", t))
                                bank = 4 if i - 1 < 8 else 5
                                vi = {3: 0, 7: 1, 15: 2}[i - 1]
                                for k in range(TT):
                                    last = pe.matmul(ps[:, bank, :], Vz[:, vi, k, :], PT[:, k, :],
                                                     start=(k == 0 and vi != 1), stop=(k == TT - 1 and vi != 0))
                                if vi:
                                    last.then_inc(*pe_m.did(f"pv{vi - 1}"))
                        pe.wait_ge(act_m.sem, act_m.at("sq", t))
                        pe.matmul(ps[:, 6, :], self.con("ones"), ON[:, 1, :], start=True, stop=True).then_inc(
                            *pe_m.did("sub"))

                @block.scalar
                def _(act):
                    with act.Fori(0, 4) as t:
                        for i in range(U + 1):
                            if i < U:
                                act.wait_ge(dve_m.sem, dve_m.at(f"m{i}", t))
                                S.activation(PR[:, i % 4, :], SC[:, i % 2, :], ACT.Exp, bias=stat[:, i, 0:1],
                                             accum_out=stat[:, i, 1:2]).then_inc(*act_m.did(f"e{i}"))
                            if i - 1 in turns:
                                q = units[i - 1][2]
                                act.wait_ge(pe_m.sem, pe_m.at(f"t{i - 1}", t))
                                n = turns.index(i - 1)
                                S.activation(PT[:, :, q * P:(q + 1) * P],
                                             ps[:, 2 + n % 2, :].rearrange("p (k c) -> p k c", k=TT),
                                             ACT.Copy).then_inc(*act_m.did(f"p{i - 1}"))
                        act.wait_ge(pe_m.sem, pe_m.at("pv0", t))
                        S.activation(O[:, ds(t, 1), :].rearrange("p a n -> p (a n)"), ps[:, 4, ::-1], ACT.Copy).then_inc(
                            *act_m.did("oa"))
                        act.wait_ge(pe_m.sem, pe_m.at("pv1", t))
                        S.activation(ON[:, 0, :], ps[:, 5, ::-1], ACT.Copy).then_inc(*act_m.did("ob"))
                        act.wait_ge(act_m.sem, act_m.at("ob", t))
                        S.activation(ON[:, 1, :], ON[:, 0, :], ACT.Square).then_inc(*act_m.did("sq"))
                        act.wait_ge(pe_m.sem, pe_m.at("sub", t))
                        S.activation(R[:, :], ps[:, 6, :], ACT.Sqrt, bias=self.tiny[:, 2:3], scale=1.0 / P).then_inc(
                            *act_m.did("root"))

                @block.vector
                def _(dve):
                    with dve.Fori(0, 4) as t:
                        dve.wait_ge(s_g, (t + 1) * 48)

                        def mine(name):
                            dve.wait_ge(dve_m.sem, dve_m.at(name, t))

                        for i in range(U + 1):
                            if i < U:
                                kind, h, q = units[i]
                                dve.wait_ge(pe_m.sem, pe_m.at(f"s{i}", t))
                                if i >= 2:
                                    dve.wait_ge(act_m.sem, act_m.at(f"e{i - 2}", t))
                                lo = q * P
                                gi = h if kind == 0 else 2
                                V.scalar_tensor_tensor(out=SC[:, i % 2, :], in0=ps[:, i % 2, :], scalar=0.125,
                                                       in1=GT[:, gi, lo:lo + SEQ], op0=ALU.mult, op1=ALU.add).then_inc(
                                    *dve_m.did(f"b{i}"))
                                mine(f"b{i}")
                                V.tensor_reduce(stat[:, i, 0:1], SC[:, i % 2, :], AX, ALU.max, negate=True).then_inc(
                                    *dve_m.did(f"m{i}"))
                            if i >= 1:
                                u = i - 1
                                kind, h, q = units[u]
                                dve.wait_ge(act_m.sem, act_m.at(f"e{u}", t))
                                V.reciprocal(stat[:, u, 2:3], stat[:, u, 1:2]).then_inc(*dve_m.did(f"r{u}"))
                                mine(f"r{u}")
                                if kind == 0 or h == 0:
                                    V.tensor_scalar(PR[:, u % 4, :], PR[:, u % 4, :], stat[:, u, 2:3], None,
                                                    ALU.mult).then_inc(*dve_m.did(f"n{u}"))
                                else:
                                    V.tensor_tensor(stat[:, u, 3:4], stat[:, u, 2:3], lam[:, 5:6], ALU.mult).then_inc(
                                        *dve_m.did(f"l{u}"))
                                    mine(f"l{u}")
                                    V.tensor_scalar(PR[:, u % 4, :], PR[:, u % 4, :], stat[:, u, 3:4], None, ALU.mult)
                                    dve.drain()
                                    V.tensor_tensor(PR[:, u % 4, :], PR[:, (u - 1) % 4, :], PR[:, u % 4, :],
                                                    ALU.subtract).then_inc(*dve_m.did(f"n{u}"))
                        dve.wait_ge(act_m.sem, act_m.at("root", t))
                        V.reciprocal(R[:, :], R[:, :]).then_inc(*dve_m.did("rec"))
                        mine("rec")
                        V.tensor_tensor(ON[:, 0, :], ON[:, 0, :], R[:, :], ALU.mult).then_inc(*dve_m.did("obn"))
                        mine("obn")
                        V.tensor_scalar(O[:, ds(t + 4, 1), :].rearrange("p a n -> p (a n)"), ON[:, 0, :], self.col("sub"),
                                        1.0 - LAMBDA_INIT, ALU.mult, ALU.mult).then_inc(*dve_m.did("obg"))

    def toeplitz(self, head, width):
        a = self.A["bias_rows"]
        x = a[ds(head, 1), 0:1]
        return AP(x.tensor, x.offset, [(1, P), (1, width)])

    def convffn(self):
        nc, A, ring, ps, X, T, H = self.nc, self.A, self.ring, self.ps, self.X, self.T, self.H
        V, S = nc.vector, nc.scalar
        self.norm("rms2", X, self.col("n2g", 0, 8), None, 2, 32, 24, center=False)
        W = 2 * KT * P + 8
        cv = [self.sem(f"conv{s}") for s in range(SLOTS)]
        hid = [self.sem(f"conv_hid{s}") for s in range(SLOTS)]
        sl = [self.sem(f"conv_silu{s}") for s in range(SLOTS)]
        s_z = self.sem("conv_zero")
        with ExitStack() as st:
            HH, HL = (st.enter_context(nc.sbuf_tensor(f"sb_conv_{q}", [P, KT, SEQ], F32R)) for q in ("hh", "hl"))
            with nc.Block() as block:
                @block.scalar
                def _(act):
                    self.split_features(act, None, HH, HL)

                @block.vector
                def _(dve):
                    self.split_features(None, dve, HH, HL)
            self.h.close()
            HID = self.sb(st, "chid", FT, SEQ)
            UP = self.sb(st, "up", SLOTS, 2, SEQ + 2)
            CV, PC = self.sb(st, "cv", SLOTS, 2, SEQ), self.sb(st, "convw", FT, 8)
            s_pc = self.sem("convw_in")
            up_split = ExitStack()
            split = Split(nc, up_split, ring, "conv_up", 2 * KT * P)
            with nc.Block() as block:
                @block.sync
                def _(sp):
                    sp.dma_start(PC[:, :, :], A["conv_cols"]).then_inc(s_pc, 16)
                    load_chunks(sp, ring, A["w_up"], FT, 2 * KT * P)

                @block.tensor
                def _(pe):
                    split.project(pe, ps, FT, 2, KT, lambda k: HH[:, k, :], lambda k: HL[:, k, :])

                @block.gpsimd
                def _(pool):
                    for q in (*cv, *hid):
                        pool.sem_inc(q, 1)
                    nc.gpsimd.memset(UP[:, :, :, :], 0.0).then_inc(s_z, 1)

                @block.scalar
                def _(act):
                    split.leading(act, 0, 0)
                    act.wait_ge(s_z, 1)

                    def body(s, trip, c):
                        with_next(FT, s, trip, c, lambda s1, t1: split.leading(act, s1, t1))
                        act.wait_ge(ring.used[s], ring.used_at(s, trip))
                        act.wait_ge(cv[s], trip * 6 + 1)
                        S.activation(UP[:, s, :, 1:SEQ + 1], ps[:, 2 * s:2 * s + 2, :], ACT.Copy).then_inc(
                            ring.drained[s], 1)
                        act.wait_ge(cv[s], trip * 6 + 7)
                        S.activation(CV[:, s, 1, :], CV[:, s, 1, :], ACT.Silu).then_inc(sl[s], 1)

                    over_chunks(act, FT, body)

                @block.vector
                def _(dve):
                    split.rest(dve, 0, 0)
                    dve.wait_ge(s_pc, 16)

                    def body(s, trip, c):
                        with_next(FT, s, trip, c, lambda s1, t1: split.rest(dve, s1, t1))
                        dve.wait_ge(ring.drained[s], ring.drained_at(s, trip))
                        dve.wait_ge(hid[s], trip + 1)

                        def w(i):
                            return PC[:, ds(c, 1), i:i + 1].rearrange("p a b -> p (a b)")

                        for m in range(2):
                            V.tensor_scalar(CV[:, s, m, :], UP[:, s, m, 1:SEQ + 1], w(4 * m + 1), w(4 * m + 3), ALU.mult,
                                            ALU.add).then_inc(cv[s], 1)
                        for n, tap in enumerate((0, 2)):
                            dve.wait_ge(cv[s], trip * 6 + 2 * n + 3)
                            for m in range(2):
                                V.scalar_tensor_tensor(out=CV[:, s, m, :], in0=UP[:, s, m, tap:tap + SEQ], scalar=w(4 * m + tap),
                                                       in1=CV[:, s, m, :], op0=ALU.mult, op1=ALU.add).then_inc(cv[s], 1)
                        dve.wait_ge(sl[s], trip + 1)
                        V.tensor_tensor(HID[:, ds(c, 1), :].rearrange("p a n -> p (a n)"), CV[:, s, 0, :], CV[:, s, 1, :],
                                        ALU.mult).then_inc(hid[s], 1)

                    over_chunks(dve, FT, body)
            up_split.close()
            split.end(FT)
            self.residual("down", A["w_down"], KT, 1, FT, lambda k: HID[:, k, :], 2, 40, None)
        s_o = self.sem("stored")
        with nc.Block() as block:
            @block.sync
            def _(sp):
                sp.dma_start(A["out"], X[:, :, :]).then_inc(s_o, 16)
                sp.wait_ge(s_o, 16)


def _blocks(w, width, dtype=np.float32):
    k, m = w.shape
    return np.ascontiguousarray(w.reshape(k // P, P, m // width, width).transpose(2, 1, 0, 3)).reshape(
        m // width, P, (k // P) * width)


def _cols(v):
    return np.asarray(v).reshape(-1, P).T


def _constants():
    c = np.zeros((P, NCONST), np.float32)

    def put(name, a):
        lo, hi = CONST[name]
        c[:, lo:hi] = a.reshape(P, hi - lo)

    i = np.arange(P)
    same = (i[:, None] // CH) == (i[None, :] // CH)
    put("id", np.eye(P))
    put("hsum", same.astype(np.float32))
    put("hmean", same / float(CH))
    put("ones", np.ones((P, P)))
    put("mean", np.full((P, P), 1.0 / D))
    a, b = i[:, None] % CH, i[None, :] % CH
    strict = [same & (a < b), same & (a > b)]
    incl = [same & (a <= b), same & (a >= b)]
    put("mS", np.stack([np.stack([strict[d] * 1.0, incl[d] * -1.0], 1) for d in range(2)], 1))
    put("mK", np.stack([np.stack([strict[d] * 1.0, incl[d] * 1.0], 1) for d in range(2)], 1))
    lv = []
    for m in LEVELS:
        low = same & (a // (2 * m) == b // (2 * m)) & (a % (2 * m) >= m) & (b % (2 * m) < m)
        lv.append(np.stack([low * -1.0, low.T * -1.0], 1))
    put("mL", np.stack(lv, 1))
    t = np.arange(TOK)
    put("scan", np.broadcast_to((t % CH != 0) * 1.0, (P, TOK)))
    pos = np.arange(GRID_W)
    cnt = [np.clip(pos + w // 2, 0, GRID_W) - np.clip(pos - w // 2, 0, GRID_W) for w in WINDOWS]
    put("rcnt", np.broadcast_to(1.0 / np.stack(cnt), (P, 4, GRID_W)))
    return c


def _layout(z):
    g = {k: np.asarray(v) for k, v in z.items()}
    par = np.zeros((P, NCOL), np.float32)

    def put(name, a):
        lo, hi = COLS[name]
        par[0:a.shape[0], lo:hi] = a

    put("c", np.concatenate([_cols(g["c"][0]), _cols(g["c"][0]), _cols(g["c_2"][0])], 1))
    put("cc", np.concatenate([_cols(g["c_ctx"]), _cols(g["c"][0]), _cols(g["c_2"][0])], 1))
    put("adab", np.concatenate([_cols(g["ada_b"][0]), _cols(g["ada_b"][1]), _cols(g["b_ada_2"][0])], 1))
    put("lng", _cols(g["ln_g"].reshape(-1)))
    put("lnb", _cols(g["ln_b"].reshape(-1)))
    put("mu", _cols(g["rk_mu"][0].reshape(-1)))
    pair = [g["rk_w0"][0, 0], g["rk_w0"][0, 1], g["rk_a0"][0, 0], g["rk_a0"][0, 1], g["rk_k_k"][0], g["rk_k_a"][0],
            g["rk_r_k"][0].reshape(-1), g["rk_lnx_g"][0], g["rk_lnx_b"][0]]
    put("pair", np.stack([_cols(v) for v in pair], 2).reshape(P, 72))
    put("pscale", _cols(g["pool_scale"][0]))
    put("n1g", _cols(g["norm1_g_2"][0]))
    put("n2g", _cols(g["norm2_g_2"][0]))
    for n, k in (("qna", "q_norm_a_2"), ("kna", "k_norm_a_2"), ("qnb", "q_norm_b_2"), ("knb", "k_norm_b_2")):
        put(n, np.tile(g[k][0], 2)[:, None])
    put("sub", g["subln_g_2"][0][:, None])
    put("lam", np.stack([g[k][0] for k in ("lambda_q1_2", "lambda_k1_2", "lambda_q2_2", "lambda_k2_2")], 1))

    a = {"params": par, "consts": _constants()}
    a["xT"] = np.ascontiguousarray(g["x"][0].T.reshape(KT, P, SEQ).transpose(1, 0, 2))
    a["ctxT"] = np.ascontiguousarray(g["ctx"][0].T.reshape(KT, P, CTX).transpose(1, 0, 2))
    ada = np.stack([g["ada_w"][0], g["ada_w"][1], g["w_ada_2"][0]])
    a["w_ada"] = np.ascontiguousarray(ada.reshape(3, 2, 4, P, 12, 512).transpose(0, 4, 1, 3, 2, 5)).reshape(72, P, 2048)
    w1 = np.concatenate([g["rk_w1"][0, 0], g["rk_w1"][0, 1]], 1)
    a1 = np.concatenate([g["rk_a1"][0, 0], g["rk_a1"][0, 1]], 1)
    a["w_lora1"] = np.stack([_blocks(w, P)[0] for w in (w1, a1, g["rk_g1"][0])])
    zero = np.zeros((64, D), np.float32)
    second = [np.concatenate([g["rk_w2"][0, 0], zero]), np.concatenate([zero, g["rk_w2"][0, 1]]),
              np.concatenate([g["rk_a2"][0, 0], zero]), np.concatenate([zero, g["rk_a2"][0, 1]]), g["rk_g2"][0]]
    a["w_pair"] = np.pad(np.concatenate([_blocks(w, P) for w in second], 2), ((0, 1), (0, 0), (0, 0)))
    a["w_o"] = _blocks(g["rk_w_o"][0], 2 * P)

    def side(x, y):
        bx, by = _blocks(x, P), _blocks(y, P)
        n = bx.shape[0]
        return np.stack([bx.reshape(n, P, -1, P), by.reshape(n, P, -1, P)], 3).reshape(n, P, -1)

    a["w_kv"] = side(g["rk_w_rkv"][0, 1], g["rk_w_rkv"][0, 2])
    a["w_r"] = _blocks(g["rk_w_rkv"][0, 0], 2 * P)
    a["w_ffn13"] = side(g["ffn_w1"][0], g["ffn_w3"][0])
    a["w_ffn2"] = _blocks(g["ffn_w2"][0], P)
    a["w_pool"] = np.concatenate([_blocks(w, 2 * P)[0] for w in g["pool_w"][0]], 1)
    a["w_router"] = _blocks(g["moe_router_w"][0], NE)[0]
    a["router_b"] = g["moe_router_b"][0:1]
    a["tie_mask"] = np.tril(np.ones((NE, NE), np.float32), -1).reshape(1, NE * NE)
    a["before"] = np.triu(np.ones((P, P), np.float32), 1)
    a["steps"] = np.concatenate([np.arange(4) * P, np.arange(ITEMS)]).astype(np.float32)[None]
    a["zeros"] = np.zeros((P, 2 * TOK), np.float32)
    up = np.stack([g["moe_w1"][0], g["moe_w3"][0]], 2).reshape(NE, KT, P, 2, FE // HCOL, HCOL)
    a["w_moe_up"] = np.ascontiguousarray(up.transpose(0, 4, 2, 1, 3, 5)).reshape(NE * (FE // HCOL), P, SLOT)
    a["w_moe_down"] = np.concatenate([_blocks(g["moe_w2"][0, e], YCOL) for e in range(NE)])
    w = g["w_in_2"][0]
    a["w_qk"] = _blocks(np.concatenate([w[:, 0:1024], w[:, 1536:2560]], 1), 2 * P)
    v = np.stack([w[:, 1024:1536], w[:, 2560:3072]])
    a["w_v"] = np.ascontiguousarray(v.reshape(2, 2, 4, P, 512).transpose(0, 1, 3, 2, 4)).reshape(4, P, 2048)
    head = 2 * np.arange(16)[:, None] + np.arange(P)[None] // CH
    to_row = (head[:, :, None] == np.arange(32)).astype(np.float32)
    a["head_sums"] = np.ascontiguousarray(to_row.transpose(1, 0, 2)) / np.float32(CH)
    a["head_spread"] = np.ascontiguousarray(to_row.transpose(2, 0, 1))
    a["w_out"] = _blocks(g["w_out_2"][0], 2 * P)
    extra = np.zeros((1, 12), np.float32)
    extra[0, :8] = 1.0
    a["bias_table"] = np.concatenate([g["rel_bias_2"], extra])
    a["bucket_onehot"] = _buckets()
    up = g["w_up_2"][0]
    a["w_up"] = side(up[:, :FF], up[:, FF:])
    cw = np.concatenate([g["conv_w_2"][0], g["conv_b_2"]])
    a["conv_cols"] = np.ascontiguousarray(cw.reshape(4, 2, FT, P).transpose(3, 2, 1, 0)).reshape(P, FT, 8)
    a["w_down"] = _blocks(g["w_down_2"][0], P)
    return a


def _buckets():
    rel = np.arange(-511, 513)
    n = np.abs(rel)
    edge = [8, 16, 32, 64, 128, 256, 512]
    large = 7 + np.searchsorted(edge, n, side="right")
    b = np.where(rel > 0, 16, 0) + np.where(n < 8, n, np.minimum(large, 15))
    out = np.zeros((33, 1024), np.float32)
    out[b, np.arange(1024)] = 1.0
    cnt = sum(((rel % d == 0) & (n <= w // 2)).astype(int) for w, d in ((128, 1), (512, 4), (2048, 16)))
    out[32] = np.where(cnt > 0, np.log(np.maximum(cnt, 1)), -1e30)
    return out


def scratch(nc):
    return {n: nc.dram_tensor(n, s, F32).ap() for n, s in (
        ("bias_rows", (12, 1024)), ("kv_rows", (KT + 1, P, 2 * TOK)), ("r_rows", (KT + 1, P, SEQ)),
        ("x_rows", ((ITEMS + 2) * P, D)), ("y_rows", (ITEMS * P, D)))}


def kernel(**inputs):
    import concourse.bacc as bacc
    from concourse.bass_utils import run_bass_kernel_spmd

    nc = bacc.Bacc("TRN2", target_bir_lowering=False, num_devices=1)
    arrays = _layout(inputs)
    A = {n: nc.dram_tensor(n, a.shape, mybir.dt.from_np(a.dtype), kind="ExternalInput").ap()
         for n, a in arrays.items()}
    A.update(scratch(nc))
    A["out"] = nc.dram_tensor("out", (P, KT, SEQ), F32, kind="ExternalOutput").ap()
    Kernel(nc, A).build()
    r = run_bass_kernel_spmd(nc, [arrays], core_ids=[0])
    y = r.results[0]["out"]
    return np.ascontiguousarray(y.transpose(1, 0, 2).reshape(D, SEQ).T)[None]
```
